# Optimizing a Trainium2 kernel written in Bass

```python
import jax, jax.numpy as jnp
from jax import lax
import numpy as np

D_MODEL = 1024
BATCH = 1
SEQ = 1024
DEPTH = 1

D_MIX = D_MODEL
HEAD_DIM = 128
GM_HEADS = 4
GM_WIDTH = GM_HEADS * HEAD_DIM
GM_CHUNK = 128
DN_HEADS = 4
DN_DK = 128
DN_DV = 128
DN_KEY = DN_HEADS * DN_DK
DN_VAL = DN_HEADS * DN_DV
DN_CHUNK = 64
CONV_W = 4
D_IN = 2 * GM_WIDTH + 2 * DN_KEY + 2 * DN_VAL + 2 * DN_HEADS
N_EXPERTS = 32
TOP_K = 4
D_FF = D_MODEL
SWIGLU_LIMIT = 7.0
SWIGLU_ALPHA = 1.702
MOE_BLOCK = 128
EPS = 1e-6

kernel_name = "hymba_gmlp_gdn_moe_layer"

def rmsnorm(x, g):
    xf = x.astype(jnp.float32)
    y = xf * lax.rsqrt(jnp.mean(xf * xf, axis=-1, keepdims=True) + EPS)
    return (y * g.astype(jnp.float32)).astype(x.dtype)

def l2norm(x):
    xf = x.astype(jnp.float32)
    return xf * lax.rsqrt(jnp.sum(xf * xf, axis=-1, keepdims=True) + EPS)

def gmlp_chunk_mixer(u, v, norm_g, ws, bs):
    b_, s_, _ = u.shape
    n = s_ // GM_CHUNK
    u = jax.nn.gelu(u, approximate=False).reshape(b_, n, GM_CHUNK, GM_HEADS, HEAD_DIM)
    v = jax.nn.gelu(v, approximate=False).reshape(b_, n, GM_CHUNK, GM_HEADS, HEAD_DIM)
    v = rmsnorm(v, norm_g)
    causal = jnp.tril(jnp.ones((GM_CHUNK, GM_CHUNK), dtype=bool))
    w = jnp.where(causal, ws, jnp.zeros_like(ws)).astype(v.dtype)
    gate = jnp.einsum('hts,bnshc->bnthc', w, v) + bs.T.astype(v.dtype)[None, None, :, :, None]
    return (u * gate).reshape(b_, s_, GM_WIDTH)

def causal_dwconv(x, w):
    c = x.shape[-1]
    return lax.conv_general_dilated(
        x, w[:, None, :].astype(x.dtype), window_strides=(1,),
        padding=[(CONV_W - 1, 0)], dimension_numbers=('NWC', 'WIO', 'NWC'),
        feature_group_count=c)

def gated_delta_rule(q, k, v, g, beta):
    b_, h_, s_, dk = q.shape
    dv = v.shape[-1]
    c = DN_CHUNK
    n = s_ // c
    q = q * (dk ** -0.5)
    qc = q.reshape(b_, h_, n, c, dk)
    kc = k.reshape(b_, h_, n, c, dk)
    vc = v.reshape(b_, h_, n, c, dv)
    bc = beta.reshape(b_, h_, n, c)
    gc = jnp.cumsum(g.reshape(b_, h_, n, c), axis=-1)
    tril_incl = jnp.tril(jnp.ones((c, c), dtype=bool))
    tril_strict = jnp.tril(jnp.ones((c, c), dtype=bool), -1)
    diff = gc[..., :, None] - gc[..., None, :]
    decay = jnp.where(tril_incl, jnp.exp(jnp.where(tril_incl, diff, 0.0)), 0.0)
    kb = kc * bc[..., None]
    lower = jnp.where(tril_strict, jnp.einsum('bhnid,bhnjd->bhnij', kb, kc) * decay, 0.0)
    a_mat = lower + jnp.eye(c, dtype=lower.dtype)
    rhs = jnp.concatenate([vc * bc[..., None], kb * jnp.exp(gc)[..., None]], axis=-1)
    sol = lax.linalg.triangular_solve(a_mat, rhs, left_side=True, lower=True, unit_diagonal=True)
    u_c = sol[..., :dv]
    w_c = sol[..., dv:]
    attn_intra = jnp.where(tril_incl, jnp.einsum('bhnid,bhnjd->bhnij', qc, kc) * decay, 0.0)
    g_last = gc[..., -1]
    k_to_end = kc * jnp.exp(g_last[..., None] - gc)[..., None]
    q_dec = qc * jnp.exp(gc)[..., None]

    def step(state, inp):
        q_i, u_i, w_i, a_i, k_e, gl = inp
        v_new = u_i - jnp.einsum('bhcd,bhde->bhce', w_i, state)
        o = jnp.einsum('bhcd,bhde->bhce', q_i, state) + jnp.einsum('bhij,bhje->bhie', a_i, v_new)
        state = state * jnp.exp(gl)[..., None, None] + jnp.einsum('bhcd,bhce->bhde', k_e, v_new)
        return state, o

    xs = tuple(jnp.moveaxis(t, 2, 0) for t in (q_dec, u_c, w_c, attn_intra, k_to_end, g_last))
    s0 = jnp.zeros((b_, h_, dk, dv), jnp.float32)
    _, o = lax.scan(step, s0, xs)
    return jnp.moveaxis(o, 0, 2).reshape(b_, h_, s_, dv)

def gated_deltanet_mixer(qkv, z, a, bb, conv_w, a_log, dt_bias, norm_g):
    b_, s_, _ = qkv.shape
    qkv = jax.nn.silu(causal_dwconv(qkv, conv_w))
    q, k, v = jnp.split(qkv, 3, axis=-1)
    q = l2norm(q.reshape(b_, s_, DN_HEADS, DN_DK)).transpose(0, 2, 1, 3)
    k = l2norm(k.reshape(b_, s_, DN_HEADS, DN_DK)).transpose(0, 2, 1, 3)
    v = v.reshape(b_, s_, DN_HEADS, DN_DV).astype(jnp.float32).transpose(0, 2, 1, 3)
    g = -jnp.exp(a_log.astype(jnp.float32)) * jax.nn.softplus(a.astype(jnp.float32) + dt_bias.astype(jnp.float32))
    beta = jax.nn.sigmoid(bb.astype(jnp.float32))
    o = gated_delta_rule(q, k, v, g.transpose(0, 2, 1), beta.transpose(0, 2, 1))
    o = o.transpose(0, 2, 1, 3)
    o = rmsnorm(o, norm_g) * jax.nn.silu(z.reshape(b_, s_, DN_HEADS, DN_DV).astype(jnp.float32))
    return o.reshape(b_, s_, DN_VAL).astype(z.dtype)

def moe_ffn(h, router_w, router_b, w_gu, b_gu, w_down, b_down):
    b_, s_, d = h.shape
    t = b_ * s_
    xf = h.reshape(t, d)
    logits = (xf @ router_w + router_b).astype(jnp.float32)
    top_val, top_idx = lax.top_k(logits, TOP_K)
    gates = jax.nn.softmax(top_val, axis=-1)
    n_assign = t * TOP_K
    flat_e = top_idx.reshape(n_assign)
    order = jnp.argsort(flat_e)
    sorted_e = flat_e[order]
    counts = jnp.zeros((N_EXPERTS,), jnp.int32).at[flat_e].add(1)
    padded = (counts + MOE_BLOCK - 1) // MOE_BLOCK * MOE_BLOCK
    pad_end = jnp.cumsum(padded)
    pad_start = pad_end - padded
    start = jnp.cumsum(counts) - counts
    dest = pad_start[sorted_e] + jnp.arange(n_assign, dtype=jnp.int32) - start[sorted_e]
    n_blocks = -(-(n_assign + N_EXPERTS * MOE_BLOCK) // MOE_BLOCK)
    p = n_blocks * MOE_BLOCK
    buf_tok = jnp.full((p,), t, jnp.int32).at[dest].set((order // TOP_K).astype(jnp.int32))
    buf_gate = jnp.zeros((p,), jnp.float32).at[dest].set(gates.reshape(n_assign)[order])
    block_e = jnp.minimum(jnp.searchsorted(pad_end, jnp.arange(n_blocks, dtype=jnp.int32) * MOE_BLOCK, side='right'), N_EXPERTS - 1)
    x_pad = jnp.concatenate([xf, jnp.zeros((1, d), xf.dtype)], axis=0)
    xin = x_pad[buf_tok].reshape(n_blocks, MOE_BLOCK, d)

    def expert_block(args):
        xb, e = args
        gu = xb @ w_gu[e] + b_gu[e]
        gate, up = jnp.split(gu, 2, axis=-1)
        gate = jnp.minimum(gate, SWIGLU_LIMIT)
        up = jnp.clip(up, -SWIGLU_LIMIT, SWIGLU_LIMIT)
        return ((up + 1.0) * (gate * jax.nn.sigmoid(SWIGLU_ALPHA * gate))) @ w_down[e] + b_down[e]

    y = lax.map(expert_block, (xin, block_e)).reshape(p, d)
    out = jnp.zeros((t + 1, d), y.dtype).at[buf_tok].add(y * buf_gate[:, None].astype(y.dtype))
    return out[:t].reshape(b_, s_, d)

def setup_inputs(seed: int = 0) -> dict:
    key = jax.random.key(seed)
    ks = jax.random.split(key, 20)
    f32 = jnp.float32
    nrm = lambda k, shape, scale: jax.random.normal(k, shape, f32) * scale
    gain = lambda k, shape: 1.0 + 0.02 * jax.random.normal(k, shape, f32)
    dt = jnp.exp(jax.random.uniform(ks[8], (DEPTH, DN_HEADS), f32, np.log(1e-3), np.log(1e-1)))
    return {
        "x": nrm(ks[0], (BATCH, SEQ, D_MODEL), 1.0),
        "norm_mix_g": gain(ks[1], (DEPTH, D_MODEL)),
        "w_in": nrm(ks[2], (DEPTH, D_MODEL, D_IN), D_MODEL ** -0.5),
        "gm_norm_g": gain(ks[3], (DEPTH, GM_HEADS, HEAD_DIM)),
        "gm_ws": nrm(ks[4], (DEPTH, GM_HEADS, GM_CHUNK, GM_CHUNK), GM_CHUNK ** -0.5),
        "gm_bs": gain(ks[5], (DEPTH, GM_HEADS, GM_CHUNK)),
        "dn_conv_w": nrm(ks[6], (DEPTH, CONV_W, 3 * DN_KEY), CONV_W ** -0.5),
        "dn_a_log": jnp.log(jax.random.uniform(ks[7], (DEPTH, DN_HEADS), f32, 1.0, 16.0)),
        "dn_dt_bias": dt + jnp.log(-jnp.expm1(-dt)),
        "dn_norm_g": gain(ks[9], (DEPTH, DN_DV)),
        "w_out": nrm(ks[10], (DEPTH, D_MIX, D_MODEL), D_MIX ** -0.5),
        "norm_ffn_g": gain(ks[11], (DEPTH, D_MODEL)),
        "router_w": nrm(ks[12], (DEPTH, D_MODEL, N_EXPERTS), D_MODEL ** -0.5),
        "router_b": nrm(ks[13], (DEPTH, N_EXPERTS), 0.01),
        "exp_w_gu": nrm(ks[14], (DEPTH, N_EXPERTS, D_MODEL, 2 * D_FF), D_MODEL ** -0.5),
        "exp_b_gu": nrm(ks[15], (DEPTH, N_EXPERTS, 2 * D_FF), 0.01),
        "exp_w_down": nrm(ks[16], (DEPTH, N_EXPERTS, D_FF, D_MODEL), D_FF ** -0.5),
        "exp_b_down": nrm(ks[17], (DEPTH, N_EXPERTS, D_MODEL), 0.01),
        "final_norm_g": gain(ks[18], (D_MODEL,)),
    }

def reference(x, norm_mix_g, w_in, gm_norm_g, gm_ws, gm_bs, dn_conv_w, dn_a_log, dn_dt_bias,
              dn_norm_g, w_out, norm_ffn_g, router_w, router_b, exp_w_gu, exp_b_gu,
              exp_w_down, exp_b_down, final_norm_g):
    split_points = [GM_WIDTH, 2 * GM_WIDTH, 2 * GM_WIDTH + 2 * DN_KEY + DN_VAL,
                    2 * GM_WIDTH + 2 * DN_KEY + 2 * DN_VAL,
                    2 * GM_WIDTH + 2 * DN_KEY + 2 * DN_VAL + DN_HEADS]
    h = x
    for l in range(DEPTH):
        y = rmsnorm(h, norm_mix_g[l])
        proj = y @ w_in[l]
        u, v_gm, qkv, z, a, bb = jnp.split(proj, split_points, axis=-1)
        out_a = gmlp_chunk_mixer(u, v_gm, gm_norm_g[l], gm_ws[l], gm_bs[l])
        out_b = gated_deltanet_mixer(qkv, z, a, bb, dn_conv_w[l], dn_a_log[l], dn_dt_bias[l], dn_norm_g[l])
        mix = jnp.concatenate([out_a, out_b], axis=-1)
        h = h + mix @ w_out[l]
        h = h + moe_ffn(rmsnorm(h, norm_ffn_g[l]), router_w[l], router_b[l], exp_w_gu[l],
                        exp_b_gu[l], exp_w_down[l], exp_b_down[l])
    return rmsnorm(h, final_norm_g)


_drawn_inputs = setup_inputs


def setup_inputs(seed=0):
    import zlib

    import numpy as np

    out = dict(_drawn_inputs(seed))
    spreads = {}
    factors = {'gm_norm_g': 2.924, 'exp_b_gu': 8.0, 'exp_b_down': 8.0, 'final_norm_g': 2.9}
    for name, (base, spread) in spreads.items():
        noise = np.random.default_rng([zlib.crc32(name.encode()), seed]).standard_normal(out[name].shape)
        drawn = base * np.exp(spread * noise) if base else spread * noise
        out[name] = __import__('jax').numpy.asarray(drawn.astype(out[name].dtype))
    for name, factor in factors.items():
        out[name] = (out[name] * factor).astype(out[name].dtype)
    return out
```

```python
import concourse.bass as bass
from concourse import mybir
from contextlib import ExitStack

D, SEQ, P = 1024, 1024, 128
KT, TT = D // P, SEQ // P
H, W = 4, 512
NE, TOPK, F = 32, 4, 1024
CONV = 4
EPS = 1e-6
LIMIT, ALPHA = 7.0, 1.702
CAP = 256
NBLK = NE + SEQ * TOPK // CAP
SLOTS = SEQ * TOPK + CAP
U0, V0, Q0, Z0, A0 = 0, W, 2 * W, 5 * W, 6 * W
LEVELS = 7
C_ID, C_TRI, C_ONE, C_M0T, C_LV = 0, 128, 256, 384, 512
C_IOTA = C_LV + LEVELS * 128
C_PART = C_IOTA + NE
C_HALF, C_EPS = C_PART + 1, C_PART + 2
NCST = C_PART + 3


def program(nc, x, norm_mix_g, w_in, gm_norm_g, gm_ws, gm_bs, dn_conv_w, dn_a_log, dn_dt_bias,
            dn_norm_g, w_out, norm_ffn_g, router_w, router_b, exp_w_gu, exp_b_gu, exp_w_down,
            exp_b_down, final_norm_g, consts, tok_ids, out, h_dram, h2_dram, list_dram, tab_dram,
            y_dram, dbg=None):
    fp32, i32, u32 = mybir.dt.float32, mybir.dt.int32, mybir.dt.uint32
    ALU, ACT, AX = mybir.AluOpType, mybir.ActivationFunctionType, mybir.AxisListType
    ds = bass.ds
    ctx = ExitStack()
    with ctx:
        def sb(name, shape, dt=fp32):
            return ctx.enter_context(nc.sbuf_tensor(name, shape, dt))

        sems = {}

        def S(name, slot=None):
            key = name if slot is None else f"{name}_{slot}"
            if key not in sems:
                sems[key] = nc.alloc_semaphore(name=key)
            return sems[key]

        cst = sb("cst", [P, NCST])
        ident, tri, ones = cst[:, 0:128], cst[:, 128:256], cst[:, 256:384]
        m0t = cst[:, C_M0T:C_M0T + 128]
        iota_e, part = cst[:, C_IOTA:C_IOTA + NE], cst[:, C_PART:C_PART + 1]

        def level(l):
            return cst[:, C_LV + 128 * l:C_LV + 128 * (l + 1)]

        ids = sb("ids", [P, TT], i32)
        ffn_g = sb("ffn_g", [P, D])
        fin_g = sb("fin_g", [P, D])
        gmg = sb("gmg", [P, W])
        dng = sb("dng", [P, P])
        rb = sb("rb", [P, NE])
        alog = sb("alog", [P, H])
        dtb = sb("dtb", [P, H])
        NV = CONV * 12 + KT + H
        vT = sb("vT", [P, NV])
        conv_T, mixg_T, bs_T = vT[:, 0:48], vT[:, 48:56], vT[:, 56:60]
        bgu_T = sb("bgu_T", [P, NE * 16])
        bd_T = sb("bd_T", [P, NE * KT])
        rw = sb("rw", [P, KT, NE])
        wsT = sb("wsT", [P, H, P])
        small = sb("small", [P, 160])
        g_all, be_all = sb("g_all", [P, TT, H]), sb("be_all", [P, TT, H])
        gc_all, bx_all = sb("gc_all", [P, TT, H]), sb("bx_all", [P, TT, H])
        ab = sb("ab", [P, TT, 2 * H])
        lg = [small[:, 64 + 32 * s:96 + 32 * s] for s in range(2)]
        best = [small[:, 128 + 8 * s:136 + 8 * s] for s in range(2)]
        best_at = [small[:, 144 + 8 * s:152 + 8 * s].bitcast(u32) for s in range(2)]
        top = sb("top", [P, TT, 8])
        tix = sb("tix", [P, TT, 8], u32)
        gates = sb("gates", [P, TT, TOPK])
        dest = sb("dest", [P, TT, TOPK], i32)
        tab = sb("tab", [1, NBLK * 4], i32)

        AW = 45632
        arena = sb("arena", [P, AW])
        used = [0]

        def cut(cols, at=None):
            a = used[0] if at is None else at
            if at is None:
                used[0] += cols
            assert a + cols <= AW, (a, cols)
            return arena[:, a:a + cols]

        def r3(ap, n):
            return ap.rearrange("p (a b) -> p a b", a=n)

        wout = r3(cut(8192), KT)
        mix0 = used[0]
        gm = r3(cut(4096), TT)
        zs = r3(cut(4096), TT)
        big0 = used[0]
        wuvz = r3(cut(KT * 1544), KT)
        qkvT = r3(cut(KT * 1536, big0), 12)
        work0 = used[0]
        yT = r3(cut(8192), KT)
        wq = [r3(cut(2048), KT) for _ in range(2)]
        tmp0 = used[0]
        ytile = [r3(cut(1024), KT) for _ in range(2)]
        gv, vsq, vn, gu, gt = [cut(512) for _ in range(5)]
        mixer_end = used[0]
        xr = [cut(1024, mix0 + 1024 * s) for s in range(2)]
        xn = [cut(1024, mix0 + 2048 + 1024 * s) for s in range(2)]
        sqj = cut(1024, mix0 + 4096)
        vec_raw = cut(128, mix0 + 5120)
        bgu_raw = r3(cut(512, mix0 + 5248), 4)
        bd_raw = r3(cut(256, mix0 + 5760), 2)
        ws_raw = r3(cut(512, mix0 + 6016), H)
        cb = [cut(CONV - 1 + SEQ, tmp0 + 1028 * s) for s in range(2)]
        cacc = [cut(1024, tmp0 + 2056 + 1024 * s) for s in range(2)]
        usq = [cut(512, work0 + 512 * s) for s in range(2)]
        urs = [cut(512, work0 + 1024 + 512 * s) for s in range(2)]
        used[0] = work0
        kP, vN, EV, QD, LT, AT, Tm, Um, kbg, ke, vb = [[cut(512) for _ in range(2)] for _ in range(11)]
        Sm = cut(512)
        mixT = [r3(cut(1024), KT) for _ in range(2)]
        xh = [cut(1024) for _ in range(2)]
        egl = [small[:, 0:4], small[:, 4:8]]
        oss = [small[:, 8:12], small[:, 12:16]]
        osq = kbg
        gst = [cut(512), cut(512)]
        used[0] = mix0
        hr = [cut(1024) for _ in range(2)]
        h2 = [cut(1024) for _ in range(2)]
        h2j = cut(1024)
        h2T = [r3(cut(1024), KT) for _ in range(2)]
        oh = [r3(cut(256), TT) for _ in range(TOPK)]
        mask = r3(cut(256), TT)
        rank = r3(cut(256), TT)
        tot = r3(cut(256), TT)
        ptmp = r3(cut(256), TT)
        pre = r3(cut(9 * 32), 9)
        sc = [cut(32) for _ in range(12)]
        tixf = cut(64)
        desf = cut(32)
        tabf = cut(4)
        tabi = cut(4).bitcast(i32)
        zero = cut(64).bitcast(i32)
        zrow = cut(1024)
        used[0] = 0
        wslot = [r3(cut(4096), KT) for _ in range(6)]
        assert used[0] >= 0
        idx = cut(2).bitcast(i32)
        xin = r3(cut(2048), 2)
        xT = r3(cut(2048), KT)
        hT = r3(cut(2048), KT)
        yv = r3(cut(2048), KT)
        yt = r3(cut(2048), 2)
        eb = cut(24)
        gmn, umn, sg = [[cut(CAP) for _ in range(2)] for _ in range(3)]
        used[0] = 0
        yg = [[cut(1024) for _ in range(TOPK)] for _ in range(2)]
        hc = [cut(1024) for _ in range(2)]
        ho = [cut(1024) for _ in range(2)]
        hj = cut(1024)

        ps = ctx.enter_context(nc.psum_tensor("ps", [P, 8, 512], fp32))

        def bank(n):
            return ps[:, n, :]

        def heads(ap):
            return ap.rearrange("p (h c) -> p h c", h=H)

        def over_cols(ap, n=P):
            return ap.unsqueeze(2).broadcast_to([P, ap.shape[1], n])

        def over_heads(ap, n=H):
            return ap.unsqueeze(1).broadcast_to([P, n, ap.shape[1]])

        w_in_v = w_in[0].rearrange("(k p) n -> p k n", p=P)
        gu_v = exp_w_gu[0].rearrange("e (k p) (g n) -> e p k g n", p=P, g=2)
        dn_v = exp_w_down[0].rearrange("e (k p) n -> e p k n", p=P)

        def mean_eps(cell, n):
            return nc.vector.tensor_scalar(cell, cell, 1.0 / n, EPS, ALU.mult, ALU.add)

        def rsqrt(cell):
            return nc.gpsimd.tensor_tensor(cell, cell, cst[:, C_HALF:C_HALF + 1].broadcast_to([P, cell.shape[1]]), ALU.pow)

        projections = ExitStack()
        block = projections.enter_context(nc.Block())

        @block.sync
        def _(sp):
            sp.dma_start(cst[:], consts).then_inc(S("cst_in"), 16)
            for t in range(2):
                sp.dma_start(xr[t], x[0, t * P:(t + 1) * P, :]).then_inc(S("x_in", t), 16)
            p = S("par_in")
            sp.dma_start(vec_raw[0:48, :], dn_conv_w[0].rearrange("w (c p) -> (w c) p", p=P)).then_inc(p, 16)
            sp.dma_start(vec_raw[48:56, :], norm_mix_g[0].rearrange("(c p) -> c p", p=P)).then_inc(p, 16)
            sp.dma_start(vec_raw[56:60, :], gm_bs[0]).then_inc(p, 16)
            sp.dma_start(wuvz[:, :, 0:512], w_in_v[:, :, V0:V0 + W]).then_inc(S("wv_in"), 16)
            sp.dma_start(ws_raw, gm_ws[0].rearrange("h t s -> t h s")).then_inc(p, 16)
            with sp.Fori(1, TT // 2) as i:
                for s in range(2):
                    sp.wait_ge(S("xn", s), i)
                    sp.dma_start(xr[s], x[0, ds((2 * i + s) * P, P), :]).then_inc(S("x_in", s), 16)
            sp.dma_start(wuvz[:, :, 512:1024], w_in_v[:, :, U0:U0 + W]).then_inc(S("wu_in"), 16)
            sp.dma_start(wuvz[:, :, 1024:1544], w_in_v[:, :, Z0:Z0 + W + 2 * H]).then_inc(S("wz_in"), 16)
            sp.dma_start(gmg[:], gm_norm_g[0].rearrange("h c -> (h c)").partition_broadcast(P)).then_inc(p, 16)
            sp.dma_start(bgu_raw, exp_b_gu[0].rearrange("e (m p) -> (e m) p", p=P).rearrange("(q r) p -> r q p", r=P)).then_inc(p, 16)
            sp.dma_start(bd_raw, exp_b_down[0].rearrange("e (m p) -> (e m) p", p=P).rearrange("(q r) p -> r q p", r=P)).then_inc(p, 16)
            sp.dma_start(dng[:], dn_norm_g[0].partition_broadcast(P)).then_inc(p, 16)
            sp.dma_start(alog[:], dn_a_log[0].partition_broadcast(P)).then_inc(p, 16)
            sp.dma_start(dtb[:], dn_dt_bias[0].partition_broadcast(P)).then_inc(p, 16)
            sp.dma_start(rb[:], router_b[0].partition_broadcast(P)).then_inc(p, 16)
            sp.dma_start(ffn_g[:], norm_ffn_g[0].partition_broadcast(P)).then_inc(p, 16)
            sp.dma_start(fin_g[:], final_norm_g.partition_broadcast(P)).then_inc(p, 16)
            sp.dma_start(ids[:], tok_ids).then_inc(p, 16)
            sp.dma_start(rw[:], router_w[0].rearrange("(k p) e -> p k e", p=P)).then_inc(p, 16)
            for u in range(2):
                sp.dma_start(wq[u], w_in_v[:, :, Q0 + 256 * u:Q0 + 256 * (u + 1)]).then_inc(S("wq_in", u), 16)
            sp.dma_start(wout, w_out[0].rearrange("(k p) n -> p k n", p=P)).then_inc(S("wout_in"), 16)
            with sp.Fori(1, 3) as i:
                for s in range(2):
                    sp.wait_ge(S("wq_used", s), i)
                    sp.dma_start(wq[s], w_in_v[:, :, ds(512 * i + (256 * s + Q0), 256)]).then_inc(S("wq_in", s), 16)

        @block.gpsimd
        def _(pool):
            v = nc.gpsimd
            pool.wait_ge(S("cst_in"), 16)
            with pool.Fori(0, TT // 2) as i:
                for s in range(2):
                    pool.wait_ge(S("x_var", s), i + 1)
                    rsqrt(small[:, 20 + s:21 + s]).then_inc(S("x_rs", s), 1)
            pool.wait_ge(S("yT_all"), 8)
            pool.wait_ge(S("par_in"), 16 * 15)
            with pool.Fori(0, TT // 2) as i:
                for s in range(2):
                    pool.wait_ge(S("ytile_free", s), i + 1)
                    v.tensor_copy(ytile[s], yT[:, :, ds((2 * i + s) * P, P)]).then_inc(S("ytile", s), 1)
                    pool.wait_ge(S("v_var"), 2 * i + s + 1)
                    rsqrt(small[:, 16:20]).then_inc(S("v_rs"), 1)
                    pool.wait_ge(S("v_rs"), 2 * i + s + 1)
                    v.tensor_tensor(heads(vsq), heads(gv), over_cols(small[:, 16:20]), ALU.mult).then_inc(S("vn_a"), 1)
                    pool.wait_ge(S("vn_a"), 2 * i + s + 1)
                    pool.wait_ge(S("vn_free"), 2 * i + s + 1)
                    v.tensor_tensor(vn, vsq, gmg[:], ALU.mult).then_inc(S("vn"), 1)
            pool.wait_ge(S("z_silu"), 1)
            v.tensor_tensor(zs.rearrange("p t (h c) -> p (t h) c", h=H), zs.rearrange("p t (h c) -> p (t h) c", h=H),
                            over_heads(dng[:], TT * H), ALU.mult).then_inc(S("z_gain"), 1)
            pool.wait_ge(S("z_gain"), 1)
            pool.wait_ge(S("unit_done"), 16)
            pool.wait_ge(S("gates_done"), 1)
            v.memset(Sm, 0.0).then_inc(S("state_zero"), 1)
            pool.wait_ge(S("state_zero"), 1)

        @block.scalar
        def _(act):
            a = nc.scalar
            with act.Fori(0, TT // 2) as i:
                for s in range(2):
                    act.wait_ge(S("x_in", s), 16 * i + 16)
                    a.activation(sqj, xr[s], ACT.Square, accum_out=small[:, 20 + s:21 + s]).then_inc(S("x_ss", s), 1)
                    act.drain()
            with act.Fori(0, TT // 2) as i:
                for s in range(2):
                    t = 2 * i + s
                    act.wait_ge(S("v_proj"), t + 1)
                    act.wait_ge(S("gv_free"), t + 1)
                    a.activation(gv, bank(2), ACT.Gelu).then_inc(S("gv"), 1)
                    act.wait_ge(S("gv"), t + 1)
                    a.activation(vsq, gv, ACT.Square).then_inc(S("vsq"), 1)
                    act.wait_ge(S("u_proj"), t + 1)
                    act.wait_ge(S("gu_free"), t + 1)
                    a.activation(gu, bank(3), ACT.Gelu).then_inc(S("gu"), 1)
                    act.wait_ge(S("z_proj"), t + 1)
                    a.activation(zs[:, t, :], bank(4), ACT.Copy).then_inc(S("z_raw"), 1)
            act.wait_ge(S("gate_done"), 8)
            act.wait_ge(S("pad_zero"), 1)
            with act.Fori(0, 3) as i:
                for u in range(2):
                    for s in range(2):
                        act.wait_ge(S("conv_used", s), 2 * i + u + 1)
                        for hf in range(2):
                            act.wait_ge(S(f"qkv_proj{hf}", s), 2 * i + u + 1)
                            a.activation(cb[s][:, CONV - 1 + 512 * hf:CONV - 1 + 512 * (hf + 1)], bank(2 * s + hf), ACT.Copy
                                         ).then_inc(S("cb", s), 1)
                    act.sem_inc(S("wq_used", u), 1)
                    for s in range(2):
                        act.wait_ge(S("cacc", s), 2 * i + u + 1)
                        a.activation(qkvT[:, 4 * i + (2 * u + s), :], cacc[s], ACT.Silu).then_inc(S("silu", s), 1)
            act.wait_ge(S("z_raw"), 8)
            a.activation(zs.rearrange("p t c -> p (t c)"), zs.rearrange("p t c -> p (t c)"), ACT.Silu).then_inc(S("z_silu"), 1)
            for part_ in range(2):
                with act.Fori(0, 4) as i:
                    for s in range(2):
                        if part_ == 0:
                            act.wait_ge(S("usq_free", s), i + 1)
                        else:
                            act.wait_ge(S("usq_free", s), i + 5)
                        if part_ == 0:
                            act.wait_ge(S("silu", 1), 6)
                            act.wait_ge(S("silu", 0), 6)
                        a.activation(usq[s], qkvT[:, i + 4 * part_, 512 * s:512 * (s + 1)], ACT.Square).then_inc(S("usq", s), 1)
                    for s in range(2):
                        act.wait_ge(S("uss", s), i + 1 + 4 * part_)
                        act.wait_ge(S("urs_free", s), i + 1 + 4 * part_)
                        a.activation(urs[s], bank(4 + s), ACT.Sqrt, bias=cst[:, C_EPS:C_EPS + 1]).then_inc(S("urt", s), 1)
            act.wait_ge(S("ga_y"), 1)
            a.activation(bx_all[:], g_all[:], ACT.Abs)
            a.activation(small[:, 24:28], alog[:], ACT.Exp)
            act.drain()
            a.activation(bx_all[:], bx_all[:], ACT.Exp, scale=-1.0)
            a.activation(be_all[:], ab[:, :, H:2 * H], ACT.Exp, scale=-1.0)
            act.drain()
            a.activation(bx_all[:], bx_all[:], ACT.Ln, bias=1.0)
            act.drain()
            act.sem_inc(S("ga_exp"), 1)
            act.wait_ge(S("gc_ready"), 1)
            a.activation(bx_all[:], gc_all[:], ACT.Exp).then_inc(S("ga_egc"), 1)
            act.wait_ge(S("gates_done"), 1)

        @block.tensor
        def _(pe):
            t_ = nc.tensor
            pe.wait_ge(S("cst_in"), 16)
            pe.wait_ge(S("ps_zero"), 1)
            with pe.Fori(0, TT // 2) as i:
                for s in range(2):
                    pe.wait_ge(S("xn", s), i + 1)
                    pe.wait_ge(S("xT_free", s), i + 1)
                    for k in range(KT):
                        last = t_.transpose(ps[:, 2 * s + k // 4, (k % 4) * P:(k % 4 + 1) * P], xn[s][:, k * P:(k + 1) * P], ident)
                    last.then_inc(S("xT", s), 1)
                    if s == 0:
                        pass
            pe.wait_ge(S("par_in"), 16 * 15)
            t_.transpose(ps[:, 4, 384:384 + NV], vec_raw[0:NV, :], ident[0:NV, 0:NV])
            for q in range(2):
                t_.transpose(ps[:, 4, q * P:(q + 1) * P], bd_raw[:, q, :], ident)
            for q in range(4):
                t_.transpose(ps[:, 5, q * P:(q + 1) * P], bgu_raw[:, q, :], ident)
            for h in range(H):
                last = t_.transpose(ps[:, 6, h * P:(h + 1) * P], ws_raw[:, h, :], ident)
            last.then_inc(S("par_T"), 1)
            for w in ("wv_in", "wu_in", "wz_in"):
                pe.wait_ge(S(w), 16)
            pe.wait_ge(S("par_done"), 1)
            with pe.Fori(0, TT // 2) as i:
                for s in range(2):
                    t = 2 * i + s
                    pe.wait_ge(S("ytile", s), i + 1)
                    for bk, c0, width, name in ((2, 0, W, "v_proj"), (3, W, W, "u_proj"),
                                                (4, 2 * W, W, "z_proj"), (5, 3 * W, 2 * H, "ab_proj")):
                        for k in range(KT):
                            last = t_.matmul(bank(bk)[:, 0:width], ytile[s][:, k, :], wuvz[:, k, c0:c0 + width],
                                             start=(k == 0), stop=(k == KT - 1))
                        last.then_inc(S(name), 1)
                    pe.wait_ge(S("vn"), t + 1)
                    pe.wait_ge(S("gt_free"), t + 1)
                    for h in range(H):
                        last = t_.matmul(bank(6)[:, h * P:(h + 1) * P], wsT[:, h, :], vn[:, h * P:(h + 1) * P],
                                         start=True, stop=True)
                    last.then_inc(S("gate_ps"), 1)
                    pe.wait_ge(S("gu"), t + 1)
                    pe.wait_ge(S("z_raw"), t + 1)
                    pe.wait_ge(S("ab_sb"), t + 1)
            with pe.Fori(0, 3) as i:
                for s in range(2):
                    pe.wait_ge(S("wq_in", s), 16 * i + 16)
                    for ct in range(2):
                        pe.wait_ge(S("qkv_bank", ct), 2 * i + s + 1)
                        for hf in range(2):
                            for k in range(KT):
                                last = t_.matmul(bank(2 * ct + hf), wq[s][:, k, ct * P:(ct + 1) * P],
                                                 yT[:, k, 512 * hf:512 * (hf + 1)], start=(k == 0), stop=(k == KT - 1))
                            last.then_inc(S(f"qkv_proj{hf}", ct), 1)
            for part_ in range(2):
                with pe.Fori(0, 4) as i:
                    for s in range(2):
                        pe.wait_ge(S("usq", s), i + 1 + 4 * part_)
                        pe.wait_ge(S("uss_used", s), i + 1 + 4 * part_)
                        t_.matmul(bank(4 + s), ones, usq[s], start=True, stop=True).then_inc(S("uss", s), 1)
            pe.wait_ge(S("g_ready"), 1)
            t_.matmul(bank(6)[:, 0:TT * H], tri, g_all[:].rearrange("p t h -> p (t h)"), start=True, stop=True).then_inc(S("gc_ps"), 1)
            pe.wait_ge(S("gates_done"), 1)
            pe.wait_ge(S("wout_in"), 16)
            pe.wait_ge(S("state_zero"), 1)

        @block.vector
        def _(dve):
            v = nc.vector

            v.memset(ps[:], 0.0).then_inc(S("ps_zero"), 1)
            for s in range(2):
                dve.sem_inc(S("xT_free", s), 1)
            dve.wait_ge(S("cst_in"), 16)
            with dve.Fori(0, TT // 2) as i:
                for s in range(2):
                    dve.wait_ge(S("x_ss", s), i + 1)
                    mean_eps(small[:, 20 + s:21 + s], D).then_inc(S("x_var", s), 1)
                    dve.wait_ge(S("x_rs", s), i + 1)
                    v.tensor_scalar(xn[s], xr[s], small[:, 20 + s:21 + s], None, ALU.mult).then_inc(S("xn", s), 1)
                for s in range(2):
                    dve.wait_ge(S("xT", s), i + 1)
                    v.tensor_copy(yT[:, :, ds((2 * i + s) * P, P)],
                                  ps[:, 2 * s:2 * s + 2, :].rearrange("p a (b c) -> p (a b) c", b=4)).then_inc(S("xT_free", s), 1)
            dve.wait_ge(S("par_T"), 1)
            v.tensor_copy(vT[:], ps[:, 4, 384:384 + NV])
            v.tensor_copy(bd_T[:], ps[:, 4, 0:256])
            v.tensor_copy(bgu_T[:], ps[:, 5, :])
            v.tensor_tensor(wsT[:], heads(bank(6)), over_heads(tri), ALU.mult)
            dve.drain()
            for k in range(KT):
                v.tensor_scalar(yT[:, k, :], yT[:, k, :], mixg_T[:, k:k + 1], None, ALU.mult).then_inc(S("yT_all"), 1)
            for n in ("gv_free", "gu_free", "gt_free", "vn_free", "par_done"):
                dve.sem_inc(S(n), 1)
            for s in range(2):
                dve.sem_inc(S("ytile_free", s), 1)
            with dve.Fori(0, TT // 2) as i:
                for s in range(2):
                    t = 2 * i + s
                    dve.wait_ge(S("vsq"), t + 1)
                    v.tensor_reduce(small[:, 16:20], heads(vsq), AX.X, ALU.add)
                    dve.drain()
                    mean_eps(small[:, 16:20], P).then_inc(S("v_var"), 1)
                    dve.wait_ge(S("ab_proj"), t + 1)
                    dve.sem_inc(S("ytile_free", s), 1)
                    v.tensor_copy(ab[:, t, :], bank(5)[:, 0:8]).then_inc(S("ab_sb"), 1)
                    dve.wait_ge(S("gate_ps"), t + 1)
                    v.tensor_tensor(heads(gt), heads(bank(6)), over_cols(bs_T), ALU.add)
                    dve.drain()
                    dve.wait_ge(S("gu"), t + 1)
                    v.tensor_tensor(gm[:, t, :], gt, gu, ALU.mult).then_inc(S("gate_done"), 1)
                    dve.drain()
                    for n in ("gv_free", "gu_free", "gt_free", "vn_free"):
                        dve.sem_inc(S(n), 1)
            dve.drain()
            for s in range(2):
                v.memset(cb[s][:, 0:CONV - 1], 0.0)
                dve.sem_inc(S("qkv_bank", s), 1)
            dve.drain()
            for s in range(2):
                dve.sem_inc(S("conv_used", s), 1)
            dve.sem_inc(S("pad_zero"), 1)
            with dve.Fori(0, 6) as i:
                for s in range(2):
                    dve.wait_ge(S("cb", s), 2 * i + 2)
                    dve.sem_inc(S("qkv_bank", s), 1)
                    v.tensor_scalar(cacc[s], cb[s][:, 0:SEQ], conv_T[:, ds(2 * i + s, 1)], None, ALU.mult)
                    for j in range(1, CONV):
                        dve.drain()
                        last = v.scalar_tensor_tensor(cacc[s], cb[s][:, j:j + SEQ], conv_T[:, ds(2 * i + (s + 12 * j), 1)],
                                                      cacc[s], ALU.mult, ALU.add)
                    last.then_inc(S("cacc", s), 1)
                for s in range(2):
                    dve.wait_ge(S("silu", s), i + 1)
                    dve.sem_inc(S("conv_used", s), 1)
            v.tensor_tensor(g_all[:], ab[:, :, 0:H], dtb[:].unsqueeze(1).broadcast_to([P, TT, H]), ALU.add)
            dve.drain()
            dve.sem_inc(S("ga_y"), 1)
            for s in range(2):
                dve.sem_inc(S("usq_free", s), 1)
                dve.sem_inc(S("uss_used", s), 1)
                dve.sem_inc(S("urs_free", s), 1)

            def unit(part_):
                with dve.Fori(0, 4) as i:
                    for s in range(2):
                        dve.wait_ge(S("uss", s), i + 1 + 4 * part_)
                        dve.sem_inc(S("usq_free", s), 1)
                        dve.wait_ge(S("urt", s), i + 1 + 4 * part_)
                        dve.sem_inc(S("uss_used", s), 1)
                        v.reciprocal(urs[s], urs[s])
                        dve.drain()
                        cell = qkvT[:, i + 4 * part_, 512 * s:512 * (s + 1)]
                        v.scalar_tensor_tensor(cell, cell, 1.0 if part_ else P ** -0.5, urs[s], ALU.mult, ALU.mult
                                               ).then_inc(S("unit_done"), 1)
                        dve.drain()
                        dve.sem_inc(S("urs_free", s), 1)

            unit(0)
            unit(1)
            dve.wait_ge(S("ga_exp"), 1)
            v.tensor_scalar(g_all[:], g_all[:], 0.0, None, ALU.max)
            v.tensor_scalar(be_all[:], be_all[:], 1.0, None, ALU.add)
            v.tensor_scalar(small[:, 24:28], small[:, 24:28], -1.0, None, ALU.mult)
            dve.drain()
            v.tensor_tensor(g_all[:], g_all[:], bx_all[:], ALU.add)
            v.reciprocal(be_all[:], be_all[:])
            dve.drain()
            v.tensor_tensor(g_all[:], g_all[:], small[:, 24:28].unsqueeze(1).broadcast_to([P, TT, H]), ALU.mult).then_inc(S("g_ready"), 1)
            dve.wait_ge(S("gc_ps"), 1)
            v.tensor_copy(gc_all[:].rearrange("p t h -> p (t h)"), bank(6)[:, 0:TT * H]).then_inc(S("gc_ready"), 1)
            dve.wait_ge(S("ga_egc"), 1)
            v.tensor_tensor(bx_all[:], bx_all[:], be_all[:], ALU.mult).then_inc(S("gates_done"), 1)

        projections.close()
        nc.clear_and_free_semaphores(list(sems.values()))
        sems.clear()
        nc.all_engine_barrier()

        mixers = ExitStack()
        block = mixers.enter_context(nc.Block())

        @block.sync
        def _(sp):
            with sp.Fori(0, TT // 2) as i:
                sp.wait_ge(S("delta_turn"), 4 * i + 4)
                for s in range(2):
                    sp.dma_start(xh[s], x[0, ds((2 * i + s) * P, P), :]).then_inc(S("xh_in", s), 16)
                for s in range(2):
                    sp.wait_ge(S("h_ready", s), i + 1)
                    sp.dma_start(h_dram[ds((2 * i + s) * P, P), :], xh[s]).then_inc(S("h_out", s), 16)
                for s in range(2):
                    sp.wait_ge(S("h_out", s), 16 * (i + 1))
                sp.sem_inc(S("h_stored"), 1)
            with sp.Fori(0, TT // 2) as i:
                sp.wait_ge(S("route_turn"), 4 * i + 4)
                for s in range(2):
                    sp.dma_start(hr[s], h_dram[ds((2 * i + s) * P, P), :]).then_inc(S("hr_in", s), 16)
                for s in range(2):
                    sp.wait_ge(S("h2_ready", s), i + 1)
                    sp.dma_start(h2_dram[ds((2 * i + s) * P, P), :], h2[s]).then_inc(S("h2_out", s), 16)
                for s in range(2):
                    sp.wait_ge(S("h2_out", s), 16 * (i + 1))
                sp.sem_inc(S("h2_stored"), 1)

        @block.gpsimd
        def _(pool):
            v = nc.gpsimd
            pool.sem_inc(S("delta_turn"), 1)
            with pool.Fori(0, TT // 2) as i:
                pool.wait_ge(S("delta_turn"), 4 * i + 4)
                for s in range(2):
                    c = 2 * i + s
                    v.tensor_tensor(heads(Um[s]), over_heads(tri), over_cols(g_all[:, c, :]), ALU.mult).then_inc(S("GU", s), 1)
                    v.tensor_tensor(heads(Tm[s]), over_heads(ident), over_cols(be_all[:, c, :]), ALU.mult).then_inc(S("BI", s), 1)
                    v.tensor_copy(heads(kP[s]), qkvT[:, 4:8, ds(c * P, P)]).then_inc(S("kst", s), 1)
                    v.tensor_copy(heads(vN[s]), qkvT[:, 8:12, ds(c * P, P)]).then_inc(S("vst", s), 1)
                for s in range(2):
                    c = 2 * i + s
                    pool.wait_ge(S("E_exp", s), i + 1)
                    v.tensor_tensor(heads(EV[s]), heads(EV[s]), over_heads(tri), ALU.mult).then_inc(S("E", s), 1)
                    pool.wait_ge(S("EB", s), i + 1)
                    v.tensor_tensor(heads(QD[s]), heads(QD[s]), qkvT[:, 0:4, ds(c * P, P)], ALU.mult).then_inc(S("QD", s), 1)
                    v.tensor_copy(gst[s], gm[:, c, :]).then_inc(S("gst", s), 1)
                for s in range(2):
                    pool.wait_ge(S("LT", s), i + 1)
                    v.tensor_tensor(heads(Um[s]), heads(LT[s]), over_heads(m0t), ALU.mult).then_inc(S("U0a", s), 1)
                    pool.wait_ge(S("U0a", s), i + 1)
                    v.tensor_tensor(heads(Um[s]), over_heads(ident), heads(Um[s]), ALU.subtract).then_inc(S("U0", s), 1)
                for s in range(2):
                    c = 2 * i + s
                    pool.wait_ge(S("o_var", s), i + 1)
                    rsqrt(oss[s]).then_inc(S("o_rs", s), 1)
                    pool.wait_ge(S("o_norm", s), i + 1)
                    v.tensor_tensor(vb[s], vb[s], zs[:, c, :], ALU.mult).then_inc(S("o_mix", s), 1)
                pool.sem_inc(S("delta_turn"), 1)
            with pool.Fori(0, TT // 2) as i:
                for s in range(2):
                    pool.wait_ge(S("h_var", s), i + 1)
                    rsqrt(small[:, 28 + s:29 + s]).then_inc(S("h_rs", s), 1)

        @block.scalar
        def _(act):
            a = nc.scalar
            act.sem_inc(S("delta_turn"), 1)
            with act.Fori(0, TT // 2) as i:
                act.wait_ge(S("delta_turn"), 4 * i + 4)
                for s in range(2):
                    b0 = 4 * s
                    act.wait_ge(S("Bp", s), i + 1)
                    a.activation(egl[s], heads(bank(b0))[:, :, P - 1], ACT.Exp).then_inc(S("egl", s), 1)
                    a.activation(QD[s], bank(b0), ACT.Exp).then_inc(S("EB", s), 1)
                    act.wait_ge(S("dD", s), i + 1)
                    a.activation(EV[s], EV[s], ACT.Exp).then_inc(S("E_exp", s), 1)
                for s in range(2):
                    act.wait_ge(S("wT", s), i + 1)
                    a.activation(vN[s], bank(4 * s + 3), ACT.Copy, scale=-1.0).then_inc(S("nwT", s), 1)
                for s in range(2):
                    act.wait_ge(S("vnew", s), i + 1)
                    a.activation(EV[s], bank(4 * s), ACT.Copy).then_inc(S("vn_sb", s), 1)
                    act.wait_ge(S("o_ps", s), i + 1)
                    for h in range(H):
                        last = a.activation(osq[s][:, h * P:(h + 1) * P], bank(4 * s + 1)[:, h * P:(h + 1) * P], ACT.Square,
                                            accum_out=oss[s][:, h:h + 1])
                    last.then_inc(S("o_ss", s), 1)
                act.sem_inc(S("delta_turn"), 1)
            act.wait_ge(S("h_stored"), 4)
            act.sem_inc(S("route_turn"), 1)
            with act.Fori(0, TT // 2) as i:
                act.wait_ge(S("route_turn"), 4 * i + 4)
                for s in range(2):
                    act.wait_ge(S("hr_in", s), 16 * i + 16)
                    a.activation(h2j, hr[s], ACT.Square, accum_out=small[:, 28 + s:29 + s]).then_inc(S("h_ss", s), 1)
                    act.drain()
                act.sem_inc(S("route_turn"), 1)

        @block.tensor
        def _(pe):
            t_ = nc.tensor
            pe.sem_inc(S("delta_turn"), 1)

            def four(out_bank, left, right, name, start=True, stop=True):
                for h in range(H):
                    c = slice(h * P, (h + 1) * P)
                    last = t_.matmul(out_bank[:, c], left[:, c], right[:, c], start=start, stop=stop)
                last.then_inc(name, 1)

            with pe.Fori(0, TT // 2) as i:
                pe.wait_ge(S("delta_turn"), 4 * i + 4)
                for s in range(2):
                    b0 = 4 * s
                    c = 2 * i + s
                    pe.wait_ge(S("GU", s), i + 1)
                    t_.matmul(bank(b0), ones, Um[s], start=True, stop=True).then_inc(S("Bp", s), 1)
                    pe.wait_ge(S("BI", s), i + 1)
                    t_.matmul(bank(b0 + 1), ones, Tm[s], start=True, stop=True).then_inc(S("Bb", s), 1)
                    pe.wait_ge(S("kst", s), i + 1)
                    four(bank(b0 + 2), kP[s], kP[s], S("Gk", s))
                    for h in range(H):
                        last = t_.matmul(bank(b0 + 3)[:, h * P:(h + 1) * P], kP[s][:, h * P:(h + 1) * P],
                                         qkvT[:, h, ds(c * P, P)], start=True, stop=True)
                    last.then_inc(S("Gq", s), 1)
                for s in range(2):
                    b0 = 4 * s
                    pe.wait_ge(S("EB", s), i + 1)
                    pe.wait_ge(S("dD", s), i + 1)
                    for h in range(H):
                        last = t_.transpose(bank(b0)[:, h * P:(h + 1) * P], kP[s][:, h * P:(h + 1) * P], ident)
                    last.then_inc(S("kt", s), 1)
                    pe.wait_ge(S("Eb", s), i + 1)
                    pe.wait_ge(S("vst", s), i + 1)
                    for h in range(H):
                        last = t_.transpose(bank(b0 + 1)[:, h * P:(h + 1) * P], vN[s][:, h * P:(h + 1) * P], ident)
                    last.then_inc(S("vt", s), 1)
                for l in range(LEVELS):
                    for s in range(2):
                        b0 = 4 * s
                        if l == 0:
                            pe.wait_ge(S("LT", s), i + 1)
                            for h in range(H):
                                last = t_.matmul(bank(b0 + 2)[:, h * P:(h + 1) * P], LT[s][:, h * P:(h + 1) * P], ident,
                                                 start=True, stop=True)
                            last.then_inc(S("LTp", s), 1)
                        else:
                            pe.wait_ge(S("Tl", s), 6 * i + l)
                            four(bank(b0 + 2), LT[s], Tm[s], S("LTp", s))
                    for s in range(2):
                        b0 = 4 * s
                        if l == 0:
                            continue
                        if l == 1:
                            pe.wait_ge(S("U0", s), i + 1)
                            pe.wait_ge(S("kvt", s), i + 1)
                            pe.wait_ge(S("AT", s), i + 1)
                        else:
                            pe.wait_ge(S("Ul", s), 6 * i + l - 1)
                        pe.wait_ge(S("Pl", s), 6 * i + l)
                        if l < LEVELS - 1:
                            four(bank(b0 + 3), Um[s], kP[s], S("TP", s))
                        four(bank(b0), kP[s], Um[s], S("PU", s))
                for s in range(2):
                    pe.wait_ge(S("Ul", s), 6 * i + 6)
                    four(bank(4 * s + 3), kbg[s], Um[s], S("wT", s))
                for s in range(2):
                    b0 = 4 * s
                    pe.wait_ge(S("nwT", s), i + 1)
                    if s == 1:
                        pe.wait_ge(S("state"), 2 * i + 1)
                    for h in range(H):
                        c_ = slice(h * P, (h + 1) * P)
                        t_.matmul(bank(b0)[:, c_], Um[s][:, c_], vb[s][:, c_], start=True, stop=False)
                        last = t_.matmul(bank(b0)[:, c_], vN[s][:, c_], Sm[:, c_], start=False, stop=True)
                    last.then_inc(S("vnew", s), 1)
                    pe.wait_ge(S("QD", s), i + 1)
                    pe.wait_ge(S("vn_sb", s), i + 1)
                    four(bank(b0 + 2), ke[s], EV[s], S("kv", s))
                    for h in range(H):
                        c_ = slice(h * P, (h + 1) * P)
                        t_.matmul(bank(b0 + 1)[:, c_], QD[s][:, c_], Sm[:, c_], start=True, stop=False)
                        last = t_.matmul(bank(b0 + 1)[:, c_], AT[s][:, c_], EV[s][:, c_], start=False, stop=True)
                    last.then_inc(S("o_ps", s), 1)
                for s in range(2):
                    b0 = 4 * s
                    pe.wait_ge(S("gst", s), i + 1)
                    for h in range(H):
                        last = t_.transpose(bank(b0 + 3)[:, h * P:(h + 1) * P], gst[s][:, h * P:(h + 1) * P], ident)
                    last.then_inc(S("mixTa", s), 1)
                    pe.wait_ge(S("o_mix", s), i + 1)
                    for h in range(H):
                        last = t_.transpose(bank(b0)[:, h * P:(h + 1) * P], vb[s][:, h * P:(h + 1) * P], ident)
                    last.then_inc(S("mixTb", s), 1)
                for s in range(2):
                    b0 = 4 * s
                    pe.wait_ge(S("mixT", s), i + 1)
                    for n in range(2):
                        for k in range(KT):
                            last = t_.matmul(bank(b0 + 1 + n), mixT[s][:, k, :], wout[:, k, 512 * n:512 * (n + 1)],
                                             start=(k == 0), stop=(k == KT - 1))
                        last.then_inc(S("proj", s), 1)
                pe.sem_inc(S("delta_turn"), 1)
            pe.sem_inc(S("route_turn"), 1)
            with pe.Fori(0, TT // 2) as i:
                pe.wait_ge(S("route_turn"), 4 * i + 4)
                for s in range(2):
                    pe.wait_ge(S("h2_ready", s), i + 1)
                    for k in range(KT):
                        last = t_.transpose(ps[:, 4 * s + k // 4, (k % 4) * P:(k % 4 + 1) * P], h2[s][:, k * P:(k + 1) * P], ident)
                    last.then_inc(S("h2T_ps", s), 1)
                for s in range(2):
                    pe.wait_ge(S("h2T", s), i + 1)
                    for k in range(KT):
                        last = t_.matmul(bank(4 * s + 2)[:, 0:NE], h2T[s][:, k, :], rw[:, k, :], start=(k == 0), stop=(k == KT - 1))
                    last.then_inc(S("lg_ps", s), 1)
                pe.sem_inc(S("route_turn"), 1)

        @block.vector
        def _(dve):
            v = nc.vector
            dve.sem_inc(S("delta_turn"), 1)
            with dve.Fori(0, TT // 2) as i:
                dve.wait_ge(S("delta_turn"), 4 * i + 4)
                for s in range(2):
                    b0, c = 4 * s, 2 * i + s
                    dve.wait_ge(S("EB", s), i + 1)
                    v.tensor_tensor(heads(EV[s]), heads(bank(b0)), over_cols(gc_all[:, c, :]), ALU.subtract)
                    dve.drain()
                    v.tensor_scalar(EV[s], EV[s], 0.0, None, ALU.min).then_inc(S("dD", s), 1)
                for s in range(2):
                    b0, c = 4 * s, 2 * i + s
                    dve.wait_ge(S("Bb", s), i + 1)
                    dve.wait_ge(S("E", s), i + 1)
                    v.tensor_tensor(LT[s], EV[s], bank(b0 + 1), ALU.mult).then_inc(S("Eb", s), 1)
                    dve.drain()
                    dve.wait_ge(S("Gk", s), i + 1)
                    v.tensor_tensor(LT[s], LT[s], bank(b0 + 2), ALU.mult).then_inc(S("LT", s), 1)
                    dve.wait_ge(S("Gq", s), i + 1)
                    v.tensor_tensor(AT[s], EV[s], bank(b0 + 3), ALU.mult).then_inc(S("AT", s), 1)
                for s in range(2):
                    b0, c = 4 * s, 2 * i + s
                    dve.wait_ge(S("kt", s), i + 1)
                    v.tensor_tensor(heads(kbg[s]), heads(bank(b0)), over_cols(bx_all[:, c, :]), ALU.mult)
                    v.tensor_tensor(heads(ke[s]), heads(bank(b0)), heads(EV[s])[:, :, P - 1:P].broadcast_to([P, H, P]), ALU.mult)
                    dve.wait_ge(S("vt", s), i + 1)
                    v.tensor_tensor(heads(vb[s]), heads(bank(b0 + 1)), over_cols(be_all[:, c, :]), ALU.mult).then_inc(S("kvt", s), 1)
                for l in range(LEVELS):
                    for s in range(2):
                        b0 = 4 * s
                        if l == 0:
                            dve.wait_ge(S("LTp", s), 7 * i + 1)
                            v.scalar_tensor_tensor(heads(Tm[s]), heads(bank(b0 + 2)), -1.0, over_heads(level(0)), ALU.mult, ALU.mult)
                            dve.drain()
                            v.tensor_tensor(heads(Tm[s]), heads(Tm[s]), over_heads(ident), ALU.add).then_inc(S("Tl", s), 1)
                        else:
                            dve.wait_ge(S("LTp", s), 7 * i + l + 1)
                            v.tensor_tensor(heads(kP[s]), heads(bank(b0 + 2)), over_heads(level(l)), ALU.mult).then_inc(S("Pl", s), 1)
                    for s in range(2):
                        b0 = 4 * s
                        if l == 0:
                            continue
                        if l < LEVELS - 1:
                            dve.wait_ge(S("TP", s), 5 * i + l)
                            v.tensor_tensor(Tm[s], Tm[s], bank(b0 + 3), ALU.subtract).then_inc(S("Tl", s), 1)
                        dve.wait_ge(S("PU", s), 6 * i + l)
                        v.tensor_tensor(Um[s], Um[s], bank(b0), ALU.subtract).then_inc(S("Ul", s), 1)
                for s in range(2):
                    b0 = 4 * s
                    dve.wait_ge(S("kv", s), i + 1)
                    dve.wait_ge(S("egl", s), i + 1)
                    dve.wait_ge(S("o_ps", s), i + 1)
                    for h in range(H):
                        c_ = slice(h * P, (h + 1) * P)
                        last = v.scalar_tensor_tensor(Sm[:, c_], Sm[:, c_], egl[s][:, h:h + 1], bank(b0 + 2)[:, c_], ALU.mult, ALU.add)
                    last.then_inc(S("state"), 1)
                    dve.wait_ge(S("o_ss", s), i + 1)
                    mean_eps(oss[s], P).then_inc(S("o_var", s), 1)
                    dve.wait_ge(S("o_rs", s), i + 1)
                    v.tensor_tensor(heads(vb[s]), heads(bank(b0 + 1)), over_cols(oss[s]), ALU.mult).then_inc(S("o_norm", s), 1)
                for s in range(2):
                    b0 = 4 * s
                    dve.wait_ge(S("mixTa", s), i + 1)
                    v.tensor_copy(mixT[s][:, 0:4, :], heads(bank(b0 + 3)))
                    dve.wait_ge(S("mixTb", s), i + 1)
                    v.tensor_copy(mixT[s][:, 4:8, :], heads(bank(b0))).then_inc(S("mixT", s), 1)
                for s in range(2):
                    b0 = 4 * s
                    dve.wait_ge(S("xh_in", s), 16 * i + 16)
                    for n in range(2):
                        dve.wait_ge(S("proj", s), 2 * i + n + 1)
                        last = v.tensor_tensor(xh[s][:, 512 * n:512 * (n + 1)], xh[s][:, 512 * n:512 * (n + 1)], bank(b0 + 1 + n), ALU.add)
                    last.then_inc(S("h_ready", s), 1)
                dve.wait_ge(S("h_stored"), i + 1)
                dve.sem_inc(S("delta_turn"), 1)
            dve.sem_inc(S("route_turn"), 2)
            with dve.Fori(0, TT // 2) as i:
                dve.wait_ge(S("route_turn"), 4 * i + 4)
                for s in range(2):
                    dve.wait_ge(S("h_ss", s), i + 1)
                    rs = small[:, 28 + s:29 + s]
                    mean_eps(rs, D).then_inc(S("h_var", s), 1)
                    dve.wait_ge(S("h_rs", s), i + 1)
                    v.scalar_tensor_tensor(h2[s], hr[s], rs, ffn_g[:], ALU.mult, ALU.mult).then_inc(S("h2_ready", s), 1)
                for s in range(2):
                    dve.wait_ge(S("h2T_ps", s), i + 1)
                    v.tensor_copy(h2T[s], ps[:, 4 * s:4 * s + 2, :].rearrange("p a (b c) -> p (a b) c", b=4)).then_inc(S("h2T", s), 1)
                for s in range(2):
                    t = 2 * i + s
                    dve.wait_ge(S("lg_ps", s), i + 1)
                    v.tensor_tensor(lg[s], bank(4 * s + 2)[:, 0:NE], rb[:], ALU.add)
                    dve.drain()
                    v.max(best[s], lg[s])
                    dve.drain()
                    v.max_index(best_at[s], best[s], lg[s])
                    v.tensor_copy(top[:, t, :], best[s])
                    dve.drain()
                    v.tensor_copy(tix[:, t, :], best_at[s])
                dve.wait_ge(S("h2_stored"), i + 1)
                dve.sem_inc(S("route_turn"), 2)

        mixers.close()
        nc.clear_and_free_semaphores(list(sems.values()))
        sems.clear()
        nc.all_engine_barrier()

        ffn = ExitStack()
        block = ffn.enter_context(nc.Block())

        @block.sync
        def _(sp):
            sp.wait_ge(S("zeroed"), 2)
            for j in range(CAP // P):
                sp.dma_start(y_dram[SEQ * TOPK + j * P:SEQ * TOPK + (j + 1) * P, :], zrow).then_inc(S("tail_zero", j), 16)
            sp.dma_start(list_dram.rearrange("(p n) o -> p (n o)", p=P), zero[:, 0:SLOTS // P]).then_inc(S("list_zero"), 16)
            sp.wait_ge(S("tab_ready"), 1)
            sp.dma_start(tab_dram, tabi[0:NBLK, :]).then_inc(S("tab_out"), 16)
            sp.wait_ge(S("tab_out"), 16)
            sp.dma_start(tab[0:1, :], tab_dram.rearrange("(o b) c -> o (b c)", o=1)).then_inc(S("tab_in"), 16)
            sp.wait_ge(S("tab_in"), 16)
            for j in range(CAP // P):
                sp.wait_ge(S("tail_zero", j), 16)
            sp.sem_inc(S("y_tail"), 1)
            sp.wait_ge(S("plan_done"), 1)
            with sp.Fori(0, NBLK) as b:
                cnt = sp.value_load(tab[0:1, ds(b * 4 + 2, 1)], min_val=0, max_val=CAP)
                with sp.If(cnt > 0):
                    e = sp.value_load(tab[0:1, ds(b * 4, 1)], min_val=0, max_val=NE - 1)
                    row = sp.value_load(tab[0:1, ds(b * 4 + 1, 1)], min_val=0, max_val=SEQ * TOPK - 1)
                    for g in range(4):
                        sp.wait_ge(S("w_used", g), b + 1)
                        for q in range(2):
                            sp.dma_start(wslot[g][:, :, 256 * q:256 * (q + 1)],
                                         gu_v[ds(e, 1), :, :, q, 256 * g:256 * (g + 1)].rearrange("o p k n -> (o p) k n")
                                         ).then_inc(S(f"w_in{q}", g), 16)
                    for g in range(4, 6):
                        sp.wait_ge(S("w_used", g), b + 1)
                        sp.dma_start(wslot[g], dn_v[ds(e, 1), :, :, 512 * (g - 4):512 * (g - 3)].rearrange("o p k n -> (o p) k n")
                                     ).then_inc(S("w_in0", g), 16)
            sp.wait_ge(S("experts_end"), 1)
            with sp.Fori(0, TT // 2) as i:
                sp.wait_ge(S("comb_turn"), 2 * i + 2)
                for s in range(2):
                    sp.dma_start(hc[s], h_dram[ds((2 * i + s) * P, P), :]).then_inc(S("hc_in", s), 16)
                for s in range(2):
                    sp.wait_ge(S("out_ready", s), i + 1)
                    sp.dma_start(out[0, ds((2 * i + s) * P, P), :], ho[s]).then_inc(S("out_done", s), 16)
                for s in range(2):
                    sp.wait_ge(S("out_done", s), 16 * (i + 1))
                sp.sem_inc(S("out_stored"), 1)

        @block.gpsimd
        def _(pool):
            v = nc.gpsimd
            v.memset(zero, 0).then_inc(S("zeroed"), 1)
            v.memset(zrow, 0.0).then_inc(S("zeroed"), 1)
            pool.wait_ge(S("list_zero"), 16)
            pool.wait_ge(S("dest_ready"), 1)
            for t in range(TT):
                for j in range(TOPK):
                    pool.indirect_dma_start(list_dram, bass.IndirectOffsetOnAxis(ap=dest[:, t, j:j + 1], axis=0),
                                            ids[:, t:t + 1], None).then_inc(S("listed"), 16)
            pool.wait_ge(S("listed"), 16 * TT * TOPK)
            pool.wait_ge(S("tab_in"), 16)
            pool.wait_ge(S("exp_ready"), 3)
            pool.wait_ge(S("y_tail"), 1)
            pool.sem_inc(S("plan_done"), 1)
            with pool.Fori(0, NBLK) as b:
                cnt = pool.value_load(tab[0:1, ds(b * 4 + 2, 1)], min_val=0, max_val=CAP)
                with pool.If(cnt > 0):
                    row = pool.value_load(tab[0:1, ds(b * 4 + 1, 1)], min_val=0, max_val=SEQ * TOPK - 1)
                    pool.wait_ge(S("xin_free"), b + 1)
                    pool.dma_start(idx, list_dram[ds(row, CAP), :].rearrange("(j p) o -> p (j o)", p=P),
                                   allow_slow_non_contiguous=True).then_inc(S("idx_in"), 16)
                    pool.wait_ge(S("idx_in"), 16 * b + 16)
                    pool.sem_inc(S("gathering"), 1)
                    for j in range(2):
                        pool.indirect_dma_start(xin[:, j, :], None, h2_dram,
                                                bass.IndirectOffsetOnAxis(ap=idx[:, j:j + 1], axis=0)).then_inc(S("xin", j), 16)
                    for m in range(8):
                        pool.wait_ge(S("um", m % 2), 4 * b + m // 2 + 1)
                        if m == 0:
                            pool.wait_ge(S("hT_free"), b + 1)
                        v.tensor_tensor(gmn[m % 2], gmn[m % 2], umn[m % 2], ALU.mult).then_inc(S("gum", m % 2), 1)
                        pool.wait_ge(S("gum", m % 2), 4 * b + m // 2 + 1)
                        pool.wait_ge(S("sg", m % 2), 4 * b + m // 2 + 1)
                        v.tensor_tensor(hT[:, m, :], gmn[m % 2], sg[m % 2], ALU.mult).then_inc(S("hT"), 1)
                    for j in range(2):
                        pool.wait_ge(S("yt", j), b + 1)
                    pool.dma_start(y_dram[ds(row, CAP), :].rearrange("(j p) n -> p j n", p=P), yt).then_inc(S("y_out"), 16)
                    pool.wait_ge(S("y_out"), 16 * b + 16)
                    pool.sem_inc(S("yt_free"), 1)
            pool.sem_inc(S("experts_end"), 1)
            pool.wait_ge(S("exp_end"), 3)
            pool.sem_inc(S("comb_turn"), 1)
            for t in range(TT):
                i, s = t // 2, t % 2
                if s == 0:
                    pool.wait_ge(S("comb_turn"), 2 * i + 2)
                for j in range(TOPK):
                    pool.indirect_dma_start(yg[s][j], None, y_dram,
                                            bass.IndirectOffsetOnAxis(ap=dest[:, t, j:j + 1], axis=0)).then_inc(S(f"yg{j}", s), 16)
                if s == 1:
                    for r in range(2):
                        pool.wait_ge(S("f_var", r), i + 1)
                        rsqrt(small[:, 30 + r:31 + r]).then_inc(S("f_rs", r), 1)
                    pool.wait_ge(S("out_stored"), i + 1)
                    pool.sem_inc(S("comb_turn"), 1)

        @block.scalar
        def _(act):
            a = nc.scalar
            act.wait_ge(S("top_rel"), 1)
            a.activation(gates[:], gates[:], ACT.Exp).then_inc(S("top_exp"), 1)
            act.wait_ge(S("tab_in"), 16)
            act.sem_inc(S("exp_ready"), 1)
            act.wait_ge(S("plan_done"), 1)
            with act.Fori(0, NBLK) as b:
                cnt = act.value_load(tab[0:1, ds(b * 4 + 2, 1)], min_val=0, max_val=CAP)
                with act.If(cnt > 0):
                    for m in range(8):
                        act.wait_ge(S("gmn", m % 2), 4 * b + m // 2 + 1)
                        a.activation(sg[m % 2], gmn[m % 2], ACT.Sigmoid, scale=ALPHA).then_inc(S("sg", m % 2), 1)
                    act.wait_ge(S("yv_free"), b + 1)
                    for d in range(8):
                        act.wait_ge(S("down", d % 2), 4 * b + d // 2 + 1)
                        if d % 4 == 3:
                            act.sem_inc(S("w_used", 4 + d // 4), 1)
                        if d == 7:
                            act.sem_inc(S("hT_free"), 1)
                        a.activation(yv[:, d, :], bank(4 + d % 2)[:, 0:CAP], ACT.Identity, bias=eb[:, 16 + d:17 + d]
                                     ).then_inc(S("yv"), 1)
            act.sem_inc(S("exp_end"), 1)
            with act.Fori(0, TT // 2) as i:
                for s in range(2):
                    act.wait_ge(S("hsum", s), i + 1)
                    a.activation(hj, hc[s], ACT.Square, accum_out=small[:, 30 + s:31 + s]).then_inc(S("f_ss", s), 1)
                    act.drain()

        @block.tensor
        def _(pe):
            t_ = nc.tensor
            pe.wait_ge(S("mask"), 1)
            t_.matmul(bank(0)[:, 0:256], tri, mask.rearrange("p a b -> p (a b)"), start=True, stop=True)
            t_.matmul(bank(1)[:, 0:256], ones, mask.rearrange("p a b -> p (a b)"), start=True, stop=True).then_inc(S("ranks"), 1)
            pe.wait_ge(S("tab_in"), 16)
            for g in range(6):
                pe.sem_inc(S("w_used", g), 1)
            for n in ("xin_free", "hT_free", "yv_free"):
                pe.sem_inc(S(n), 1)
            pe.sem_inc(S("exp_ready"), 1)
            pe.wait_ge(S("plan_done"), 1)

            def expert(b, n):
                for m in range(8):
                    g, c = m // 2, (m % 2) * P
                    pe.wait_ge(S("gu_bank", m % 4), 2 * b + m // 4 + 1)
                    for q in range(2):
                        if m % 2 == 0:
                            pe.wait_ge(S(f"w_in{q}", g), 16 * b + 16)
                        for k in range(KT):
                            last = t_.matmul(bank(m % 4)[:, q * CAP:q * CAP + n], wslot[g][:, k, 256 * q + c:256 * q + c + P],
                                             xT[:, k, 0:n], start=(k == 0), stop=(k == KT - 1))
                    last.then_inc(S("gu_ps", m % 4), 1)
                for d in range(8):
                    g, c = 4 + d // 4, (d % 4) * P
                    if d % 4 == 0:
                        pe.wait_ge(S("w_in0", g), 16 * b + 16)
                    if d < 2:
                        pe.wait_ge(S("down_bank", d), b + 1)
                    else:
                        pe.wait_ge(S("yv"), 8 * b + d - 1)
                    for k in range(KT):
                        if d == 0:
                            pe.wait_ge(S("hT"), 8 * b + k + 1)
                        last = t_.matmul(bank(4 + d % 2)[:, 0:n], wslot[g][:, k, c:c + P], hT[:, k, 0:n],
                                         start=(k == 0), stop=(k == KT - 1))
                    last.then_inc(S("down", d % 2), 1)

            with pe.Fori(0, NBLK) as b:
                cnt = pe.value_load(tab[0:1, ds(b * 4 + 2, 1)], min_val=0, max_val=CAP)
                with pe.If(cnt > 0):
                    for j in range(2):
                        pe.wait_ge(S("xin", j), 16 * b + 16)
                        for r in range(2):
                            n = 2 * j + r
                            pe.wait_ge(S("tr_bank", r), 4 * b + j + 1)
                            for k in range(4):
                                last = t_.transpose(bank(6 + r)[:, k * P:(k + 1) * P],
                                                    xin[:, j, (4 * r + k) * P:(4 * r + k + 1) * P], ident)
                            last.then_inc(S("xT_ps", r), 1)
                    pe.wait_ge(S("xT_sb"), 4 * b + 4)
                    with pe.If(cnt > 160):
                        with pe.If(cnt > 192):
                            expert(b, 256)
                        with pe.Else():
                            expert(b, 192)
                    with pe.Else():
                        with pe.If(cnt > 128):
                            expert(b, 160)
                        with pe.Else():
                            expert(b, 128)
                    pe.wait_ge(S("yv"), 8 * b + 8)
                    for j in range(2):
                        for r in range(2):
                            pe.wait_ge(S("tr_bank", r), 4 * b + j + 3)
                            for k in range(4):
                                last = t_.transpose(bank(6 + r)[:, k * P:(k + 1) * P], yv[:, 4 * r + k, j * P:(j + 1) * P], ident)
                            last.then_inc(S("yt_ps", r), 1)
            pe.sem_inc(S("exp_end"), 1)

        @block.vector
        def _(dve):
            v = nc.vector
            v.tensor_tensor(gates[:], top[:, :, 0:TOPK], top[:, :, 0:1].broadcast_to([P, TT, TOPK]), ALU.subtract).then_inc(S("top_rel"), 1)
            v.tensor_copy(r3(tixf, TT), tix[:])
            dve.drain()
            for j in range(TOPK):
                v.tensor_tensor(oh[j], iota_e.unsqueeze(1).broadcast_to([P, TT, NE]),
                                r3(tixf, TT)[:, :, j:j + 1].broadcast_to([P, TT, NE]), ALU.is_equal)
            dve.drain()
            v.tensor_tensor(mask, oh[0], oh[1], ALU.add)
            v.tensor_tensor(ptmp, oh[2], oh[3], ALU.add)
            dve.drain()
            v.tensor_tensor(mask, mask, ptmp, ALU.add).then_inc(S("mask"), 1)
            dve.wait_ge(S("top_exp"), 1)
            gs = sc[11][:, 0:TT]
            v.tensor_reduce(gs, gates[:], AX.X, ALU.add)
            dve.drain()
            v.reciprocal(gs, gs)
            dve.drain()
            v.tensor_tensor(gates[:], gates[:], gs.unsqueeze(2).broadcast_to([P, TT, TOPK]), ALU.mult)
            dve.wait_ge(S("ranks"), 1)
            v.tensor_copy(tot.rearrange("p a b -> p (a b)"), bank(1)[:, 0:256])
            v.memset(pre[:, 0, :], 0.0)
            dve.drain()
            for t in range(TT):
                v.tensor_tensor(pre[:, t + 1, :], pre[:, t, :], tot[:, t, :], ALU.add)
                dve.drain()
            count = pre[:, TT, :]

            def running(o, src, spare):
                v.tensor_copy(o, src)
                dve.drain()
                sh = 1
                while sh < NE:
                    v.tensor_copy(spare, o)
                    dve.drain()
                    v.tensor_tensor(o[:, sh:NE], spare[:, sh:NE], spare[:, 0:NE - sh], ALU.add)
                    dve.drain()
                    sh *= 2

            start, cblk, nblk, t0, t1, onehot, before = sc[0:7]
            running(start, count, t0)
            v.tensor_tensor(start, start, count, ALU.subtract)
            dve.drain()
            v.tensor_tensor(rank, bank(0)[:, 0:256].rearrange("p (a b) -> p a b", a=TT), pre[:, 0:TT, :], ALU.add)
            dve.drain()
            v.tensor_tensor(rank, rank, start.unsqueeze(1).broadcast_to([P, TT, NE]), ALU.add)
            dve.drain()
            for j in range(TOPK):
                v.tensor_tensor(oh[j], oh[j], rank, ALU.mult)
            dve.drain()
            for j in range(TOPK):
                v.tensor_reduce(r3(desf, TT)[:, :, j], oh[j], AX.X, ALU.add)
            dve.drain()
            v.tensor_scalar(dest[:].rearrange("p t j -> p (t j)"), desf, -1.0, None, ALU.add).then_inc(S("dest_ready"), 1)
            v.tensor_scalar(nblk, count, 0.0, None, ALU.is_gt)
            for n in range(1, SEQ // CAP):
                v.tensor_scalar(t0, count, float(n * CAP), None, ALU.is_gt)
                dve.drain()
                v.tensor_tensor(nblk, nblk, t0, ALU.add)
                dve.drain()
            running(cblk, nblk, t0)
            v.tensor_tensor(before, cblk, nblk, ALU.subtract)
            dve.drain()
            v.tensor_scalar(t0, before, part, None, ALU.is_le)
            v.tensor_scalar(t1, cblk, part, None, ALU.is_gt)
            dve.drain()
            v.tensor_tensor(onehot, t0, t1, ALU.mult)
            v.tensor_scalar(before, before, part, -float(CAP), ALU.subtract, ALU.mult)
            dve.drain()
            v.tensor_tensor(t0, start, before, ALU.add)
            v.tensor_tensor(t1, count, before, ALU.subtract)
            dve.drain()
            v.tensor_tensor(t0, t0, onehot, ALU.mult)
            v.tensor_tensor(t1, t1, onehot, ALU.mult)
            v.tensor_tensor(sc[7], iota_e, onehot, ALU.mult)
            dve.drain()
            v.tensor_reduce(tabf[:, 0:1], sc[7], AX.X, ALU.add)
            v.tensor_reduce(tabf[:, 1:2], t0, AX.X, ALU.add)
            v.tensor_reduce(tabf[:, 2:3], t1, AX.X, ALU.add)
            v.memset(tabf[:, 3:4], 0.0)
            dve.drain()
            v.tensor_scalar(tabf[:, 2:3], tabf[:, 2:3], float(CAP), None, ALU.min)
            dve.drain()
            v.tensor_copy(tabi, tabf).then_inc(S("tab_ready"), 1)
            dve.wait_ge(S("tab_in"), 16)
            for m in range(4):
                dve.sem_inc(S("gu_bank", m), 1)
            for r in range(2):
                dve.sem_inc(S("down_bank", r), 1)
                dve.sem_inc(S("tr_bank", r), 1)
            dve.sem_inc(S("exp_ready"), 1)
            dve.wait_ge(S("plan_done"), 1)
            dve.sem_inc(S("yt_free"), 1)
            with dve.Fori(0, NBLK) as b:
                cnt = dve.value_load(tab[0:1, ds(b * 4 + 2, 1)], min_val=0, max_val=CAP)
                with dve.If(cnt > 0):
                    e = dve.value_load(tab[0:1, ds(b * 4, 1)], min_val=0, max_val=NE - 1)
                    v.tensor_copy(eb[:, 0:16], bgu_T[:, ds(e * 16, 16)])
                    v.tensor_copy(eb[:, 16:24], bd_T[:, ds(e * 8, 8)])
                    for j in range(2):
                        for r in range(2):
                            dve.wait_ge(S("xT_ps", r), 2 * b + j + 1)
                            v.tensor_copy(xT[:, 4 * r:4 * r + 4, j * P:(j + 1) * P], heads(bank(6 + r))).then_inc(S("xT_sb"), 1)
                            dve.drain()
                            dve.sem_inc(S("tr_bank", r), 1)
                    dve.sem_inc(S("xin_free"), 1)
                    for m in range(8):
                        r = m % 2
                        dve.wait_ge(S("gu_ps", m % 4), 2 * b + m // 4 + 1)
                        if m % 2 == 1:
                            dve.sem_inc(S("w_used", m // 2), 1)
                        if m >= 2:
                            dve.wait_ge(S("hT"), 8 * b + m - 1)
                        v.tensor_scalar(gmn[r], bank(m % 4)[:, 0:CAP], eb[:, m:m + 1], LIMIT, ALU.add, ALU.min).then_inc(S("gmn", r), 1)
                        v.tensor_scalar(umn[r], bank(m % 4)[:, CAP:2 * CAP], eb[:, 8 + m:9 + m], LIMIT, ALU.add, ALU.min)
                        dve.drain()
                        dve.sem_inc(S("gu_bank", m % 4), 1)
                        v.tensor_scalar(umn[r], umn[r], -LIMIT, 1.0, ALU.max, ALU.add)
                        dve.drain()
                        dve.wait_ge(S("sg", r), 4 * b + m // 2 + 1)
                        dve.sem_inc(S("um", r), 1)
                    dve.wait_ge(S("hT"), 8 * b + 8)
                    dve.wait_ge(S("yv"), 8 * b + 8)
                    for r in range(2):
                        dve.sem_inc(S("down_bank", r), 1)
                    dve.wait_ge(S("yt_free"), b + 1)
                    for j in range(2):
                        for r in range(2):
                            dve.wait_ge(S("yt_ps", r), 2 * b + j + 1)
                            v.tensor_copy(yt[:, j, 512 * r:512 * (r + 1)], bank(6 + r))
                            dve.drain()
                            dve.sem_inc(S("tr_bank", r), 1)
                        dve.sem_inc(S("yt", j), 1)
                    dve.sem_inc(S("yv_free"), 1)
            dve.sem_inc(S("exp_end"), 1)
            dve.sem_inc(S("comb_turn"), 1)
            with dve.Fori(0, TT // 2) as i:
                for s in range(2):
                    dve.wait_ge(S("hc_in", s), 16 * i + 16)
                    for j in range(TOPK):
                        dve.wait_ge(S(f"yg{j}", s), 16 * i + 16)
                        last = v.scalar_tensor_tensor(hc[s], yg[s][j], gates[:, 2 * i + s, j:j + 1], hc[s], ALU.mult, ALU.add)
                        dve.drain()
                    dve.sem_inc(S("hsum", s), 1)
                for s in range(2):
                    dve.wait_ge(S("f_ss", s), i + 1)
                    rs = small[:, 30 + s:31 + s]
                    mean_eps(rs, D).then_inc(S("f_var", s), 1)
                    dve.wait_ge(S("f_rs", s), i + 1)
                    v.scalar_tensor_tensor(ho[s], hc[s], rs, fin_g[:], ALU.mult, ALU.mult).then_inc(S("out_ready", s), 1)
                dve.wait_ge(S("out_stored"), i + 1)
                dve.sem_inc(S("comb_turn"), 1)

        ffn.close()


_INS = ["x", "norm_mix_g", "w_in", "gm_norm_g", "gm_ws", "gm_bs", "dn_conv_w", "dn_a_log", "dn_dt_bias", "dn_norm_g",
        "w_out", "norm_ffn_g", "router_w", "router_b", "exp_w_gu", "exp_b_gu", "exp_w_down", "exp_b_down", "final_norm_g"]


def _constants(np):
    i = np.arange(P)
    row, col = i[:, None], i[None, :]
    c = np.zeros((P, NCST), np.float32)
    c[:, C_ID:C_ID + P] = row == col
    c[:, C_TRI:C_TRI + P] = row <= col
    c[:, C_ONE:C_ONE + P] = 1.0
    for l in range(LEVELS):
        c[:, C_LV + P * l:C_LV + P * (l + 1)] = ((row >> l) ^ (col >> l) == 1) & (row > col)
    c[:, C_M0T:C_M0T + P] = ((row ^ col) == 1) & (row < col)
    c[:, C_IOTA:C_IOTA + NE] = np.arange(NE)
    c[:, C_PART] = i
    c[:, C_HALF], c[:, C_EPS] = -0.5, EPS
    return c, (np.arange(TT)[None, :] * P + i[:, None]).astype(np.int32)


def kernel(**inputs):
    import numpy as np
    import concourse.bacc as bacc
    from concourse.bass_utils import run_bass_kernel_spmd as run

    dt = mybir.dt
    nc = bacc.Bacc("TRN2", target_bir_lowering=False, num_devices=1)
    arrays, args = {}, []
    for name in _INS:
        a = np.ascontiguousarray(inputs[name])
        arrays[f"in_{name}"] = a
        args.append(nc.dram_tensor(f"in_{name}", a.shape, dt.float32, kind="ExternalInput").ap())
    arrays["consts"], arrays["tok_ids"] = _constants(np)
    args.append(nc.dram_tensor("consts", (P, NCST), dt.float32, kind="ExternalInput").ap())
    args.append(nc.dram_tensor("tok_ids", (P, TT), dt.int32, kind="ExternalInput").ap())
    args.append(nc.dram_tensor("out", (1, SEQ, D), dt.float32, kind="ExternalOutput").ap())
    kind = "Internal"
    args.append(nc.dram_tensor("h_dram", (SEQ, D), dt.float32, kind=kind).ap())
    args.append(nc.dram_tensor("h2_dram", (SEQ, D), dt.float32, kind=kind).ap())
    args.append(nc.dram_tensor("list_dram", (SLOTS, 1), dt.int32, kind=kind).ap())
    args.append(nc.dram_tensor("tab_dram", (NBLK, 4), dt.int32, kind=kind).ap())
    args.append(nc.dram_tensor("y_dram", (SLOTS, D), dt.float32, kind="Internal").ap())
    program(nc, *args, None)
    r = run(nc, [arrays], core_ids=[0])
    return r.results[0]["out"]
```

```python
import concourse.bass as bass
from concourse import mybir
from contextlib import ExitStack

D, SEQ, P = 1024, 1024, 128
KT, TT = D // P, SEQ // P
H, W = 4, 512
NE, TOPK, F = 32, 4, 1024
CONV = 4
EPS = 1e-6
LIMIT, ALPHA = 7.0, 1.702
CAP = 256
NBLK = NE + SEQ * TOPK // CAP
WIDTHS = (112, 128, 144, 160, 192, CAP)
SLOTS = SEQ * TOPK + CAP
U0, V0, Q0, Z0, A0 = 0, W, 2 * W, 5 * W, 6 * W
LROWS = NE * SEQ + CAP
TABC = 5
LEVELS = 7
C_ID, C_TRI, C_ONE, C_M0T, C_LV = 0, 128, 256, 384, 512
C_IOTA = C_LV + LEVELS * 128
C_PART = C_IOTA + NE
C_HALF, C_EPS = C_PART + 1, C_PART + 2
NCST = C_PART + 3


def program(nc, x, norm_mix_g, w_in, gm_norm_g, gm_ws, gm_bs, dn_conv_w, dn_a_log, dn_dt_bias,
            dn_norm_g, w_out, norm_ffn_g, router_w, router_b, exp_w_gu, exp_b_gu, exp_w_down,
            exp_b_down, final_norm_g, consts, tok_ids, out, h_dram, h2_dram, list_dram, tab_dram,
            y_dram, dbg=None):
    fp32, i32, u32 = mybir.dt.float32, mybir.dt.int32, mybir.dt.uint32
    ALU, ACT, AX = mybir.AluOpType, mybir.ActivationFunctionType, mybir.AxisListType
    ds = bass.ds
    ctx = ExitStack()
    with ctx:
        def sb(name, shape, dt=fp32):
            return ctx.enter_context(nc.sbuf_tensor(name, shape, dt))

        sems = {}

        def S(name, slot=None):
            key = name if slot is None else f"{name}_{slot}"
            if key not in sems:
                sems[key] = nc.alloc_semaphore(name=key)
            return sems[key]

        cst = sb("cst", [P, NCST])
        ident, tri, ones = cst[:, 0:128], cst[:, 128:256], cst[:, 256:384]
        m0t = cst[:, C_M0T:C_M0T + 128]
        iota_e, part = cst[:, C_IOTA:C_IOTA + NE], cst[:, C_PART:C_PART + 1]

        def level(l):
            return cst[:, C_LV + 128 * l:C_LV + 128 * (l + 1)]

        ids = sb("ids", [P, TT], i32)
        ffn_g = sb("ffn_g", [P, D])
        fin_g = sb("fin_g", [P, D])
        gmg = sb("gmg", [P, W])
        dng = sb("dng", [P, P])
        rb = sb("rb", [P, NE])
        alog = sb("alog", [P, H])
        dtb = sb("dtb", [P, H])
        NV = CONV * 12 + KT + H
        vT = sb("vT", [P, NV])
        conv_T, mixg_T, bs_T = vT[:, 0:48], vT[:, 48:56], vT[:, 56:60]
        bgu_T = sb("bgu_T", [P, NE * 16])
        bd_T = sb("bd_T", [P, NE * KT])
        rw = sb("rw", [P, KT, NE])
        wsT = sb("wsT", [P, H, P])
        small = sb("small", [P, 160])
        g_all, be_all = sb("g_all", [P, TT, H]), sb("be_all", [P, TT, H])
        gc_all, bx_all = sb("gc_all", [P, TT, H]), sb("bx_all", [P, TT, H])
        ab = sb("ab", [P, TT, 2 * H])
        lg = [small[:, 64 + 32 * s:96 + 32 * s] for s in range(2)]
        best = [small[:, 128 + 8 * s:136 + 8 * s] for s in range(2)]
        best_at = [small[:, 144 + 8 * s:152 + 8 * s].bitcast(u32) for s in range(2)]
        top = sb("top", [P, TT, 8])
        gates = sb("gates", [P, TT, TOPK])
        dest = sb("dest", [P, TT, TOPK], i32)
        tixf = sb("tixf", [P, TT, TOPK])
        ranks = sb("ranks", [P, TT, TOPK])
        count = sb("count", [P, NE])
        tab = sb("tab", [1, (NBLK + 1) * TABC], i32)

        AW = 45632
        arena = sb("arena", [P, AW])
        used = [0]

        def cut(cols, at=None):
            a = used[0] if at is None else at
            if at is None:
                used[0] += cols
            assert a + cols <= AW, (a, cols)
            return arena[:, a:a + cols]

        def r3(ap, n):
            return ap.rearrange("p (a b) -> p a b", a=n)

        wout = r3(cut(8192), KT)
        mix0 = used[0]
        gm = r3(cut(4096), TT)
        zs = r3(cut(4096), TT)
        big0 = used[0]
        wuvz = r3(cut(KT * 1544), KT)
        qkvT = r3(cut(KT * 1536, big0), 12)
        work0 = used[0]
        yT = r3(cut(8192), KT)
        wq = [r3(cut(2048), KT) for _ in range(2)]
        tmp0 = used[0]
        ytile = [r3(cut(1024), KT) for _ in range(2)]
        gv, vsq, vn, gu, gt = [cut(512) for _ in range(5)]
        mixer_end = used[0]
        xr = [cut(1024, mix0 + 1024 * s) for s in range(2)]
        xn = [cut(1024, mix0 + 2048 + 1024 * s) for s in range(2)]
        sqj = cut(1024, mix0 + 4096)
        vec_raw = cut(128, mix0 + 5120)
        bgu_raw = r3(cut(512, mix0 + 5248), 4)
        bd_raw = r3(cut(256, mix0 + 5760), 2)
        ws_raw = r3(cut(512, mix0 + 6016), H)
        cb = [cut(CONV - 1 + SEQ, tmp0 + 1028 * s) for s in range(2)]
        cacc = [cut(1024, tmp0 + 2056 + 1024 * s) for s in range(2)]
        usq = [cut(512, work0 + 512 * s) for s in range(2)]
        urs = [cut(512, work0 + 1024 + 512 * s) for s in range(2)]
        used[0] = work0
        kP, vN, EV, QD, LT, AT, Tm, Um, kbg, ke, vb = [[cut(512) for _ in range(2)] for _ in range(11)]
        Sm = cut(512)
        mixT = [r3(cut(1024), KT) for _ in range(2)]
        xh = [cut(1024) for _ in range(2)]
        egl = [small[:, 0:4], small[:, 4:8]]
        oss = [small[:, 8:12], small[:, 12:16]]
        osq = kbg
        gst = [cut(512), cut(512)]
        used[0] = mix0
        hr = [cut(1024) for _ in range(2)]
        h2 = [cut(1024) for _ in range(2)]
        h2j = cut(1024)
        h2T = [r3(cut(1024), KT) for _ in range(2)]
        oh = [cut(128).rearrange("p (j e) -> p j e", j=TOPK) for _ in range(2)]
        ohr = [cut(128).rearrange("p (j e) -> p j e", j=TOPK) for _ in range(2)]
        msk, rnk = [[cut(32) for _ in range(2)] for _ in range(2)]
        ixf, rkf = [[cut(4) for _ in range(2)] for _ in range(2)]
        ldest = [cut(4).bitcast(i32) for _ in range(2)]
        lid = [cut(1).bitcast(i32) for _ in range(2)]
        zero = cut(264).bitcast(i32)
        used[0] = 6 * 4096
        sc = [cut(32) for _ in range(10)]
        zrow = cut(1024)
        big = cut(1024).rearrange("p (a b) -> p a b", b=NE)
        desf = cut(32)
        tabf = cut(TABC)
        tabi = cut(TABC).bitcast(i32)
        gs = cut(TT)
        used[0] = 0
        wslot = [r3(cut(4096), KT) for _ in range(6)]
        assert used[0] >= 0
        assert used[0] == 6 * 4096
        used[0] = 6 * 4096 + 4096
        idx = cut(2).bitcast(i32)
        xin = r3(cut(2048), 2)
        xT = r3(cut(2048), KT)
        hT = r3(cut(2048), KT)
        yv = r3(cut(2048), KT)
        yt = r3(cut(2048), 2)
        eb = cut(24)
        gmn, umn, sg = [[cut(CAP) for _ in range(2)] for _ in range(3)]
        used[0] = 0
        yg = [[cut(1024) for _ in range(TOPK)] for _ in range(4)]
        hc = [cut(1024) for _ in range(4)]
        ho = [cut(1024) for _ in range(4)]
        hj = cut(1024)

        ps = ctx.enter_context(nc.psum_tensor("ps", [P, 8, 512], fp32))

        def bank(n):
            return ps[:, n, :]

        def heads(ap):
            return ap.rearrange("p (h c) -> p h c", h=H)

        def over_cols(ap, n=P):
            return ap.unsqueeze(2).broadcast_to([P, ap.shape[1], n])

        def over_heads(ap, n=H):
            return ap.unsqueeze(1).broadcast_to([P, n, ap.shape[1]])

        w_in_v = w_in[0].rearrange("(k p) n -> p k n", p=P)
        gu_v = exp_w_gu[0].rearrange("e (k p) (g n) -> e p k g n", p=P, g=2)
        dn_v = exp_w_down[0].rearrange("e (k p) n -> e p k n", p=P)

        def mean_eps(cell, n):
            return nc.vector.tensor_scalar(cell, cell, 1.0 / n, EPS, ALU.mult, ALU.add)

        def rsqrt(cell):
            return nc.gpsimd.tensor_tensor(cell, cell, cst[:, C_HALF:C_HALF + 1].broadcast_to([P, cell.shape[1]]), ALU.pow)

        projections = ExitStack()
        block = projections.enter_context(nc.Block())

        @block.sync
        def _(sp):
            sp.dma_start(cst[:], consts).then_inc(S("cst_in"), 16)
            for t in range(2):
                sp.dma_start(xr[t], x[0, t * P:(t + 1) * P, :]).then_inc(S("x_in", t), 16)
            p = S("par_in")
            sp.dma_start(vec_raw[0:48, :], dn_conv_w[0].rearrange("w (c p) -> (w c) p", p=P)).then_inc(p, 16)
            sp.dma_start(vec_raw[48:56, :], norm_mix_g[0].rearrange("(c p) -> c p", p=P)).then_inc(p, 16)
            sp.dma_start(vec_raw[56:60, :], gm_bs[0]).then_inc(p, 16)
            sp.dma_start(wuvz[:, :, 0:512], w_in_v[:, :, V0:V0 + W]).then_inc(S("wv_in"), 16)
            sp.dma_start(ws_raw, gm_ws[0].rearrange("h t s -> t h s")).then_inc(p, 16)
            with sp.Fori(1, TT // 2) as i:
                for s in range(2):
                    sp.wait_ge(S("xn", s), i)
                    sp.dma_start(xr[s], x[0, ds((2 * i + s) * P, P), :]).then_inc(S("x_in", s), 16)
            sp.dma_start(wuvz[:, :, 512:1024], w_in_v[:, :, U0:U0 + W]).then_inc(S("wu_in"), 16)
            sp.dma_start(wuvz[:, :, 1024:1544], w_in_v[:, :, Z0:Z0 + W + 2 * H]).then_inc(S("wz_in"), 16)
            sp.dma_start(gmg[:], gm_norm_g[0].rearrange("h c -> (h c)").partition_broadcast(P)).then_inc(p, 16)
            sp.dma_start(bgu_raw, exp_b_gu[0].rearrange("e (m p) -> (e m) p", p=P).rearrange("(q r) p -> r q p", r=P)).then_inc(p, 16)
            sp.dma_start(bd_raw, exp_b_down[0].rearrange("e (m p) -> (e m) p", p=P).rearrange("(q r) p -> r q p", r=P)).then_inc(p, 16)
            sp.dma_start(dng[:], dn_norm_g[0].partition_broadcast(P)).then_inc(p, 16)
            sp.dma_start(alog[:], dn_a_log[0].partition_broadcast(P)).then_inc(p, 16)
            sp.dma_start(dtb[:], dn_dt_bias[0].partition_broadcast(P)).then_inc(p, 16)
            sp.dma_start(rb[:], router_b[0].partition_broadcast(P)).then_inc(p, 16)
            sp.dma_start(ffn_g[:], norm_ffn_g[0].partition_broadcast(P)).then_inc(p, 16)
            sp.dma_start(fin_g[:], final_norm_g.partition_broadcast(P)).then_inc(p, 16)
            sp.dma_start(ids[:], tok_ids).then_inc(p, 16)
            sp.dma_start(rw[:], router_w[0].rearrange("(k p) e -> p k e", p=P)).then_inc(p, 16)
            for u in range(2):
                sp.dma_start(wq[u], w_in_v[:, :, Q0 + 256 * u:Q0 + 256 * (u + 1)]).then_inc(S("wq_in", u), 16)
            sp.dma_start(wout, w_out[0].rearrange("(k p) n -> p k n", p=P)).then_inc(S("wout_in"), 16)
            with sp.Fori(1, 3) as i:
                for s in range(2):
                    sp.wait_ge(S("wq_used", s), i)
                    sp.dma_start(wq[s], w_in_v[:, :, ds(512 * i + (256 * s + Q0), 256)]).then_inc(S("wq_in", s), 16)

        @block.gpsimd
        def _(pool):
            v = nc.gpsimd
            pool.wait_ge(S("cst_in"), 16)
            with pool.Fori(0, TT // 2) as i:
                for s in range(2):
                    pool.wait_ge(S("x_var", s), i + 1)
                    rsqrt(small[:, 20 + s:21 + s]).then_inc(S("x_rs", s), 1)
            pool.wait_ge(S("yT_all"), 8)
            pool.wait_ge(S("par_in"), 16 * 15)
            with pool.Fori(0, TT // 2) as i:
                for s in range(2):
                    pool.wait_ge(S("ytile_free", s), i + 1)
                    v.tensor_copy(ytile[s], yT[:, :, ds((2 * i + s) * P, P)]).then_inc(S("ytile", s), 1)
                    pool.wait_ge(S("v_var"), 2 * i + s + 1)
                    rsqrt(small[:, 16:20]).then_inc(S("v_rs"), 1)
                    pool.wait_ge(S("v_rs"), 2 * i + s + 1)
                    v.tensor_tensor(heads(vsq), heads(gv), over_cols(small[:, 16:20]), ALU.mult).then_inc(S("vn_a"), 1)
                    pool.wait_ge(S("vn_a"), 2 * i + s + 1)
                    pool.wait_ge(S("vn_free"), 2 * i + s + 1)
                    v.tensor_tensor(vn, vsq, gmg[:], ALU.mult).then_inc(S("vn"), 1)
            pool.wait_ge(S("z_silu"), 1)
            v.tensor_tensor(zs.rearrange("p t (h c) -> p (t h) c", h=H), zs.rearrange("p t (h c) -> p (t h) c", h=H),
                            over_heads(dng[:], TT * H), ALU.mult).then_inc(S("z_gain"), 1)
            pool.wait_ge(S("z_gain"), 1)
            pool.wait_ge(S("unit_done"), 16)
            pool.wait_ge(S("gates_done"), 1)
            v.memset(Sm, 0.0).then_inc(S("state_zero"), 1)
            pool.wait_ge(S("state_zero"), 1)

        @block.scalar
        def _(act):
            a = nc.scalar
            with act.Fori(0, TT // 2) as i:
                for s in range(2):
                    act.wait_ge(S("x_in", s), 16 * i + 16)
                    a.activation(sqj, xr[s], ACT.Square, accum_out=small[:, 20 + s:21 + s]).then_inc(S("x_ss", s), 1)
                    act.drain()
            with act.Fori(0, TT // 2) as i:
                for s in range(2):
                    t = 2 * i + s
                    act.wait_ge(S("v_proj"), t + 1)
                    act.wait_ge(S("gv_free"), t + 1)
                    a.activation(gv, bank(2), ACT.Gelu).then_inc(S("gv"), 1)
                    act.wait_ge(S("gv"), t + 1)
                    a.activation(vsq, gv, ACT.Square).then_inc(S("vsq"), 1)
                    act.wait_ge(S("u_proj"), t + 1)
                    act.wait_ge(S("gu_free"), t + 1)
                    a.activation(gu, bank(3), ACT.Gelu).then_inc(S("gu"), 1)
                    act.wait_ge(S("z_proj"), t + 1)
                    a.activation(zs[:, t, :], bank(4), ACT.Copy).then_inc(S("z_raw"), 1)
            act.wait_ge(S("gate_done"), 8)
            act.wait_ge(S("pad_zero"), 1)
            with act.Fori(0, 3) as i:
                for u in range(2):
                    for s in range(2):
                        act.wait_ge(S("conv_used", s), 2 * i + u + 1)
                        for hf in range(2):
                            act.wait_ge(S(f"qkv_proj{hf}", s), 2 * i + u + 1)
                            a.activation(cb[s][:, CONV - 1 + 512 * hf:CONV - 1 + 512 * (hf + 1)], bank(2 * s + hf), ACT.Copy
                                         ).then_inc(S("cb", s), 1)
                    act.sem_inc(S("wq_used", u), 1)
                    for s in range(2):
                        act.wait_ge(S("cacc", s), 2 * i + u + 1)
                        a.activation(qkvT[:, 4 * i + (2 * u + s), :], cacc[s], ACT.Silu).then_inc(S("silu", s), 1)
            act.wait_ge(S("z_raw"), 8)
            a.activation(zs.rearrange("p t c -> p (t c)"), zs.rearrange("p t c -> p (t c)"), ACT.Silu).then_inc(S("z_silu"), 1)
            for part_ in range(2):
                with act.Fori(0, 4) as i:
                    for s in range(2):
                        if part_ == 0:
                            act.wait_ge(S("usq_free", s), i + 1)
                        else:
                            act.wait_ge(S("usq_free", s), i + 5)
                        if part_ == 0:
                            act.wait_ge(S("silu", 1), 6)
                            act.wait_ge(S("silu", 0), 6)
                        a.activation(usq[s], qkvT[:, i + 4 * part_, 512 * s:512 * (s + 1)], ACT.Square).then_inc(S("usq", s), 1)
                    for s in range(2):
                        act.wait_ge(S("uss", s), i + 1 + 4 * part_)
                        act.wait_ge(S("urs_free", s), i + 1 + 4 * part_)
                        a.activation(urs[s], bank(4 + s), ACT.Sqrt, bias=cst[:, C_EPS:C_EPS + 1]).then_inc(S("urt", s), 1)
            act.wait_ge(S("ga_y"), 1)
            a.activation(bx_all[:], g_all[:], ACT.Abs)
            a.activation(small[:, 24:28], alog[:], ACT.Exp)
            act.drain()
            a.activation(bx_all[:], bx_all[:], ACT.Exp, scale=-1.0)
            a.activation(be_all[:], ab[:, :, H:2 * H], ACT.Exp, scale=-1.0)
            act.drain()
            a.activation(bx_all[:], bx_all[:], ACT.Ln, bias=1.0)
            act.drain()
            act.sem_inc(S("ga_exp"), 1)
            act.wait_ge(S("gc_ready"), 1)
            a.activation(bx_all[:], gc_all[:], ACT.Exp).then_inc(S("ga_egc"), 1)
            act.wait_ge(S("gates_done"), 1)

        @block.tensor
        def _(pe):
            t_ = nc.tensor
            pe.wait_ge(S("cst_in"), 16)
            pe.wait_ge(S("ps_zero"), 1)
            with pe.Fori(0, TT // 2) as i:
                for s in range(2):
                    pe.wait_ge(S("xn", s), i + 1)
                    pe.wait_ge(S("xT_free", s), i + 1)
                    for k in range(KT):
                        last = t_.transpose(ps[:, 2 * s + k // 4, (k % 4) * P:(k % 4 + 1) * P], xn[s][:, k * P:(k + 1) * P], ident)
                    last.then_inc(S("xT", s), 1)
                    if s == 0:
                        pass
            pe.wait_ge(S("par_in"), 16 * 15)
            t_.transpose(ps[:, 4, 384:384 + NV], vec_raw[0:NV, :], ident[0:NV, 0:NV])
            for q in range(2):
                t_.transpose(ps[:, 4, q * P:(q + 1) * P], bd_raw[:, q, :], ident)
            for q in range(4):
                t_.transpose(ps[:, 5, q * P:(q + 1) * P], bgu_raw[:, q, :], ident)
            for h in range(H):
                last = t_.transpose(ps[:, 6, h * P:(h + 1) * P], ws_raw[:, h, :], ident)
            last.then_inc(S("par_T"), 1)
            for w in ("wv_in", "wu_in", "wz_in"):
                pe.wait_ge(S(w), 16)
            pe.wait_ge(S("par_done"), 1)
            with pe.Fori(0, TT // 2) as i:
                for s in range(2):
                    t = 2 * i + s
                    pe.wait_ge(S("ytile", s), i + 1)
                    for bk, c0, width, name in ((2, 0, W, "v_proj"), (3, W, W, "u_proj"),
                                                (4, 2 * W, W, "z_proj"), (5, 3 * W, 2 * H, "ab_proj")):
                        for k in range(KT):
                            last = t_.matmul(bank(bk)[:, 0:width], ytile[s][:, k, :], wuvz[:, k, c0:c0 + width],
                                             start=(k == 0), stop=(k == KT - 1))
                        last.then_inc(S(name), 1)
                    pe.wait_ge(S("vn"), t + 1)
                    pe.wait_ge(S("gt_free"), t + 1)
                    for h in range(H):
                        last = t_.matmul(bank(6)[:, h * P:(h + 1) * P], wsT[:, h, :], vn[:, h * P:(h + 1) * P],
                                         start=True, stop=True)
                    last.then_inc(S("gate_ps"), 1)
                    pe.wait_ge(S("gu"), t + 1)
                    pe.wait_ge(S("z_raw"), t + 1)
                    pe.wait_ge(S("ab_sb"), t + 1)
            with pe.Fori(0, 3) as i:
                for s in range(2):
                    pe.wait_ge(S("wq_in", s), 16 * i + 16)
                    for ct in range(2):
                        pe.wait_ge(S("qkv_bank", ct), 2 * i + s + 1)
                        for hf in range(2):
                            for k in range(KT):
                                last = t_.matmul(bank(2 * ct + hf), wq[s][:, k, ct * P:(ct + 1) * P],
                                                 yT[:, k, 512 * hf:512 * (hf + 1)], start=(k == 0), stop=(k == KT - 1))
                            last.then_inc(S(f"qkv_proj{hf}", ct), 1)
            for part_ in range(2):
                with pe.Fori(0, 4) as i:
                    for s in range(2):
                        pe.wait_ge(S("usq", s), i + 1 + 4 * part_)
                        pe.wait_ge(S("uss_used", s), i + 1 + 4 * part_)
                        t_.matmul(bank(4 + s), ones, usq[s], start=True, stop=True).then_inc(S("uss", s), 1)
            pe.wait_ge(S("g_ready"), 1)
            t_.matmul(bank(6)[:, 0:TT * H], tri, g_all[:].rearrange("p t h -> p (t h)"), start=True, stop=True).then_inc(S("gc_ps"), 1)
            pe.wait_ge(S("gates_done"), 1)
            pe.wait_ge(S("wout_in"), 16)
            pe.wait_ge(S("state_zero"), 1)

        @block.vector
        def _(dve):
            v = nc.vector

            v.memset(ps[:], 0.0).then_inc(S("ps_zero"), 1)
            for s in range(2):
                dve.sem_inc(S("xT_free", s), 1)
            dve.wait_ge(S("cst_in"), 16)
            with dve.Fori(0, TT // 2) as i:
                for s in range(2):
                    dve.wait_ge(S("x_ss", s), i + 1)
                    mean_eps(small[:, 20 + s:21 + s], D).then_inc(S("x_var", s), 1)
                    dve.wait_ge(S("x_rs", s), i + 1)
                    v.tensor_scalar(xn[s], xr[s], small[:, 20 + s:21 + s], None, ALU.mult).then_inc(S("xn", s), 1)
                for s in range(2):
                    dve.wait_ge(S("xT", s), i + 1)
                    v.tensor_copy(yT[:, :, ds((2 * i + s) * P, P)],
                                  ps[:, 2 * s:2 * s + 2, :].rearrange("p a (b c) -> p (a b) c", b=4)).then_inc(S("xT_free", s), 1)
            dve.wait_ge(S("par_T"), 1)
            v.tensor_copy(vT[:], ps[:, 4, 384:384 + NV])
            v.tensor_copy(bd_T[:], ps[:, 4, 0:256])
            v.tensor_copy(bgu_T[:], ps[:, 5, :])
            v.tensor_tensor(wsT[:], heads(bank(6)), over_heads(tri), ALU.mult)
            dve.drain()
            for k in range(KT):
                v.tensor_scalar(yT[:, k, :], yT[:, k, :], mixg_T[:, k:k + 1], None, ALU.mult).then_inc(S("yT_all"), 1)
            for n in ("gv_free", "gu_free", "gt_free", "vn_free", "par_done"):
                dve.sem_inc(S(n), 1)
            for s in range(2):
                dve.sem_inc(S("ytile_free", s), 1)
            with dve.Fori(0, TT // 2) as i:
                for s in range(2):
                    t = 2 * i + s
                    dve.wait_ge(S("vsq"), t + 1)
                    v.tensor_reduce(small[:, 16:20], heads(vsq), AX.X, ALU.add)
                    dve.drain()
                    mean_eps(small[:, 16:20], P).then_inc(S("v_var"), 1)
                    dve.wait_ge(S("ab_proj"), t + 1)
                    dve.sem_inc(S("ytile_free", s), 1)
                    v.tensor_copy(ab[:, t, :], bank(5)[:, 0:8]).then_inc(S("ab_sb"), 1)
                    dve.wait_ge(S("gate_ps"), t + 1)
                    v.tensor_tensor(heads(gt), heads(bank(6)), over_cols(bs_T), ALU.add)
                    dve.drain()
                    dve.wait_ge(S("gu"), t + 1)
                    v.tensor_tensor(gm[:, t, :], gt, gu, ALU.mult).then_inc(S("gate_done"), 1)
                    dve.drain()
                    for n in ("gv_free", "gu_free", "gt_free", "vn_free"):
                        dve.sem_inc(S(n), 1)
            dve.drain()
            for s in range(2):
                v.memset(cb[s][:, 0:CONV - 1], 0.0)
                dve.sem_inc(S("qkv_bank", s), 1)
            dve.drain()
            for s in range(2):
                dve.sem_inc(S("conv_used", s), 1)
            dve.sem_inc(S("pad_zero"), 1)
            with dve.Fori(0, 6) as i:
                for s in range(2):
                    dve.wait_ge(S("cb", s), 2 * i + 2)
                    dve.sem_inc(S("qkv_bank", s), 1)
                    v.tensor_scalar(cacc[s], cb[s][:, 0:SEQ], conv_T[:, ds(2 * i + s, 1)], None, ALU.mult)
                    for j in range(1, CONV):
                        dve.drain()
                        last = v.scalar_tensor_tensor(cacc[s], cb[s][:, j:j + SEQ], conv_T[:, ds(2 * i + (s + 12 * j), 1)],
                                                      cacc[s], ALU.mult, ALU.add)
                    last.then_inc(S("cacc", s), 1)
                for s in range(2):
                    dve.wait_ge(S("silu", s), i + 1)
                    dve.sem_inc(S("conv_used", s), 1)
            v.tensor_tensor(g_all[:], ab[:, :, 0:H], dtb[:].unsqueeze(1).broadcast_to([P, TT, H]), ALU.add)
            dve.drain()
            dve.sem_inc(S("ga_y"), 1)
            for s in range(2):
                dve.sem_inc(S("usq_free", s), 1)
                dve.sem_inc(S("uss_used", s), 1)
                dve.sem_inc(S("urs_free", s), 1)

            def unit(part_):
                with dve.Fori(0, 4) as i:
                    for s in range(2):
                        dve.wait_ge(S("uss", s), i + 1 + 4 * part_)
                        dve.sem_inc(S("usq_free", s), 1)
                        dve.wait_ge(S("urt", s), i + 1 + 4 * part_)
                        dve.sem_inc(S("uss_used", s), 1)
                        v.reciprocal(urs[s], urs[s])
                        dve.drain()
                        cell = qkvT[:, i + 4 * part_, 512 * s:512 * (s + 1)]
                        v.scalar_tensor_tensor(cell, cell, 1.0 if part_ else P ** -0.5, urs[s], ALU.mult, ALU.mult
                                               ).then_inc(S("unit_done"), 1)
                        dve.drain()
                        dve.sem_inc(S("urs_free", s), 1)

            unit(0)
            unit(1)
            dve.wait_ge(S("ga_exp"), 1)
            v.tensor_scalar(g_all[:], g_all[:], 0.0, None, ALU.max)
            v.tensor_scalar(be_all[:], be_all[:], 1.0, None, ALU.add)
            v.tensor_scalar(small[:, 24:28], small[:, 24:28], -1.0, None, ALU.mult)
            dve.drain()
            v.tensor_tensor(g_all[:], g_all[:], bx_all[:], ALU.add)
            v.reciprocal(be_all[:], be_all[:])
            dve.drain()
            v.tensor_tensor(g_all[:], g_all[:], small[:, 24:28].unsqueeze(1).broadcast_to([P, TT, H]), ALU.mult).then_inc(S("g_ready"), 1)
            dve.wait_ge(S("gc_ps"), 1)
            v.tensor_copy(gc_all[:].rearrange("p t h -> p (t h)"), bank(6)[:, 0:TT * H]).then_inc(S("gc_ready"), 1)
            dve.wait_ge(S("ga_egc"), 1)
            v.tensor_tensor(bx_all[:], bx_all[:], be_all[:], ALU.mult).then_inc(S("gates_done"), 1)

        projections.close()
        nc.clear_and_free_semaphores(list(sems.values()))
        sems.clear()
        nc.all_engine_barrier()

        mixers = ExitStack()
        block = mixers.enter_context(nc.Block())

        @block.sync
        def _(sp):
            with sp.Fori(0, TT // 2) as i:
                sp.wait_ge(S("delta_turn"), 4 * i + 4)
                for s in range(2):
                    sp.dma_start(xh[s], x[0, ds((2 * i + s) * P, P), :]).then_inc(S("xh_in", s), 16)
                for s in range(2):
                    sp.wait_ge(S("h_ready", s), i + 1)
                    sp.dma_start(h_dram[ds((2 * i + s) * P, P), :], xh[s]).then_inc(S("h_out", s), 16)
                for s in range(2):
                    sp.wait_ge(S("h_out", s), 16 * (i + 1))
                sp.sem_inc(S("h_stored"), 1)
            sp.wait_ge(S("zeroed"), 1)
            sp.dma_start(list_dram.rearrange("(p n) o -> p (n o)", p=P), zero[:, 0:LROWS // P]).then_inc(S("list_zero"), 16)
            with sp.Fori(0, TT // 2) as i:
                sp.wait_ge(S("route_turn"), 5 * i + 5)
                for s in range(2):
                    sp.dma_start(hr[s], h_dram[ds((2 * i + s) * P, P), :]).then_inc(S("hr_in", s), 16)
                for s in range(2):
                    sp.wait_ge(S("h2_ready", s), i + 1)
                    sp.dma_start(h2_dram[ds((2 * i + s) * P, P), :], h2[s]).then_inc(S("h2_out", s), 16)
                for s in range(2):
                    sp.wait_ge(S("h2_out", s), 16 * (i + 1))
                sp.sem_inc(S("h2_stored"), 1)

        @block.gpsimd
        def _(pool):
            v = nc.gpsimd
            pool.sem_inc(S("delta_turn"), 1)
            with pool.Fori(0, TT // 2) as i:
                pool.wait_ge(S("delta_turn"), 4 * i + 4)
                for s in range(2):
                    c = 2 * i + s
                    v.tensor_tensor(heads(Um[s]), over_heads(tri), over_cols(g_all[:, c, :]), ALU.mult).then_inc(S("GU", s), 1)
                    v.tensor_tensor(heads(Tm[s]), over_heads(ident), over_cols(be_all[:, c, :]), ALU.mult).then_inc(S("BI", s), 1)
                    v.tensor_copy(heads(kP[s]), qkvT[:, 4:8, ds(c * P, P)]).then_inc(S("kst", s), 1)
                    v.tensor_copy(heads(vN[s]), qkvT[:, 8:12, ds(c * P, P)]).then_inc(S("vst", s), 1)
                for s in range(2):
                    c = 2 * i + s
                    pool.wait_ge(S("E_exp", s), i + 1)
                    v.tensor_tensor(heads(EV[s]), heads(EV[s]), over_heads(tri), ALU.mult).then_inc(S("E", s), 1)
                    pool.wait_ge(S("EB", s), i + 1)
                    v.tensor_tensor(heads(QD[s]), heads(QD[s]), qkvT[:, 0:4, ds(c * P, P)], ALU.mult).then_inc(S("QD", s), 1)
                    v.tensor_copy(gst[s], gm[:, c, :]).then_inc(S("gst", s), 1)
                for s in range(2):
                    pool.wait_ge(S("LT", s), i + 1)
                    v.tensor_tensor(heads(Um[s]), heads(LT[s]), over_heads(m0t), ALU.mult).then_inc(S("U0a", s), 1)
                    pool.wait_ge(S("U0a", s), i + 1)
                    v.tensor_tensor(heads(Um[s]), over_heads(ident), heads(Um[s]), ALU.subtract).then_inc(S("U0", s), 1)
                for s in range(2):
                    c = 2 * i + s
                    pool.wait_ge(S("o_var", s), i + 1)
                    rsqrt(oss[s]).then_inc(S("o_rs", s), 1)
                    pool.wait_ge(S("o_norm", s), i + 1)
                    v.tensor_tensor(vb[s], vb[s], zs[:, c, :], ALU.mult).then_inc(S("o_mix", s), 1)
                pool.sem_inc(S("delta_turn"), 1)
            pool.wait_ge(S("h_stored"), 4)
            v.memset(zero, 0).then_inc(S("zeroed"), 1)
            pool.sem_inc(S("route_turn"), 1)
            pool.wait_ge(S("list_zero"), 16)
            with pool.Fori(0, TT // 2) as i:
                for s in range(2):
                    pool.wait_ge(S("h_var", s), i + 1)
                    rsqrt(small[:, 28 + s:29 + s]).then_inc(S("h_rs", s), 1)
                for s in range(2):
                    pool.wait_ge(S("ldest", s), i + 1)
                    pool.sem_inc(S("listing"), 1)
                    for j in range(TOPK):
                        pool.indirect_dma_start(list_dram, bass.IndirectOffsetOnAxis(ap=ldest[s][:, j:j + 1], axis=0),
                                                lid[s], None).then_inc(S("listed"), 16)
                pool.wait_ge(S("listed"), 16 * 2 * TOPK * (i + 1))
                pool.sem_inc(S("route_turn"), 1)

        @block.scalar
        def _(act):
            a = nc.scalar
            act.sem_inc(S("delta_turn"), 1)
            with act.Fori(0, TT // 2) as i:
                act.wait_ge(S("delta_turn"), 4 * i + 4)
                for s in range(2):
                    b0 = 4 * s
                    act.wait_ge(S("Bp", s), i + 1)
                    a.activation(egl[s], heads(bank(b0))[:, :, P - 1], ACT.Exp).then_inc(S("egl", s), 1)
                    a.activation(QD[s], bank(b0), ACT.Exp).then_inc(S("EB", s), 1)
                    act.wait_ge(S("dD", s), i + 1)
                    a.activation(EV[s], EV[s], ACT.Exp).then_inc(S("E_exp", s), 1)
                for s in range(2):
                    act.wait_ge(S("wT", s), i + 1)
                    a.activation(vN[s], bank(4 * s + 3), ACT.Copy, scale=-1.0).then_inc(S("nwT", s), 1)
                for s in range(2):
                    act.wait_ge(S("vnew", s), i + 1)
                    a.activation(EV[s], bank(4 * s), ACT.Copy).then_inc(S("vn_sb", s), 1)
                    act.wait_ge(S("o_ps", s), i + 1)
                    for h in range(H):
                        last = a.activation(osq[s][:, h * P:(h + 1) * P], bank(4 * s + 1)[:, h * P:(h + 1) * P], ACT.Square,
                                            accum_out=oss[s][:, h:h + 1])
                    last.then_inc(S("o_ss", s), 1)
                act.sem_inc(S("delta_turn"), 1)
            act.wait_ge(S("h_stored"), 4)
            act.sem_inc(S("route_turn"), 1)
            with act.Fori(0, TT // 2) as i:
                act.wait_ge(S("route_turn"), 5 * i + 5)
                for s in range(2):
                    act.wait_ge(S("hr_in", s), 16 * i + 16)
                    a.activation(h2j, hr[s], ACT.Square, accum_out=small[:, 28 + s:29 + s]).then_inc(S("h_ss", s), 1)
                    act.drain()
                act.sem_inc(S("route_turn"), 1)

        @block.tensor
        def _(pe):
            t_ = nc.tensor
            pe.sem_inc(S("delta_turn"), 1)

            def four(out_bank, left, right, name, start=True, stop=True):
                for h in range(H):
                    c = slice(h * P, (h + 1) * P)
                    last = t_.matmul(out_bank[:, c], left[:, c], right[:, c], start=start, stop=stop)
                last.then_inc(name, 1)

            with pe.Fori(0, TT // 2) as i:
                pe.wait_ge(S("delta_turn"), 4 * i + 4)
                for s in range(2):
                    b0 = 4 * s
                    c = 2 * i + s
                    pe.wait_ge(S("GU", s), i + 1)
                    t_.matmul(bank(b0), ones, Um[s], start=True, stop=True).then_inc(S("Bp", s), 1)
                    pe.wait_ge(S("BI", s), i + 1)
                    t_.matmul(bank(b0 + 1), ones, Tm[s], start=True, stop=True).then_inc(S("Bb", s), 1)
                    pe.wait_ge(S("kst", s), i + 1)
                    four(bank(b0 + 2), kP[s], kP[s], S("Gk", s))
                    for h in range(H):
                        last = t_.matmul(bank(b0 + 3)[:, h * P:(h + 1) * P], kP[s][:, h * P:(h + 1) * P],
                                         qkvT[:, h, ds(c * P, P)], start=True, stop=True)
                    last.then_inc(S("Gq", s), 1)
                for s in range(2):
                    b0 = 4 * s
                    pe.wait_ge(S("EB", s), i + 1)
                    pe.wait_ge(S("dD", s), i + 1)
                    for h in range(H):
                        last = t_.transpose(bank(b0)[:, h * P:(h + 1) * P], kP[s][:, h * P:(h + 1) * P], ident)
                    last.then_inc(S("kt", s), 1)
                    pe.wait_ge(S("Eb", s), i + 1)
                    pe.wait_ge(S("vst", s), i + 1)
                    for h in range(H):
                        last = t_.transpose(bank(b0 + 1)[:, h * P:(h + 1) * P], vN[s][:, h * P:(h + 1) * P], ident)
                    last.then_inc(S("vt", s), 1)
                for l in range(LEVELS):
                    for s in range(2):
                        b0 = 4 * s
                        if l == 0:
                            pe.wait_ge(S("LT", s), i + 1)
                            for h in range(H):
                                last = t_.matmul(bank(b0 + 2)[:, h * P:(h + 1) * P], LT[s][:, h * P:(h + 1) * P], ident,
                                                 start=True, stop=True)
                            last.then_inc(S("LTp", s), 1)
                        else:
                            pe.wait_ge(S("Tl", s), 6 * i + l)
                            four(bank(b0 + 2), LT[s], Tm[s], S("LTp", s))
                    for s in range(2):
                        b0 = 4 * s
                        if l == 0:
                            continue
                        if l == 1:
                            pe.wait_ge(S("U0", s), i + 1)
                            pe.wait_ge(S("kvt", s), i + 1)
                            pe.wait_ge(S("AT", s), i + 1)
                        else:
                            pe.wait_ge(S("Ul", s), 6 * i + l - 1)
                        pe.wait_ge(S("Pl", s), 6 * i + l)
                        if l < LEVELS - 1:
                            four(bank(b0 + 3), Um[s], kP[s], S("TP", s))
                        four(bank(b0), kP[s], Um[s], S("PU", s))
                for s in range(2):
                    pe.wait_ge(S("Ul", s), 6 * i + 6)
                    four(bank(4 * s + 3), kbg[s], Um[s], S("wT", s))
                for s in range(2):
                    b0 = 4 * s
                    pe.wait_ge(S("nwT", s), i + 1)
                    if s == 1:
                        pe.wait_ge(S("state"), 2 * i + 1)
                    for h in range(H):
                        c_ = slice(h * P, (h + 1) * P)
                        t_.matmul(bank(b0)[:, c_], Um[s][:, c_], vb[s][:, c_], start=True, stop=False)
                        last = t_.matmul(bank(b0)[:, c_], vN[s][:, c_], Sm[:, c_], start=False, stop=True)
                    last.then_inc(S("vnew", s), 1)
                    pe.wait_ge(S("QD", s), i + 1)
                    pe.wait_ge(S("vn_sb", s), i + 1)
                    four(bank(b0 + 2), ke[s], EV[s], S("kv", s))
                    for h in range(H):
                        c_ = slice(h * P, (h + 1) * P)
                        t_.matmul(bank(b0 + 1)[:, c_], QD[s][:, c_], Sm[:, c_], start=True, stop=False)
                        last = t_.matmul(bank(b0 + 1)[:, c_], AT[s][:, c_], EV[s][:, c_], start=False, stop=True)
                    last.then_inc(S("o_ps", s), 1)
                for s in range(2):
                    b0 = 4 * s
                    pe.wait_ge(S("gst", s), i + 1)
                    for h in range(H):
                        last = t_.transpose(bank(b0 + 3)[:, h * P:(h + 1) * P], gst[s][:, h * P:(h + 1) * P], ident)
                    last.then_inc(S("mixTa", s), 1)
                    pe.wait_ge(S("o_mix", s), i + 1)
                    for h in range(H):
                        last = t_.transpose(bank(b0)[:, h * P:(h + 1) * P], vb[s][:, h * P:(h + 1) * P], ident)
                    last.then_inc(S("mixTb", s), 1)
                for s in range(2):
                    b0 = 4 * s
                    pe.wait_ge(S("mixT", s), i + 1)
                    for n in range(2):
                        for k in range(KT):
                            last = t_.matmul(bank(b0 + 1 + n), mixT[s][:, k, :], wout[:, k, 512 * n:512 * (n + 1)],
                                             start=(k == 0), stop=(k == KT - 1))
                        last.then_inc(S("proj", s), 1)
                pe.sem_inc(S("delta_turn"), 1)
            pe.sem_inc(S("route_turn"), 1)
            with pe.Fori(0, TT // 2) as i:
                pe.wait_ge(S("route_turn"), 5 * i + 5)
                for s in range(2):
                    pe.wait_ge(S("h2_ready", s), i + 1)
                    for k in range(KT):
                        last = t_.transpose(ps[:, 4 * s + k // 4, (k % 4) * P:(k % 4 + 1) * P], h2[s][:, k * P:(k + 1) * P], ident)
                    last.then_inc(S("h2T_ps", s), 1)
                for s in range(2):
                    pe.wait_ge(S("h2T", s), i + 1)
                    for k in range(KT):
                        last = t_.matmul(bank(4 * s + 2)[:, 0:NE], h2T[s][:, k, :], rw[:, k, :], start=(k == 0), stop=(k == KT - 1))
                    last.then_inc(S("lg_ps", s), 1)
                for s in range(2):
                    pe.wait_ge(S("mask", s), i + 1)
                    t_.matmul(bank(4 * s + 3)[:, 0:NE], tri, msk[s], start=True, stop=True)
                    t_.matmul(bank(4 * s + 3)[:, NE:2 * NE], ones, msk[s], start=True, stop=True).then_inc(S("rank_ps", s), 1)
                pe.sem_inc(S("route_turn"), 1)

        @block.vector
        def _(dve):
            v = nc.vector
            dve.sem_inc(S("delta_turn"), 1)
            with dve.Fori(0, TT // 2) as i:
                dve.wait_ge(S("delta_turn"), 4 * i + 4)
                for s in range(2):
                    b0, c = 4 * s, 2 * i + s
                    dve.wait_ge(S("EB", s), i + 1)
                    v.tensor_tensor(heads(EV[s]), heads(bank(b0)), over_cols(gc_all[:, c, :]), ALU.subtract)
                    dve.drain()
                    v.tensor_scalar(EV[s], EV[s], 0.0, None, ALU.min).then_inc(S("dD", s), 1)
                for s in range(2):
                    b0, c = 4 * s, 2 * i + s
                    dve.wait_ge(S("Bb", s), i + 1)
                    dve.wait_ge(S("E", s), i + 1)
                    v.tensor_tensor(LT[s], EV[s], bank(b0 + 1), ALU.mult).then_inc(S("Eb", s), 1)
                    dve.drain()
                    dve.wait_ge(S("Gk", s), i + 1)
                    v.tensor_tensor(LT[s], LT[s], bank(b0 + 2), ALU.mult).then_inc(S("LT", s), 1)
                    dve.wait_ge(S("Gq", s), i + 1)
                    v.tensor_tensor(AT[s], EV[s], bank(b0 + 3), ALU.mult).then_inc(S("AT", s), 1)
                for s in range(2):
                    b0, c = 4 * s, 2 * i + s
                    dve.wait_ge(S("kt", s), i + 1)
                    v.tensor_tensor(heads(kbg[s]), heads(bank(b0)), over_cols(bx_all[:, c, :]), ALU.mult)
                    v.tensor_tensor(heads(ke[s]), heads(bank(b0)), heads(EV[s])[:, :, P - 1:P].broadcast_to([P, H, P]), ALU.mult)
                    dve.wait_ge(S("vt", s), i + 1)
                    v.tensor_tensor(heads(vb[s]), heads(bank(b0 + 1)), over_cols(be_all[:, c, :]), ALU.mult).then_inc(S("kvt", s), 1)
                for l in range(LEVELS):
                    for s in range(2):
                        b0 = 4 * s
                        if l == 0:
                            dve.wait_ge(S("LTp", s), 7 * i + 1)
                            v.scalar_tensor_tensor(heads(Tm[s]), heads(bank(b0 + 2)), -1.0, over_heads(level(0)), ALU.mult, ALU.mult)
                            dve.drain()
                            v.tensor_tensor(heads(Tm[s]), heads(Tm[s]), over_heads(ident), ALU.add).then_inc(S("Tl", s), 1)
                        else:
                            dve.wait_ge(S("LTp", s), 7 * i + l + 1)
                            v.tensor_tensor(heads(kP[s]), heads(bank(b0 + 2)), over_heads(level(l)), ALU.mult).then_inc(S("Pl", s), 1)
                    for s in range(2):
                        b0 = 4 * s
                        if l == 0:
                            continue
                        if l < LEVELS - 1:
                            dve.wait_ge(S("TP", s), 5 * i + l)
                            v.tensor_tensor(Tm[s], Tm[s], bank(b0 + 3), ALU.subtract).then_inc(S("Tl", s), 1)
                        dve.wait_ge(S("PU", s), 6 * i + l)
                        v.tensor_tensor(Um[s], Um[s], bank(b0), ALU.subtract).then_inc(S("Ul", s), 1)
                for s in range(2):
                    b0 = 4 * s
                    dve.wait_ge(S("kv", s), i + 1)
                    dve.wait_ge(S("egl", s), i + 1)
                    dve.wait_ge(S("o_ps", s), i + 1)
                    for h in range(H):
                        c_ = slice(h * P, (h + 1) * P)
                        last = v.scalar_tensor_tensor(Sm[:, c_], Sm[:, c_], egl[s][:, h:h + 1], bank(b0 + 2)[:, c_], ALU.mult, ALU.add)
                    last.then_inc(S("state"), 1)
                    dve.wait_ge(S("o_ss", s), i + 1)
                    mean_eps(oss[s], P).then_inc(S("o_var", s), 1)
                    dve.wait_ge(S("o_rs", s), i + 1)
                    v.tensor_tensor(heads(vb[s]), heads(bank(b0 + 1)), over_cols(oss[s]), ALU.mult).then_inc(S("o_norm", s), 1)
                for s in range(2):
                    b0 = 4 * s
                    dve.wait_ge(S("mixTa", s), i + 1)
                    v.tensor_copy(mixT[s][:, 0:4, :], heads(bank(b0 + 3)))
                    dve.wait_ge(S("mixTb", s), i + 1)
                    v.tensor_copy(mixT[s][:, 4:8, :], heads(bank(b0))).then_inc(S("mixT", s), 1)
                for s in range(2):
                    b0 = 4 * s
                    dve.wait_ge(S("xh_in", s), 16 * i + 16)
                    for n in range(2):
                        dve.wait_ge(S("proj", s), 2 * i + n + 1)
                        last = v.tensor_tensor(xh[s][:, 512 * n:512 * (n + 1)], xh[s][:, 512 * n:512 * (n + 1)], bank(b0 + 1 + n), ALU.add)
                    last.then_inc(S("h_ready", s), 1)
                dve.wait_ge(S("h_stored"), i + 1)
                dve.sem_inc(S("delta_turn"), 1)
            v.memset(count[:], 0.0)
            dve.drain()
            dve.sem_inc(S("route_turn"), 2)
            with dve.Fori(0, TT // 2) as i:
                dve.wait_ge(S("route_turn"), 5 * i + 5)
                for s in range(2):
                    dve.wait_ge(S("h_ss", s), i + 1)
                    rs = small[:, 28 + s:29 + s]
                    mean_eps(rs, D).then_inc(S("h_var", s), 1)
                    dve.wait_ge(S("h_rs", s), i + 1)
                    v.scalar_tensor_tensor(h2[s], hr[s], rs, ffn_g[:], ALU.mult, ALU.mult).then_inc(S("h2_ready", s), 1)
                for s in range(2):
                    dve.wait_ge(S("h2T_ps", s), i + 1)
                    v.tensor_copy(h2T[s], ps[:, 4 * s:4 * s + 2, :].rearrange("p a (b c) -> p (a b) c", b=4)).then_inc(S("h2T", s), 1)
                for s in range(2):
                    t = 2 * i + s
                    dve.wait_ge(S("lg_ps", s), i + 1)
                    v.tensor_tensor(lg[s], bank(4 * s + 2)[:, 0:NE], rb[:], ALU.add)
                    dve.drain()
                    v.max(best[s], lg[s])
                    dve.drain()
                    v.max_index(best_at[s], best[s], lg[s])
                    v.tensor_copy(top[:, t, :], best[s])
                    v.tensor_copy(lid[s], ids[:, ds(t, 1)])
                    dve.drain()
                    v.tensor_copy(ixf[s], best_at[s][:, 0:TOPK])
                    dve.drain()
                    v.tensor_copy(tixf[:, t, :], ixf[s])
                    v.tensor_tensor(oh[s], iota_e.unsqueeze(1).broadcast_to([P, TOPK, NE]),
                                    ixf[s].unsqueeze(2).broadcast_to([P, TOPK, NE]), ALU.is_equal)
                    dve.drain()
                    v.tensor_reduce(msk[s], oh[s].rearrange("p j e -> p e j"), AX.X, ALU.add).then_inc(S("mask", s), 1)
                for s in range(2):
                    t = 2 * i + s
                    dve.wait_ge(S("rank_ps", s), i + 1)
                    v.tensor_tensor(rnk[s], bank(4 * s + 3)[:, 0:NE], count[:], ALU.add)
                    dve.drain()
                    v.tensor_tensor(count[:], bank(4 * s + 3)[:, NE:2 * NE], count[:], ALU.add)
                    v.tensor_tensor(ohr[s], oh[s], rnk[s].unsqueeze(1).broadcast_to([P, TOPK, NE]), ALU.mult)
                    dve.drain()
                    v.tensor_reduce(rkf[s], ohr[s], AX.X, ALU.add)
                    dve.drain()
                    v.tensor_scalar(rkf[s], rkf[s], -1.0, None, ALU.add)
                    v.tensor_scalar(ixf[s], ixf[s], float(SEQ), None, ALU.mult)
                    dve.drain()
                    v.tensor_copy(ranks[:, t, :], rkf[s])
                    v.tensor_tensor(ldest[s], ixf[s], rkf[s], ALU.add).then_inc(S("ldest", s), 1)
                dve.wait_ge(S("h2_stored"), i + 1)
                dve.sem_inc(S("route_turn"), 2)

        mixers.close()
        nc.clear_and_free_semaphores(list(sems.values()))
        sems.clear()
        nc.all_engine_barrier()

        ffn = ExitStack()
        block = ffn.enter_context(nc.Block())

        @block.sync
        def _(sp):
            sp.wait_ge(S("zrow_set"), 1)
            for j in range(CAP // P):
                sp.dma_start(y_dram[SEQ * TOPK + j * P:SEQ * TOPK + (j + 1) * P, :], zrow).then_inc(S("tail_zero", j), 16)
            sp.wait_ge(S("tab_ready"), 1)
            sp.dma_start(tab_dram, tabi[0:NBLK + 1, :]).then_inc(S("tab_out"), 16)
            sp.wait_ge(S("tab_out"), 16)
            sp.dma_start(tab[0:1, :], tab_dram.rearrange("(o b) c -> o (b c)", o=1)).then_inc(S("tab_in"), 16)
            for j in range(CAP // P):
                sp.wait_ge(S("tail_zero", j), 16)
            sp.sem_inc(S("y_tail"), 1)
            sp.wait_ge(S("tab_in"), 16)
            with sp.Fori(0, NBLK) as b:
                cnt = sp.value_load(tab[0:1, ds(b * TABC + 2, 1)], min_val=0, max_val=CAP)
                with sp.If(cnt > 0):
                    e = sp.value_load(tab[0:1, ds(b * TABC, 1)], min_val=0, max_val=NE - 1)
                    for g in range(4):
                        sp.wait_ge(S("w_used", g), b + 1)
                        for q in range(2):
                            sp.dma_start(wslot[g][:, :, 256 * q:256 * (q + 1)],
                                         gu_v[ds(e, 1), :, :, q, 256 * g:256 * (g + 1)].rearrange("o p k n -> (o p) k n")
                                         ).then_inc(S(f"w_in{q}", g), 16)
                    for g in range(4, 6):
                        sp.wait_ge(S("w_used", g), b + 1)
                        sp.dma_start(wslot[g], dn_v[ds(e, 1), :, :, 512 * (g - 4):512 * (g - 3)].rearrange("o p k n -> (o p) k n")
                                     ).then_inc(S("w_in0", g), 16)
            sp.wait_ge(S("exp_end"), 3)
            with sp.Fori(0, TT // 4) as i:
                for q in range(4):
                    t = 4 * i + q
                    sp.wait_ge(S("hc_free", q), i + 1)
                    sp.dma_start(hc[q], h_dram[ds(t * P, P), :]).then_inc(S("hc_in", q), 16)
                for q in range(4):
                    sp.wait_ge(S("out_ready", q), i + 1)
                    sp.dma_start(out[0, ds((4 * i + q) * P, P), :], ho[q]).then_inc(S("out_done", q), 16)
                for q in range(4):
                    sp.wait_ge(S("out_done", q), 16 * i + 16)
                    sp.sem_inc(S("ho_free", q), 1)

        @block.gpsimd
        def _(pool):
            v = nc.gpsimd
            v.memset(zrow, 0.0).then_inc(S("zrow_set"), 1)
            pool.wait_ge(S("tab_in"), 16)
            pool.wait_ge(S("exp_ready"), 3)
            pool.wait_ge(S("y_tail"), 1)
            pool.sem_inc(S("plan_done"), 1)

            def gather(b):
                lrow = pool.value_load(tab[0:1, ds(b * TABC + 3, 1)], min_val=0, max_val=LROWS - CAP)
                pool.dma_start(idx, list_dram[ds(lrow, CAP), :].rearrange("(j p) o -> p (j o)", p=P),
                               allow_slow_non_contiguous=True).then_inc(S("idx_in"), 16)
                pool.wait_ge(S("idx_in"), 16 * b + 16)
                pool.sem_inc(S("gathering"), 1)
                for j in range(2):
                    pool.indirect_dma_start(xin[:, j, :], None, h2_dram,
                                            bass.IndirectOffsetOnAxis(ap=idx[:, j:j + 1], axis=0)).then_inc(S("xin", j), 16)

            gather(0)
            with pool.Fori(0, NBLK) as b:
                cnt = pool.value_load(tab[0:1, ds(b * TABC + 2, 1)], min_val=0, max_val=CAP)
                with pool.If(cnt > 0):
                    pool.wait_ge(S("xin_free"), b + 1)
                    for j in range(2):
                        pool.wait_ge(S("xin", j), 16 * b + 16)
                    gather(b + 1)
                    for m in range(8):
                        pool.wait_ge(S("um", m % 2), 4 * b + m // 2 + 1)
                        if m == 0:
                            pool.wait_ge(S("hT_free"), b + 1)
                        v.tensor_tensor(gmn[m % 2], gmn[m % 2], umn[m % 2], ALU.mult).then_inc(S("gum", m % 2), 1)
                        pool.wait_ge(S("gum", m % 2), 4 * b + m // 2 + 1)
                        pool.wait_ge(S("sg", m % 2), 4 * b + m // 2 + 1)
                        v.tensor_tensor(hT[:, m, :], gmn[m % 2], sg[m % 2], ALU.mult).then_inc(S("hT"), 1)
            pool.wait_ge(S("exp_end"), 3)
            def root(t):
                pool.wait_ge(S("f_var", t % 4), t // 4 + 1)
                rsqrt(small[:, 32 + t % 4:33 + t % 4]).then_inc(S("f_rs", t % 4), 1)

            for t in range(TT):
                q = t % 4
                if t >= 4:
                    root(t - 4)
                    pool.wait_ge(S("yg_used", q), t // 4)
                for j in range(TOPK):
                    pool.indirect_dma_start(yg[q][j], None, y_dram,
                                            bass.IndirectOffsetOnAxis(ap=dest[:, t, j:j + 1], axis=0)).then_inc(S(f"yg{j}", q), 16)
            for t in range(TT - 4, TT):
                root(t)

        @block.scalar
        def _(act):
            a = nc.scalar
            act.wait_ge(S("top_rel"), 1)
            a.activation(gates[:], gates[:], ACT.Exp).then_inc(S("top_exp"), 1)
            act.wait_ge(S("tab_in"), 16)
            act.sem_inc(S("exp_ready"), 1)
            act.sem_inc(S("y_out"), 16)
            act.wait_ge(S("plan_done"), 1)
            with act.Fori(0, NBLK) as b:
                cnt = act.value_load(tab[0:1, ds(b * TABC + 2, 1)], min_val=0, max_val=CAP)
                with act.If(cnt > 0):
                    for m in range(8):
                        act.wait_ge(S("gmn", m % 2), 4 * b + m // 2 + 1)
                        a.activation(sg[m % 2], gmn[m % 2], ACT.Sigmoid, scale=ALPHA).then_inc(S("sg", m % 2), 1)
                    act.wait_ge(S("yv_free"), b + 1)
                    for d in range(8):
                        act.wait_ge(S("down", d % 2), 4 * b + d // 2 + 1)
                        if d % 4 == 3:
                            act.sem_inc(S("w_used", 4 + d // 4), 1)
                        if d == 7:
                            act.sem_inc(S("hT_free"), 1)
                        a.activation(yv[:, d, :], bank(4 + d % 2)[:, 0:CAP], ACT.Identity, bias=eb[:, 16 + d:17 + d]
                                     ).then_inc(S("yv"), 1)
                    row = act.value_load(tab[0:1, ds(b * TABC + 1, 1)], min_val=0, max_val=SEQ * TOPK - 1)
                    act.wait_ge(S("y_out"), 16 * b + 16)
                    act.wait_ge(S("yt"), b + 1)
                    act.sem_inc(S("rows_out"), 1)
                    with act.If(cnt > P):
                        act.dma_start(y_dram[ds(row, CAP), :].rearrange("(j p) n -> p j n", p=P), yt).then_inc(S("y_out"), 16)
                    with act.Else():
                        act.dma_start(y_dram[ds(row, P), :], yt[:, 0, :]).then_inc(S("y_out"), 16)
            blocks = act.value_load(tab[0:1, 4:5], min_val=1, max_val=NBLK)
            act.wait_ge(S("y_out"), 16 * blocks + 16)
            act.sem_inc(S("exp_end"), 1)
            with act.Fori(0, TT // 4) as i:
                for q in range(4):
                    act.wait_ge(S("hsum", q), i + 1)
                    a.activation(hj, hc[q], ACT.Square, accum_out=small[:, 32 + q:33 + q]).then_inc(S("f_ss", q), 1)
                    act.drain()

        @block.tensor
        def _(pe):
            t_ = nc.tensor
            pe.wait_ge(S("tab_in"), 16)
            for g in range(6):
                pe.sem_inc(S("w_used", g), 1)
            for n in ("hT_free", "yv_free"):
                pe.sem_inc(S(n), 1)
            pe.sem_inc(S("exp_ready"), 1)
            pe.wait_ge(S("plan_done"), 1)

            def half_in(j, use):
                for r in range(2):
                    pe.wait_ge(S("tr_bank", r), use + j + 1)
                    for k in range(4):
                        last = t_.transpose(bank(6 + r)[:, k * P:(k + 1) * P],
                                            xin[:, j, (4 * r + k) * P:(4 * r + k + 1) * P], ident)
                    last.then_inc(S("xT_ps", r), 1)

            def rows_in(b, use):
                rows = pe.value_load(tab[0:1, ds(b * TABC + 2, 1)], min_val=0, max_val=CAP)
                pe.wait_ge(S("xin", 0), 16 * b + 16)
                half_in(0, use)
                pe.wait_ge(S("xin", 1), 16 * b + 16)
                with pe.If(rows > P):
                    half_in(1, use)
                with pe.Else():
                    for r in range(2):
                        pe.wait_ge(S("tr_bank", r), use + 2)
                        pe.sem_inc(S("xT_ps", r), 1)

            def gate_up(b, n):
                for m in range(8):
                    g, c = m // 2, (m % 2) * P
                    pe.wait_ge(S("gu_bank", m % 4), 2 * b + m // 4 + 1)
                    for q in range(2):
                        if m % 2 == 0:
                            pe.wait_ge(S(f"w_in{q}", g), 16 * b + 16)
                        for k in range(KT):
                            last = t_.matmul(bank(m % 4)[:, q * CAP:q * CAP + n], wslot[g][:, k, 256 * q + c:256 * q + c + P],
                                             xT[:, k, 0:n], start=(k == 0), stop=(k == KT - 1))
                    last.then_inc(S("gu_ps", m % 4), 1)

            def rows_out(b, r, n):
                for j in range(2):
                    pe.wait_ge(S("tr_bank", j), 4 * b + r + 5)
                    if j and n <= P:
                        pe.sem_inc(S("yt_ps", j), 1)
                        continue
                    for k in range(4):
                        last = t_.transpose(bank(6 + j)[:, k * P:(k + 1) * P], yv[:, 4 * r + k, j * P:(j + 1) * P], ident)
                    last.then_inc(S("yt_ps", j), 1)

            def down(b, n):
                for d in range(8):
                    g, c = 4 + d // 4, (d % 4) * P
                    if d % 4 == 0:
                        pe.wait_ge(S("w_in0", g), 16 * b + 16)
                    if d < 2:
                        pe.wait_ge(S("down_bank", d), b + 1)
                    else:
                        pe.wait_ge(S("yv"), 8 * b + d - 1)
                    for k in range(KT):
                        if d == 0:
                            pe.wait_ge(S("hT"), 8 * b + k + 1)
                        last = t_.matmul(bank(4 + d % 2)[:, 0:n], wslot[g][:, k, c:c + P], hT[:, k, 0:n],
                                         start=(k == 0), stop=(k == KT - 1))
                    last.then_inc(S("down", d % 2), 1)
                    if d == 6:
                        rows_out(b, 0, n)
                pe.wait_ge(S("yv"), 8 * b + 8)
                rows_out(b, 1, n)

            def by_count(cnt, work, b, widths=WIDTHS):
                if len(widths) == 1:
                    work(b, widths[0])
                    return
                half = len(widths) // 2
                with pe.If(cnt > widths[half - 1]):
                    by_count(cnt, work, b, widths[half:])
                with pe.Else():
                    by_count(cnt, work, b, widths[:half])

            rows_in(0, 0)
            with pe.Fori(0, NBLK) as b:
                cnt = pe.value_load(tab[0:1, ds(b * TABC + 2, 1)], min_val=0, max_val=CAP)
                with pe.If(cnt > 0):
                    pe.wait_ge(S("xT_sb"), 4 * b + 4)
                    by_count(cnt, gate_up, b)
                    rows_in(b + 1, 4 * b + 2)
                    by_count(cnt, down, b)
            pe.sem_inc(S("exp_end"), 1)

        @block.vector
        def _(dve):
            v = nc.vector
            def running(o, src, spare):
                v.tensor_copy(o, src)
                dve.drain()
                sh = 1
                while sh < NE:
                    v.tensor_copy(spare, o)
                    dve.drain()
                    v.tensor_tensor(o[:, sh:NE], spare[:, sh:NE], spare[:, 0:NE - sh], ALU.add)
                    dve.drain()
                    sh *= 2

            start, cblk, nblk, t0, t1, onehot, before = sc[0:7]
            running(start, count[:], t0)
            v.tensor_tensor(start, start, count[:], ALU.subtract)
            dve.drain()
            v.tensor_scalar(nblk, count[:], 0.0, None, ALU.is_gt)
            for n in range(1, SEQ // CAP):
                v.tensor_scalar(t0, count[:], float(n * CAP), None, ALU.is_gt)
                dve.drain()
                v.tensor_tensor(nblk, nblk, t0, ALU.add)
                dve.drain()
            running(cblk, nblk, t0)
            v.tensor_tensor(before, cblk, nblk, ALU.subtract)
            dve.drain()
            v.tensor_scalar(t0, before, part, None, ALU.is_le)
            v.tensor_scalar(t1, cblk, part, None, ALU.is_gt)
            dve.drain()
            v.tensor_tensor(onehot, t0, t1, ALU.mult)
            v.tensor_scalar(before, before, part, -float(CAP), ALU.subtract, ALU.mult)
            v.tensor_scalar(sc[8], iota_e, float(SEQ), None, ALU.mult)
            dve.drain()
            v.tensor_tensor(t0, start, before, ALU.add)
            v.tensor_tensor(sc[8], sc[8], before, ALU.add)
            v.tensor_tensor(t1, count[:], before, ALU.subtract)
            dve.drain()
            v.tensor_tensor(t0, t0, onehot, ALU.mult)
            v.tensor_tensor(t1, t1, onehot, ALU.mult)
            v.tensor_tensor(sc[7], iota_e, onehot, ALU.mult)
            v.tensor_tensor(sc[8], sc[8], onehot, ALU.mult)
            dve.drain()
            v.tensor_reduce(tabf[:, 0:1], sc[7], AX.X, ALU.add)
            v.tensor_reduce(tabf[:, 1:2], t0, AX.X, ALU.add)
            v.tensor_reduce(tabf[:, 2:3], t1, AX.X, ALU.add)
            v.tensor_reduce(tabf[:, 3:4], sc[8], AX.X, ALU.add)
            v.tensor_copy(tabf[:, 4:5], cblk[:, NE - 1:NE])
            dve.drain()
            v.tensor_scalar(tabf[:, 2:3], tabf[:, 2:3], float(CAP), None, ALU.min)
            dve.drain()
            v.tensor_copy(tabi, tabf).then_inc(S("tab_ready"), 1)
            v.tensor_tensor(big, iota_e.unsqueeze(1).broadcast_to([P, TT * TOPK, NE]),
                            over_cols(tixf[:].rearrange("p t j -> p (t j)"), NE), ALU.is_equal)
            dve.drain()
            v.tensor_tensor(big, big, start.unsqueeze(1).broadcast_to([P, TT * TOPK, NE]), ALU.mult)
            dve.drain()
            v.tensor_reduce(desf, big, AX.X, ALU.add)
            dve.drain()
            v.tensor_tensor(dest[:].rearrange("p t j -> p (t j)"), desf, ranks[:].rearrange("p t j -> p (t j)"), ALU.add)
            v.tensor_tensor(gates[:], top[:, :, 0:TOPK], top[:, :, 0:1].broadcast_to([P, TT, TOPK]), ALU.subtract).then_inc(S("top_rel"), 1)
            dve.wait_ge(S("top_exp"), 1)
            v.tensor_reduce(gs, gates[:], AX.X, ALU.add)
            dve.drain()
            v.reciprocal(gs, gs)
            dve.drain()
            v.tensor_tensor(gates[:], gates[:], gs.unsqueeze(2).broadcast_to([P, TT, TOPK]), ALU.mult)
            dve.drain()
            dve.wait_ge(S("tab_in"), 16)
            for m in range(4):
                dve.sem_inc(S("gu_bank", m), 1)
            for r in range(2):
                dve.sem_inc(S("down_bank", r), 1)
                dve.sem_inc(S("tr_bank", r), 1)
            dve.sem_inc(S("exp_ready"), 1)
            dve.wait_ge(S("plan_done"), 1)

            def rows_in(b):
                for j in range(2):
                    for r in range(2):
                        dve.wait_ge(S("xT_ps", r), 2 * b + j + 1)
                        v.tensor_copy(xT[:, 4 * r:4 * r + 4, j * P:(j + 1) * P], heads(bank(6 + r))).then_inc(S("xT_sb"), 1)
                        dve.drain()
                        dve.sem_inc(S("tr_bank", r), 1)
                dve.sem_inc(S("xin_free"), 1)

            rows_in(0)
            with dve.Fori(0, NBLK) as b:
                cnt = dve.value_load(tab[0:1, ds(b * TABC + 2, 1)], min_val=0, max_val=CAP)
                with dve.If(cnt > 0):
                    e = dve.value_load(tab[0:1, ds(b * TABC, 1)], min_val=0, max_val=NE - 1)
                    v.tensor_copy(eb[:, 0:16], bgu_T[:, ds(e * 16, 16)])
                    v.tensor_copy(eb[:, 16:24], bd_T[:, ds(e * 8, 8)])
                    dve.drain()
                    for m in range(8):
                        r = m % 2
                        dve.wait_ge(S("gu_ps", m % 4), 2 * b + m // 4 + 1)
                        if m % 2 == 1:
                            dve.sem_inc(S("w_used", m // 2), 1)
                        if m >= 2:
                            dve.wait_ge(S("hT"), 8 * b + m - 1)
                        v.tensor_scalar(gmn[r], bank(m % 4)[:, 0:CAP], eb[:, m:m + 1], LIMIT, ALU.add, ALU.min).then_inc(S("gmn", r), 1)
                        v.tensor_scalar(umn[r], bank(m % 4)[:, CAP:2 * CAP], eb[:, 8 + m:9 + m], LIMIT, ALU.add, ALU.min)
                        dve.drain()
                        dve.sem_inc(S("gu_bank", m % 4), 1)
                        v.tensor_scalar(umn[r], umn[r], -LIMIT, 1.0, ALU.max, ALU.add)
                        dve.drain()
                        dve.wait_ge(S("sg", r), 4 * b + m // 2 + 1)
                        dve.sem_inc(S("um", r), 1)
                    rows_in(b + 1)
                    dve.wait_ge(S("y_out"), 16 * b + 16)
                    for r in range(2):
                        for j in range(2):
                            dve.wait_ge(S("yt_ps", j), 2 * b + r + 1)
                            v.tensor_copy(yt[:, j, 512 * r:512 * (r + 1)], bank(6 + j))
                            dve.drain()
                            dve.sem_inc(S("tr_bank", j), 1)
                    dve.wait_ge(S("hT"), 8 * b + 8)
                    dve.wait_ge(S("yv"), 8 * b + 8)
                    for r in range(2):
                        dve.sem_inc(S("down_bank", r), 1)
                    dve.sem_inc(S("yt"), 1)
                    dve.sem_inc(S("yv_free"), 1)
            dve.sem_inc(S("exp_end"), 1)
            for q in range(4):
                dve.sem_inc(S("hc_free", q), 1)
                dve.sem_inc(S("ho_free", q), 1)
            with dve.Fori(0, TT // 4) as i:
                def norm(q, n):
                    dve.wait_ge(S("f_ss", q), n)
                    mean_eps(small[:, 32 + q:33 + q], D).then_inc(S("f_var", q), 1)
                    dve.wait_ge(S("f_rs", q), n)
                    dve.wait_ge(S("ho_free", q), n)
                    v.scalar_tensor_tensor(ho[q], hc[q], small[:, 32 + q:33 + q], fin_g[:], ALU.mult, ALU.mult
                                           ).then_inc(S("out_ready", q), 1)
                    dve.drain()
                    dve.sem_inc(S("hc_free", q), 1)

                for q in range(4):
                    dve.wait_ge(S("hc_in", q), 16 * i + 16)
                    for j in range(TOPK):
                        dve.wait_ge(S(f"yg{j}", q), 16 * i + 16)
                        v.scalar_tensor_tensor(hc[q], yg[q][j], gates[:, 4 * i + q, j:j + 1], hc[q], ALU.mult, ALU.add)
                        dve.drain()
                    dve.sem_inc(S("hsum", q), 1)
                    dve.sem_inc(S("yg_used", q), 1)
                    if q:
                        norm(q - 1, i + 1)
                norm(3, i + 1)

        ffn.close()


_INS = ["x", "norm_mix_g", "w_in", "gm_norm_g", "gm_ws", "gm_bs", "dn_conv_w", "dn_a_log", "dn_dt_bias", "dn_norm_g",
        "w_out", "norm_ffn_g", "router_w", "router_b", "exp_w_gu", "exp_b_gu", "exp_w_down", "exp_b_down", "final_norm_g"]


def _constants(np):
    i = np.arange(P)
    row, col = i[:, None], i[None, :]
    c = np.zeros((P, NCST), np.float32)
    c[:, C_ID:C_ID + P] = row == col
    c[:, C_TRI:C_TRI + P] = row <= col
    c[:, C_ONE:C_ONE + P] = 1.0
    for l in range(LEVELS):
        c[:, C_LV + P * l:C_LV + P * (l + 1)] = ((row >> l) ^ (col >> l) == 1) & (row > col)
    c[:, C_M0T:C_M0T + P] = ((row ^ col) == 1) & (row < col)
    c[:, C_IOTA:C_IOTA + NE] = np.arange(NE)
    c[:, C_PART] = i
    c[:, C_HALF], c[:, C_EPS] = -0.5, EPS
    return c, (np.arange(TT)[None, :] * P + i[:, None]).astype(np.int32)


def kernel(**inputs):
    import numpy as np
    import concourse.bacc as bacc
    from concourse.bass_utils import run_bass_kernel_spmd as run

    dt = mybir.dt
    nc = bacc.Bacc("TRN2", target_bir_lowering=False, num_devices=1)
    arrays, args = {}, []
    for name in _INS:
        a = np.ascontiguousarray(inputs[name])
        arrays[f"in_{name}"] = a
        args.append(nc.dram_tensor(f"in_{name}", a.shape, dt.float32, kind="ExternalInput").ap())
    arrays["consts"], arrays["tok_ids"] = _constants(np)
    args.append(nc.dram_tensor("consts", (P, NCST), dt.float32, kind="ExternalInput").ap())
    args.append(nc.dram_tensor("tok_ids", (P, TT), dt.int32, kind="ExternalInput").ap())
    args.append(nc.dram_tensor("out", (1, SEQ, D), dt.float32, kind="ExternalOutput").ap())
    kind = "Internal"
    args.append(nc.dram_tensor("h_dram", (SEQ, D), dt.float32, kind=kind).ap())
    args.append(nc.dram_tensor("h2_dram", (SEQ, D), dt.float32, kind=kind).ap())
    args.append(nc.dram_tensor("list_dram", (LROWS, 1), dt.int32, kind=kind).ap())
    args.append(nc.dram_tensor("tab_dram", (NBLK + 1, TABC), dt.int32, kind=kind).ap())
    args.append(nc.dram_tensor("y_dram", (SLOTS, D), dt.float32, kind="Internal").ap())
    program(nc, *args, None)
    r = run(nc, [arrays], core_ids=[0])
    return r.results[0]["out"]
```

```python
import concourse.bass as bass
from concourse import mybir
from contextlib import ExitStack, contextmanager

D, SEQ, P = 1024, 1024, 128
KT, TT = D // P, SEQ // P
H, W = 4, 512
NE, TOPK, F = 32, 4, 1024
CONV = 4
EPS = 1e-6
LIMIT, ALPHA = 7.0, 1.702
CAP = 256
NBLK = NE + SEQ * TOPK // CAP
WIDTHS = (96, 112, 128, 136, 152, 176, 208, CAP)
GROUP = 8
SLOTS = SEQ * TOPK + CAP
U0, V0, Q0, Z0, A0 = 0, W, 2 * W, 5 * W, 6 * W
LROWS = NE * SEQ + CAP
TABC = 5
LEVELS = 7
C_ID, C_TRI, C_ONE, C_M0T, C_LV = 0, 128, 256, 384, 512
C_IOTA = C_LV + LEVELS * 128
C_PART = C_IOTA + NE
C_HALF, C_EPS = C_PART + 1, C_PART + 2
NCST = C_PART + 3


def program(nc, x, norm_mix_g, w_in, gm_norm_g, gm_ws, gm_bs, dn_conv_w, dn_a_log, dn_dt_bias,
            dn_norm_g, w_out, norm_ffn_g, router_w, router_b, exp_w_gu, exp_b_gu, exp_w_down,
            exp_b_down, final_norm_g, consts, tok_ids, out, h_dram, h2_dram, list_dram, tab_dram,
            y_dram):
    fp32, i32, u32 = mybir.dt.float32, mybir.dt.int32, mybir.dt.uint32
    ALU, ACT, AX = mybir.AluOpType, mybir.ActivationFunctionType, mybir.AxisListType
    ds = bass.ds
    ctx = ExitStack()
    with ctx:
        def sb(name, shape, dt=fp32):
            return ctx.enter_context(nc.sbuf_tensor(name, shape, dt))

        sems = {}

        def S(name, slot=None):
            key = name if slot is None else f"{name}_{slot}"
            if key not in sems:
                sems[key] = nc.alloc_semaphore(name=key)
            return sems[key]

        cst = sb("cst", [P, NCST])
        ident, tri, ones = cst[:, 0:128], cst[:, 128:256], cst[:, 256:384]
        m0t = cst[:, C_M0T:C_M0T + 128]
        iota_e, blk = cst[:, C_IOTA:C_IOTA + NE], cst[:, C_PART:C_PART + 1]

        def level(l):
            return cst[:, C_LV + 128 * l:C_LV + 128 * (l + 1)]

        ids = sb("ids", [P, TT], i32)
        ffn_g = sb("ffn_g", [P, D])
        fin_g = sb("fin_g", [P, D])
        gmg = sb("gmg", [P, W])
        dng = sb("dng", [P, P])
        rb = sb("rb", [P, NE])
        alog = sb("alog", [P, H])
        dtb = sb("dtb", [P, H])
        NV = CONV * 12 + KT + H
        vT = sb("vT", [P, NV])
        conv_T, mixg_T, bs_T = vT[:, 0:48], vT[:, 48:56], vT[:, 56:60]
        bgu_T = sb("bgu_T", [P, NE * 16])
        bd_T = sb("bd_T", [P, NE * KT])
        rw = sb("rw", [P, KT, NE])
        wsT = sb("wsT", [P, H, P])
        small = sb("small", [P, 160])
        g_all, be_all = sb("g_all", [P, TT, H]), sb("be_all", [P, TT, H])
        gc_all, bx_all = sb("gc_all", [P, TT, H]), sb("bx_all", [P, TT, H])
        ab = sb("ab", [P, TT, 2 * H])
        lg = [small[:, 64 + 32 * s:96 + 32 * s] for s in range(2)]
        best = [small[:, 128 + 8 * s:136 + 8 * s] for s in range(2)]
        best_at = [small[:, 144 + 8 * s:152 + 8 * s].bitcast(u32) for s in range(2)]
        top = sb("top", [P, TT, 8])
        gates = sb("gates", [P, TT, TOPK])
        dest = sb("dest", [P, TT, TOPK], i32)
        tixf = sb("tixf", [P, TT, TOPK])
        ranks = sb("ranks", [P, TT, TOPK])
        count = sb("count", [P, NE])
        tab = sb("tab", [1, (NBLK + 2) * TABC], i32)

        AW = 45632
        arena = sb("arena", [P, AW])
        used = [0]

        def cut(cols, at=None):
            a = used[0] if at is None else at
            if at is None:
                used[0] += cols
            assert a + cols <= AW, (a, cols)
            return arena[:, a:a + cols]

        def r3(ap, n):
            return ap.rearrange("p (a b) -> p a b", a=n)

        wout = r3(cut(8192), KT)
        mix0 = used[0]
        gm = r3(cut(4096), TT)
        zs = r3(cut(4096), TT)
        big0 = used[0]
        wuvz = r3(cut(KT * 1544), KT)
        qkvT = r3(cut(KT * 1536, big0), 12)
        work0 = used[0]
        yT = r3(cut(8192), KT)
        wq = [r3(cut(2048), KT) for _ in range(2)]
        tmp0 = used[0]
        ytile = [r3(cut(1024), KT) for _ in range(2)]
        gv, vsq, vn, gu, gt = [cut(512) for _ in range(5)]
        xr = cut(8192, 0).rearrange("p (t c) -> p t c", t=TT)
        xn = [cut(1024, mix0 + 1024 * s) for s in range(4)]
        sqj = cut(1024, mix0 + 4096)
        vec_raw = cut(128, mix0 + 5120)
        bgu_raw = r3(cut(512, mix0 + 5248), 4)
        bd_raw = r3(cut(256, mix0 + 5760), 2)
        ws_raw = r3(cut(512, mix0 + 6016), H)
        cb = [cut(CONV - 1 + SEQ, tmp0 + 1028 * s) for s in range(2)]
        cacc = [cut(1024, tmp0 + 2056 + 1024 * s) for s in range(2)]
        usq = cut(8192, 0).rearrange("p (u c) -> p u c", u=2 * KT)
        used[0] = work0
        kP, vN, EV, QD, LT, AT, Tm, Um, kbg, ke, vb = [[cut(512) for _ in range(2)] for _ in range(11)]
        Sm = cut(512)
        mixT = [r3(cut(1024), KT) for _ in range(2)]
        xh = [cut(1024) for _ in range(2)]
        egl = [small[:, 0:4], small[:, 4:8]]
        oss = [small[:, 8:12], small[:, 12:16]]
        osq = kbg
        gst = [cut(512), cut(512)]
        used[0] = mix0
        hr = [cut(1024) for _ in range(2)]
        h2 = [cut(1024) for _ in range(2)]
        h2j = cut(1024)
        h2T = [r3(cut(1024), KT) for _ in range(2)]
        oh = [cut(128).rearrange("p (j e) -> p j e", j=TOPK) for _ in range(2)]
        ohr = [cut(128).rearrange("p (j e) -> p j e", j=TOPK) for _ in range(2)]
        msk, rnk = [[cut(32) for _ in range(2)] for _ in range(2)]
        ixf, rkf = [[cut(4) for _ in range(2)] for _ in range(2)]
        ldest = cut(TT * TOPK).bitcast(i32).rearrange("p (t j) -> p t j", t=TT)
        zero = cut(264).bitcast(i32)
        used[0] = 6 * 4096
        sc = [cut(32) for _ in range(10)]
        zrow = cut(1024)
        big = cut(1024).rearrange("p (a b) -> p a b", b=NE)
        desf = cut(32)
        tabf = cut(TABC)
        tabi = cut(TABC).bitcast(i32)
        gs = cut(TT)
        used[0] = 0
        wslot = [r3(cut(4096), KT) for _ in range(6)]
        assert used[0] == 6 * 4096
        used[0] = 6 * 4096 + 4096
        idx = cut(2).bitcast(i32)
        xin = r3(cut(2048), 2)
        xT = r3(cut(2048), KT)
        hT = r3(cut(2048), KT)
        yv = r3(cut(2048), KT)
        yt = r3(cut(2048), 2)
        eb = cut(24)
        gmn, umn, sg = [[cut(CAP) for _ in range(2)] for _ in range(3)]
        hc = cut(8192, AW - 8192).rearrange("p (t c) -> p t c", t=TT)
        assert used[0] <= AW - 4096
        used[0] = 0
        yg = [[cut(1024) for _ in range(TOPK)] for _ in range(4)]
        ho = [cut(1024) for _ in range(4)]
        hj = cut(1024)
        assert used[0] <= AW - 8192

        ps = ctx.enter_context(nc.psum_tensor("ps", [P, 8, 512], fp32))

        def bank(n):
            return ps[:, n, :]

        def heads(ap):
            return ap.rearrange("p (h c) -> p h c", h=H)

        def over_cols(ap, n=P):
            return ap.unsqueeze(2).broadcast_to([P, ap.shape[1], n])

        def over_heads(ap, n=H):
            return ap.unsqueeze(1).broadcast_to([P, n, ap.shape[1]])

        w_in_v = w_in[0].rearrange("(k p) n -> p k n", p=P)
        gu_v = exp_w_gu[0].rearrange("e (k p) (g n) -> e p k g n", p=P, g=2)
        dn_v = exp_w_down[0].rearrange("e (k p) n -> e p k n", p=P)

        def mean_eps(cell, n):
            return nc.vector.tensor_scalar(cell, cell, 1.0 / n, EPS, ALU.mult, ALU.add)

        def rsqrt(cell):
            return nc.gpsimd.tensor_tensor(cell, cell, cst[:, C_HALF:C_HALF + 1].broadcast_to([P, cell.shape[1]]), ALU.pow)

        projections = ExitStack()
        block = projections.enter_context(nc.Block())

        @block.sync
        def _(sp):
            sp.dma_start(cst[:], consts).then_inc(S("cst_in"), 16)
            p = S("par_in")
            sp.dma_start(vec_raw[0:48, :], dn_conv_w[0].rearrange("w (c p) -> (w c) p", p=P)).then_inc(p, 16)
            sp.dma_start(vec_raw[48:56, :], norm_mix_g[0].rearrange("(c p) -> c p", p=P)).then_inc(p, 16)
            sp.dma_start(vec_raw[56:60, :], gm_bs[0]).then_inc(p, 16)
            sp.dma_start(ws_raw, gm_ws[0].rearrange("h t s -> t h s")).then_inc(p, 16)
            sp.dma_start(bgu_raw, exp_b_gu[0].rearrange("e (m p) -> (e m) p", p=P).rearrange("(q r) p -> r q p", r=P)).then_inc(p, 16)
            sp.dma_start(bd_raw, exp_b_down[0].rearrange("e (m p) -> (e m) p", p=P).rearrange("(q r) p -> r q p", r=P)).then_inc(p, 16)
            with sp.Fori(0, TT // 4) as i:
                for s in range(4):
                    if s % 2 == 0:
                        for q in range(2):
                            sp.wait_ge(S("x_in", s + q), 16 * i + 16)
                    sp.dma_start(xr[:, 4 * i + s, :], x[0, ds((4 * i + s) * P, P), :]).then_inc(S("x_in", s), 16)
            sp.dma_start(gmg[:], gm_norm_g[0].rearrange("h c -> (h c)").partition_broadcast(P)).then_inc(S("gmg_in"), 16)
            sp.dma_start(wuvz[:, :, 0:512], w_in_v[:, :, V0:V0 + W]).then_inc(S("wv_in"), 16)
            sp.dma_start(wuvz[:, :, 512:1024], w_in_v[:, :, U0:U0 + W]).then_inc(S("wu_in"), 16)
            sp.dma_start(wuvz[:, :, 1024:1544], w_in_v[:, :, Z0:Z0 + W + 2 * H]).then_inc(S("wz_in"), 16)
            p = S("late_in")
            sp.dma_start(dng[:], dn_norm_g[0].partition_broadcast(P)).then_inc(p, 16)
            sp.dma_start(alog[:], dn_a_log[0].partition_broadcast(P)).then_inc(p, 16)
            sp.dma_start(dtb[:], dn_dt_bias[0].partition_broadcast(P)).then_inc(p, 16)
            sp.dma_start(rb[:], router_b[0].partition_broadcast(P)).then_inc(p, 16)
            sp.dma_start(ffn_g[:], norm_ffn_g[0].partition_broadcast(P)).then_inc(p, 16)
            sp.dma_start(fin_g[:], final_norm_g.partition_broadcast(P)).then_inc(p, 16)
            sp.dma_start(ids[:], tok_ids).then_inc(p, 16)
            sp.dma_start(rw[:], router_w[0].rearrange("(k p) e -> p k e", p=P)).then_inc(p, 16)
            for u in range(2):
                sp.dma_start(wq[u], w_in_v[:, :, Q0 + 256 * u:Q0 + 256 * (u + 1)]).then_inc(S("wq_in", u), 16)
            with sp.Fori(1, 3) as i:
                for s in range(2):
                    sp.wait_ge(S("wq_used", s), i)
                    sp.dma_start(wq[s], w_in_v[:, :, ds(512 * i + (256 * s + Q0), 256)]).then_inc(S("wq_in", s), 16)

        @block.gpsimd
        def _(pool):
            v = nc.gpsimd
            pool.wait_ge(S("cst_in"), 16)
            with pool.Fori(0, TT // 4) as i:
                pool.wait_ge(S("x_var"), i + 1)
                rsqrt(small[:, 20:24]).then_inc(S("x_rs"), 1)
            pool.wait_ge(S("yT_all"), 1)
            pool.wait_ge(S("gmg_in"), 16)
            with pool.Fori(0, TT // 2) as i:
                for s in range(2):
                    pool.wait_ge(S("ytile_free", s), i + 1)
                    v.tensor_copy(ytile[s], yT[:, :, ds((2 * i + s) * P, P)]).then_inc(S("ytile", s), 1)
                    pool.wait_ge(S("v_var"), 2 * i + s + 1)
                    rsqrt(small[:, 16:20]).then_inc(S("v_rs"), 1)
                    pool.wait_ge(S("v_rs"), 2 * i + s + 1)
                    v.tensor_tensor(heads(vsq), heads(gv), over_cols(small[:, 16:20]), ALU.mult).then_inc(S("vn_a"), 1)
                    pool.wait_ge(S("vn_a"), 2 * i + s + 1)
                    pool.wait_ge(S("vn_free"), 2 * i + s + 1)
                    v.tensor_tensor(vn, vsq, gmg[:], ALU.mult).then_inc(S("vn"), 1)
            pool.wait_ge(S("late_in"), 16 * 8)
            pool.wait_ge(S("z_silu"), 8)
            v.tensor_tensor(zs.rearrange("p t (h c) -> p (t h) c", h=H), zs.rearrange("p t (h c) -> p (t h) c", h=H),
                            over_heads(dng[:], TT * H), ALU.mult).then_inc(S("z_gain"), 1)
            for s in range(2):
                pool.wait_ge(S("silu", s), 4)
            for s in range(4):
                pool.wait_ge(S("xn", s), TT // 4)
            with pool.Fori(0, KT) as i:
                for hf in range(2):
                    cell = qkvT[:, i, 512 * hf:512 * (hf + 1)]
                    v.tensor_tensor(usq[:, 2 * i + hf, :], cell, cell, ALU.mult).then_inc(S("usq"), 1)
            pool.wait_ge(S("silu", 0), 6)
            pool.wait_ge(S("silu", 1), 6)
            v.memset(Sm, 0.0).then_inc(S("state_zero"), 1)
            pool.wait_ge(S("z_gain"), 1)
            pool.wait_ge(S("state_zero"), 1)

        @block.scalar
        def _(act):
            a = nc.scalar
            act.sem_inc(S("x_turn"), 1)
            for s in range(4):
                act.sem_inc(S("x_in", s), 16)
            with act.Fori(0, TT // 4) as i:
                act.wait_ge(S("x_turn"), i + 1)
                for s in range(4):
                    act.wait_ge(S("x_in", s), 16 * i + 32)
                    last = a.activation(sqj, xr[:, 4 * i + s, :], ACT.Square, accum_out=small[:, 20 + s:21 + s])
                    if s < 3:
                        act.drain()
                last.then_inc(S("x_ss"), 1)
            with act.Fori(0, TT // 2) as i:
                for s in range(2):
                    t = 2 * i + s
                    act.wait_ge(S("v_proj"), t + 1)
                    act.wait_ge(S("gv_free"), t + 1)
                    a.activation(gv, bank(2), ACT.Gelu).then_inc(S("gv"), 1)
                    act.wait_ge(S("gv"), t + 1)
                    a.activation(vsq, gv, ACT.Square).then_inc(S("vsq"), 1)
                    act.wait_ge(S("u_proj"), t + 1)
                    act.wait_ge(S("gu_free"), t + 1)
                    a.activation(gu, bank(3), ACT.Gelu).then_inc(S("gu"), 1)
                    act.wait_ge(S("z_proj"), t + 1)
                    a.activation(zs[:, t, :], bank(4), ACT.Silu).then_inc(S("z_silu"), 1)
            act.wait_ge(S("ga_y"), 1)
            a.activation(bx_all[:], g_all[:], ACT.Abs)
            a.activation(small[:, 24:28], alog[:], ACT.Exp)
            act.drain()
            a.activation(bx_all[:], bx_all[:], ACT.Exp, scale=-1.0)
            a.activation(be_all[:], ab[:, :, H:2 * H], ACT.Exp, scale=-1.0)
            act.drain()
            a.activation(bx_all[:], bx_all[:], ACT.Ln, bias=1.0)
            act.drain()
            act.sem_inc(S("ga_exp"), 1)
            act.wait_ge(S("gate_done"), 8)
            act.wait_ge(S("pad_zero"), 1)
            with act.Fori(0, 3) as i:
                for u in range(2):
                    for s in range(2):
                        act.wait_ge(S("conv_used", s), 2 * i + u + 1)
                        for hf in range(2):
                            act.wait_ge(S(f"qkv_proj{hf}", s), 2 * i + u + 1)
                            a.activation(cb[s][:, CONV - 1 + 512 * hf:CONV - 1 + 512 * (hf + 1)], bank(2 * s + hf), ACT.Copy
                                         ).then_inc(S("cb", s), 1)
                    act.sem_inc(S("wq_used", u), 1)
                    for s in range(2):
                        act.wait_ge(S("cacc", s), 2 * i + u + 1)
                        a.activation(qkvT[:, 4 * i + (2 * u + s), :], cacc[s], ACT.Silu).then_inc(S("silu", s), 1)
            act.wait_ge(S("gc_ready"), 1)
            a.activation(bx_all[:], gc_all[:], ACT.Exp).then_inc(S("ga_egc"), 1)
            with act.Fori(0, KT // 2) as i:
                for s in range(4):
                    act.wait_ge(S("uss", s), i + 1)
                    a.activation(usq[:, 4 * i + s, :], bank(4 + s), ACT.Ln, bias=cst[:, C_EPS:C_EPS + 1])
                act.drain()
                act.sem_inc(S("uss_log"), 1)
                for s in range(4):
                    a.activation(usq[:, 4 * i + s, :], usq[:, 4 * i + s, :], ACT.Exp, scale=-0.5).then_inc(S("urs", s), 1)

        @block.tensor
        def _(pe):
            t_ = nc.tensor
            pe.wait_ge(S("cst_in"), 16)
            pe.wait_ge(S("ps_zero"), 1)
            pe.wait_ge(S("par_in"), 16 * 6)
            t_.transpose(ps[:, 4, 384:384 + NV], vec_raw[0:NV, :], ident[0:NV, 0:NV])
            for q in range(2):
                t_.transpose(ps[:, 4, q * P:(q + 1) * P], bd_raw[:, q, :], ident)
            for q in range(4):
                t_.transpose(ps[:, 5, q * P:(q + 1) * P], bgu_raw[:, q, :], ident)
            for h in range(H):
                last = t_.transpose(ps[:, 6, h * P:(h + 1) * P], ws_raw[:, h, :], ident)
            last.then_inc(S("par_T"), 1)
            with pe.Fori(0, TT // 4) as i:
                for s in range(4):
                    pe.wait_ge(S("xn", s), i + 1)
                    pe.wait_ge(S("xT_free", s), i + 1)
                    for k in range(KT):
                        last = t_.transpose(ps[:, 2 * s + k // 4, (k % 4) * P:(k % 4 + 1) * P], xn[s][:, k * P:(k + 1) * P], ident)
                    last.then_inc(S("xT", s), 1)
            pe.wait_ge(S("par_done"), 1)
            for s in range(2, 4):
                pe.wait_ge(S("xT_free", s), 3)
            with pe.Fori(0, TT // 2) as i:
                for s in range(2):
                    t = 2 * i + s
                    pe.wait_ge(S("ytile", s), i + 1)
                    for bk, c0, width, weights, name in ((2, 0, W, "wv_in", "v_proj"), (3, W, W, "wu_in", "u_proj"),
                                                         (4, 2 * W, W, "wz_in", "z_proj"),
                                                         (5, 3 * W, 2 * H, "wz_in", "ab_proj")):
                        pe.wait_ge(S(weights), 16)
                        for k in range(KT):
                            last = t_.matmul(bank(bk)[:, 0:width], ytile[s][:, k, :], wuvz[:, k, c0:c0 + width],
                                             start=(k == 0), stop=(k == KT - 1))
                        last.then_inc(S(name), 1)
                    pe.wait_ge(S("vn"), t + 1)
                    pe.wait_ge(S("gt_free"), t + 1)
                    for h in range(H):
                        last = t_.matmul(bank(6)[:, h * P:(h + 1) * P], wsT[:, h, :], vn[:, h * P:(h + 1) * P],
                                         start=True, stop=True)
                    last.then_inc(S("gate_ps"), 1)
                    pe.wait_ge(S("gu"), t + 1)
                    pe.wait_ge(S("z_silu"), t + 1)
                    pe.wait_ge(S("ab_sb"), t + 1)
            with pe.Fori(0, 3) as i:
                for s in range(2):
                    pe.wait_ge(S("wq_in", s), 16 * i + 16)
                    for ct in range(2):
                        pe.wait_ge(S("qkv_bank", ct), 2 * i + s + 1)
                        for hf in range(2):
                            for k in range(KT):
                                last = t_.matmul(bank(2 * ct + hf), wq[s][:, k, ct * P:(ct + 1) * P],
                                                 yT[:, k, 512 * hf:512 * (hf + 1)], start=(k == 0), stop=(k == KT - 1))
                            last.then_inc(S(f"qkv_proj{hf}", ct), 1)
            pe.wait_ge(S("g_ready"), 1)
            t_.matmul(bank(6)[:, 0:TT * H], tri, g_all[:].rearrange("p t h -> p (t h)"), start=True, stop=True).then_inc(S("gc_ps"), 1)
            with pe.Fori(0, KT // 2) as i:
                pe.wait_ge(S("uss_used"), i + 1)
                for s in range(4):
                    pe.wait_ge(S("usq"), 4 * i + (s + 1))
                    t_.matmul(bank(4 + s), ones, usq[:, 4 * i + s, :], start=True, stop=True).then_inc(S("uss", s), 1)

        @block.vector
        def _(dve):
            v = nc.vector

            v.memset(ps[:], 0.0).then_inc(S("ps_zero"), 1)
            dve.wait_ge(S("cst_in"), 16)
            dve.wait_ge(S("par_T"), 1)
            v.tensor_copy(vT[:], ps[:, 4, 384:384 + NV])
            v.tensor_copy(bd_T[:], ps[:, 4, 0:256])
            v.tensor_copy(bgu_T[:], ps[:, 5, :])
            v.tensor_tensor(wsT[:], heads(bank(6)), over_heads(tri), ALU.mult)
            dve.drain()
            for s in range(4):
                dve.sem_inc(S("xT_free", s), 1)
            with dve.Fori(0, TT // 4) as i:
                dve.wait_ge(S("x_ss"), i + 1)
                mean_eps(small[:, 20:24], D).then_inc(S("x_var"), 1)
                dve.wait_ge(S("x_rs"), i + 1)
                for s in range(4):
                    v.tensor_scalar(xn[s], xr[:, 4 * i + s, :], small[:, 20 + s:21 + s], None, ALU.mult).then_inc(S("xn", s), 1)
                dve.drain()
                dve.sem_inc(S("x_turn"), 1)
                for s in range(4):
                    dve.wait_ge(S("xT", s), i + 1)
                    v.tensor_tensor(yT[:, :, ds((4 * i + s) * P, P)], ps[:, 2 * s:2 * s + 2, :].rearrange("p a (b c) -> p (a b) c", b=4),
                                    over_cols(mixg_T), ALU.mult).then_inc(S("xT_free", s), 1)
            dve.drain()
            dve.sem_inc(S("yT_all"), 1)
            for n in ("gv_free", "gu_free", "gt_free", "vn_free", "par_done"):
                dve.sem_inc(S(n), 1)
            for s in range(2):
                dve.sem_inc(S("ytile_free", s), 1)
            with dve.Fori(0, TT // 2) as i:
                for s in range(2):
                    t = 2 * i + s
                    dve.wait_ge(S("vsq"), t + 1)
                    v.tensor_reduce(small[:, 16:20], heads(vsq), AX.X, ALU.add)
                    dve.drain()
                    mean_eps(small[:, 16:20], P).then_inc(S("v_var"), 1)
                    dve.wait_ge(S("ab_proj"), t + 1)
                    dve.sem_inc(S("ytile_free", s), 1)
                    v.tensor_copy(ab[:, t, :], bank(5)[:, 0:8]).then_inc(S("ab_sb"), 1)
                    dve.wait_ge(S("gate_ps"), t + 1)
                    v.tensor_tensor(heads(gt), heads(bank(6)), over_cols(bs_T), ALU.add)
                    dve.drain()
                    dve.wait_ge(S("gu"), t + 1)
                    v.tensor_tensor(gm[:, t, :], gt, gu, ALU.mult).then_inc(S("gate_done"), 1)
                    dve.drain()
                    for n in ("gv_free", "gu_free", "gt_free", "vn_free"):
                        dve.sem_inc(S(n), 1)
            dve.wait_ge(S("late_in"), 16 * 8)
            v.tensor_tensor(g_all[:], ab[:, :, 0:H], dtb[:].unsqueeze(1).broadcast_to([P, TT, H]), ALU.add)
            dve.drain()
            dve.sem_inc(S("ga_y"), 1)
            dve.wait_ge(S("ga_exp"), 1)
            v.tensor_scalar(g_all[:], g_all[:], 0.0, None, ALU.max)
            v.tensor_scalar(be_all[:], be_all[:], 1.0, None, ALU.add)
            v.tensor_scalar(small[:, 24:28], small[:, 24:28], -1.0, None, ALU.mult)
            dve.drain()
            v.tensor_tensor(g_all[:], g_all[:], bx_all[:], ALU.add)
            v.reciprocal(be_all[:], be_all[:])
            dve.drain()
            v.tensor_tensor(g_all[:], g_all[:], small[:, 24:28].unsqueeze(1).broadcast_to([P, TT, H]), ALU.mult).then_inc(S("g_ready"), 1)
            dve.drain()
            for s in range(2):
                v.memset(cb[s][:, 0:CONV - 1], 0.0)
                dve.sem_inc(S("qkv_bank", s), 1)
            dve.drain()
            for s in range(2):
                dve.sem_inc(S("conv_used", s), 1)
            dve.sem_inc(S("pad_zero"), 1)
            with dve.Fori(0, 6) as i:
                for s in range(2):
                    dve.wait_ge(S("cb", s), 2 * i + 2)
                    dve.sem_inc(S("qkv_bank", s), 1)
                    v.tensor_scalar(cacc[s], cb[s][:, 0:SEQ], conv_T[:, ds(2 * i + s, 1)], None, ALU.mult)
                    for j in range(1, CONV):
                        dve.drain()
                        last = v.scalar_tensor_tensor(cacc[s], cb[s][:, j:j + SEQ], conv_T[:, ds(2 * i + (s + 12 * j), 1)],
                                                      cacc[s], ALU.mult, ALU.add)
                    last.then_inc(S("cacc", s), 1)
                for s in range(2):
                    dve.wait_ge(S("silu", s), i + 1)
                    dve.sem_inc(S("conv_used", s), 1)
            dve.wait_ge(S("gc_ps"), 1)
            v.tensor_copy(gc_all[:].rearrange("p t h -> p (t h)"), bank(6)[:, 0:TT * H]).then_inc(S("gc_ready"), 1)
            dve.drain()
            dve.sem_inc(S("uss_used"), 1)
            for half, scale in ((0, P ** -0.5), (1, 1.0)):
                with dve.Fori(2 * half, 2 * half + 2) as i:
                    dve.wait_ge(S("uss_log"), i + 1)
                    dve.sem_inc(S("uss_used"), 1)
                    for s in range(4):
                        dve.wait_ge(S("urs", s), i + 1)
                        cell = qkvT[:, 2 * i + s // 2, 512 * (s % 2):512 * (s % 2 + 1)]
                        v.scalar_tensor_tensor(cell, cell, scale, usq[:, 4 * i + s, :], ALU.mult, ALU.mult)
            dve.wait_ge(S("ga_egc"), 1)
            v.tensor_tensor(bx_all[:], bx_all[:], be_all[:], ALU.mult).then_inc(S("gates_done"), 1)
            dve.wait_ge(S("gates_done"), 1)

        projections.close()
        nc.clear_and_free_semaphores(list(sems.values()))
        sems.clear()
        nc.all_engine_barrier()

        mixers = ExitStack()
        block = mixers.enter_context(nc.Block())

        @block.sync
        def _(sp):
            sp.dma_start(wout, w_out[0].rearrange("(k p) n -> p k n", p=P)).then_inc(S("wout_in"), 16)
            with sp.Fori(0, TT // 2) as i:
                for s in range(2):
                    sp.dma_start(xh[s], x[0, ds((2 * i + s) * P, P), :]).then_inc(S("xh_in", s), 16)
                for s in range(2):
                    sp.wait_ge(S("h_ready", s), i + 2)
                    sp.dma_start(h_dram[ds((2 * i + s) * P, P), :], xh[s]).then_inc(S("h_out", s), 16)
                for s in range(2):
                    sp.wait_ge(S("h_out", s), 16 * (i + 1))
                sp.sem_inc(S("h_stored"), 1)
            sp.wait_ge(S("zeroed"), 1)
            sp.dma_start(list_dram.rearrange("(p n) o -> p (n o)", p=P), zero[:, 0:LROWS // P]).then_inc(S("list_zero"), 16)
            for s in range(2):
                sp.dma_start(hr[s], h_dram[s * P:(s + 1) * P, :]).then_inc(S("hr_in", s), 16)

            def store(t, s):
                sp.dma_start(h2_dram[ds(t * P, P), :], h2[s]).then_inc(S("h2_out", s), 16)

            with sp.Fori(0, TT // 2 - 1) as i:
                for s in range(2):
                    sp.wait_ge(S("h2_ready", s), i + 1)
                    sp.dma_start(hr[s], h_dram[ds((2 * i + (s + 2)) * P, P), :]).then_inc(S("hr_in", s), 16)
                    store(2 * i + s, s)
            for s in range(2):
                sp.wait_ge(S("h2_ready", s), TT // 2)
                store(TT - 2 + s, s)
            for s in range(2):
                sp.wait_ge(S("h2_out", s), 16 * (TT // 2 + 1))

        @block.gpsimd
        def _(pool):
            v = nc.gpsimd
            def start(i):
                for s in range(2):
                    c = 2 * i + s
                    v.tensor_tensor(heads(Um[s]), over_heads(tri), over_cols(g_all[:, c, :]), ALU.mult).then_inc(S("GU", s), 1)
                    v.tensor_tensor(heads(Tm[s]), over_heads(ident), over_cols(be_all[:, c, :]), ALU.mult).then_inc(S("BI", s), 1)
                    v.tensor_copy(heads(kP[s]), qkvT[:, 4:8, ds(c * P, P)]).then_inc(S("kst", s), 1)
                    v.tensor_copy(heads(vN[s]), qkvT[:, 8:12, ds(c * P, P)]).then_inc(S("vst", s), 1)
                for s in range(2):
                    c = 2 * i + s
                    pool.wait_ge(S("E_exp", s), i + 1)
                    v.tensor_tensor(heads(EV[s]), heads(EV[s]), over_heads(tri), ALU.mult).then_inc(S("E", s), 1)
                    pool.wait_ge(S("EB", s), i + 1)
                    v.tensor_tensor(heads(QD[s]), heads(QD[s]), qkvT[:, 0:4, ds(c * P, P)], ALU.mult).then_inc(S("QD", s), 1)
                    v.tensor_copy(gst[s], gm[:, c, :]).then_inc(S("gst", s), 1)

            def finish(i):
                for s in range(2):
                    pool.wait_ge(S("LT", s), i + 1)
                    v.tensor_tensor(heads(Um[s]), heads(LT[s]), over_heads(m0t), ALU.mult).then_inc(S("U0a", s), 1)
                    pool.wait_ge(S("U0a", s), i + 1)
                    v.tensor_tensor(heads(Um[s]), over_heads(ident), heads(Um[s]), ALU.subtract).then_inc(S("U0", s), 1)
                for s in range(2):
                    c = 2 * i + s
                    pool.wait_ge(S("o_var", s), i + 1)
                    rsqrt(oss[s]).then_inc(S("o_rs", s), 1)
                    pool.wait_ge(S("o_norm", s), i + 1)
                    v.tensor_tensor(vb[s], vb[s], zs[:, c, :], ALU.mult).then_inc(S("o_mix", s), 1)

            start(0)
            with pool.Fori(0, TT // 2 - 1) as i:
                finish(i)
                start(i + 1)
            finish(TT // 2 - 1)
            pool.wait_ge(S("h_stored"), 4)
            v.memset(zero, 0).then_inc(S("zeroed"), 1)
            pool.wait_ge(S("list_zero"), 16)
            for i in range(TT // 2 + 1):
                for s in range(2):
                    if i < TT // 2:
                        pool.wait_ge(S("h_var", s), i + 1)
                        rsqrt(small[:, 28 + s:29 + s]).then_inc(S("h_rs", s), 1)
                for s in range(2):
                    if i:
                        pool.wait_ge(S("ldest", s), i)
                        t = 2 * i - 2 + s
                        for j in range(TOPK):
                            pool.indirect_dma_start(list_dram, bass.IndirectOffsetOnAxis(ap=ldest[:, t, j:j + 1], axis=0),
                                                    ids[:, t:t + 1], None).then_inc(S("listed"), 16)
            pool.wait_ge(S("listed"), 16 * TT * TOPK)

        @block.scalar
        def _(act):
            a = nc.scalar
            def start(i):
                for s in range(2):
                    b0 = 4 * s
                    act.wait_ge(S("Bp", s), i + 1)
                    a.activation(egl[s], heads(bank(b0))[:, :, P - 1], ACT.Exp).then_inc(S("egl", s), 1)
                    a.activation(QD[s], bank(b0), ACT.Exp).then_inc(S("EB", s), 1)
                    act.wait_ge(S("dD", s), i + 1)
                    a.activation(EV[s], EV[s], ACT.Exp).then_inc(S("E_exp", s), 1)

            def finish(i):
                for s in range(2):
                    act.wait_ge(S("wT", s), i + 1)
                    a.activation(vN[s], bank(4 * s + 3), ACT.Copy, scale=-1.0).then_inc(S("nwT", s), 1)
                for s in range(2):
                    act.wait_ge(S("vnew", s), i + 1)
                    a.activation(EV[s], bank(4 * s), ACT.Copy).then_inc(S("vn_sb", s), 1)
                    act.wait_ge(S("o_ps", s), i + 1)
                    for h in range(H):
                        last = a.activation(osq[s][:, h * P:(h + 1) * P], bank(4 * s + 1)[:, h * P:(h + 1) * P], ACT.Square,
                                            accum_out=oss[s][:, h:h + 1])
                    last.then_inc(S("o_ss", s), 1)

            start(0)
            with act.Fori(0, TT // 2 - 1) as i:
                finish(i)
                start(i + 1)
            finish(TT // 2 - 1)
            with act.Fori(0, TT // 2) as i:
                for s in range(2):
                    act.wait_ge(S("hr_in", s), 16 * i + 16)
                    act.wait_ge(S("rs_free", s), i + 1)
                    a.activation(h2j, hr[s], ACT.Square, accum_out=small[:, 28 + s:29 + s]).then_inc(S("h_ss", s), 1)
                    act.drain()

        @block.tensor
        def _(pe):
            t_ = nc.tensor

            def four(out_bank, left, right, name, start=True, stop=True):
                for h in range(H):
                    c = slice(h * P, (h + 1) * P)
                    last = t_.matmul(out_bank[:, c], left[:, c], right[:, c], start=start, stop=stop)
                last.then_inc(name, 1)

            def start(i):
                for s in range(2):
                    b0 = 4 * s
                    pe.wait_ge(S("GU", s), i + 1)
                    t_.matmul(bank(b0), ones, Um[s], start=True, stop=True).then_inc(S("Bp", s), 1)
                    pe.wait_ge(S("BI", s), i + 1)
                    t_.matmul(bank(b0 + 3), ones, Tm[s], start=True, stop=True).then_inc(S("Bb", s), 1)

            def chunk(i):
                for s in range(2):
                    b0, c = 4 * s, 2 * i + s
                    pe.wait_ge(S("kst", s), i + 1)
                    pe.wait_ge(S("h_ready", s), i + 1)
                    four(bank(b0 + 2), kP[s], kP[s], S("Gk", s))
                    for h in range(H):
                        last = t_.matmul(bank(b0 + 1)[:, h * P:(h + 1) * P], kP[s][:, h * P:(h + 1) * P],
                                         qkvT[:, h, ds(c * P, P)], start=True, stop=True)
                    last.then_inc(S("Gq", s), 1)
                for s in range(2):
                    b0 = 4 * s
                    pe.wait_ge(S("EB", s), i + 1)
                    pe.wait_ge(S("dD", s), i + 1)
                    for h in range(H):
                        last = t_.transpose(bank(b0)[:, h * P:(h + 1) * P], kP[s][:, h * P:(h + 1) * P], ident)
                    last.then_inc(S("kt", s), 1)
                    pe.wait_ge(S("Eb", s), i + 1)
                    pe.wait_ge(S("vst", s), i + 1)
                    for h in range(H):
                        last = t_.transpose(bank(b0 + 3)[:, h * P:(h + 1) * P], vN[s][:, h * P:(h + 1) * P], ident)
                    last.then_inc(S("vt", s), 1)
                for l in range(LEVELS):
                    for s in range(2):
                        b0 = 4 * s
                        if l == 0:
                            pe.wait_ge(S("LT", s), i + 1)
                            for h in range(H):
                                last = t_.matmul(bank(b0 + 2)[:, h * P:(h + 1) * P], LT[s][:, h * P:(h + 1) * P], ident,
                                                 start=True, stop=True)
                            last.then_inc(S("LTp", s), 1)
                        else:
                            pe.wait_ge(S("Tl", s), 6 * i + l)
                            four(bank(b0 + 2), LT[s], Tm[s], S("LTp", s))
                    for s in range(2):
                        b0 = 4 * s
                        if l == 0:
                            continue
                        if l == 1:
                            pe.wait_ge(S("U0", s), i + 1)
                            pe.wait_ge(S("kvt", s), i + 1)
                            pe.wait_ge(S("AT", s), i + 1)
                        else:
                            pe.wait_ge(S("Ul", s), 6 * i + l - 1)
                        pe.wait_ge(S("Pl", s), 6 * i + l)
                        if l < LEVELS - 1:
                            four(bank(b0 + 3), Um[s], kP[s], S("TP", s))
                        four(bank(b0), kP[s], Um[s], S("PU", s))
                for s in range(2):
                    pe.wait_ge(S("Ul", s), 6 * i + 6)
                    four(bank(4 * s + 3), kbg[s], Um[s], S("wT", s))
                for s in range(2):
                    b0 = 4 * s
                    pe.wait_ge(S("nwT", s), i + 1)
                    if s == 1:
                        pe.wait_ge(S("state"), 2 * i + 1)
                    for h in range(H):
                        c_ = slice(h * P, (h + 1) * P)
                        t_.matmul(bank(b0)[:, c_], Um[s][:, c_], vb[s][:, c_], start=True, stop=False)
                        last = t_.matmul(bank(b0)[:, c_], vN[s][:, c_], Sm[:, c_], start=False, stop=True)
                    last.then_inc(S("vnew", s), 1)
                    pe.wait_ge(S("QD", s), i + 1)
                    pe.wait_ge(S("vn_sb", s), i + 1)
                    four(bank(b0 + 2), ke[s], EV[s], S("kv", s))
                    for h in range(H):
                        c_ = slice(h * P, (h + 1) * P)
                        t_.matmul(bank(b0 + 1)[:, c_], QD[s][:, c_], Sm[:, c_], start=True, stop=False)
                        last = t_.matmul(bank(b0 + 1)[:, c_], AT[s][:, c_], EV[s][:, c_], start=False, stop=True)
                    last.then_inc(S("o_ps", s), 1)
                pe.wait_ge(S("wout_in"), 16)
                for s in range(2):
                    b0 = 4 * s
                    pe.wait_ge(S("gst", s), i + 1)
                    for h in range(H):
                        last = t_.transpose(bank(b0 + 3)[:, h * P:(h + 1) * P], gst[s][:, h * P:(h + 1) * P], ident)
                    last.then_inc(S("mixTa", s), 1)
                    pe.wait_ge(S("o_mix", s), i + 1)
                    for h in range(H):
                        last = t_.transpose(bank(b0)[:, h * P:(h + 1) * P], vb[s][:, h * P:(h + 1) * P], ident)
                    last.then_inc(S("mixTb", s), 1)

            def project(i):
                for s in range(2):
                    b0 = 4 * s
                    pe.wait_ge(S("mixT", s), i + 1)
                    for n in range(2):
                        for k in range(KT):
                            last = t_.matmul(bank(b0 + 1 + n), mixT[s][:, k, :], wout[:, k, 512 * n:512 * (n + 1)],
                                             start=(k == 0), stop=(k == KT - 1))
                        last.then_inc(S("proj", s), 1)

            start(0)
            with pe.Fori(0, TT // 2 - 1) as i:
                chunk(i)
                for s in range(2):
                    pe.wait_ge(S("mixT", s), i + 1)
                start(i + 1)
                project(i)
            chunk(TT // 2 - 1)
            project(TT // 2 - 1)
            with pe.Fori(0, TT // 2) as i:
                for s in range(2):
                    pe.wait_ge(S("h2_ready", s), i + 1)
                    for k in range(KT):
                        last = t_.transpose(ps[:, 4 * s + k // 4, (k % 4) * P:(k % 4 + 1) * P], h2[s][:, k * P:(k + 1) * P], ident)
                    last.then_inc(S("h2T_ps", s), 1)
                for s in range(2):
                    pe.wait_ge(S("h2T", s), i + 1)
                    for k in range(KT):
                        last = t_.matmul(bank(4 * s + 2)[:, 0:NE], h2T[s][:, k, :], rw[:, k, :], start=(k == 0), stop=(k == KT - 1))
                    last.then_inc(S("lg_ps", s), 1)
                for s in range(2):
                    pe.wait_ge(S("mask", s), i + 1)
                    t_.matmul(bank(4 * s + 3)[:, 0:NE], tri, msk[s], start=True, stop=True)
                    t_.matmul(bank(4 * s + 3)[:, NE:2 * NE], ones, msk[s], start=True, stop=True).then_inc(S("rank_ps", s), 1)

        @block.vector
        def _(dve):
            v = nc.vector
            for s in range(2):
                dve.sem_inc(S("h_ready", s), 1)

            def start(i):
                for s in range(2):
                    b0, c = 4 * s, 2 * i + s
                    dve.wait_ge(S("EB", s), i + 1)
                    v.tensor_tensor(heads(EV[s]), heads(bank(b0)), over_cols(gc_all[:, c, :]), ALU.subtract)
                    dve.drain()
                    v.tensor_scalar(EV[s], EV[s], 0.0, None, ALU.min).then_inc(S("dD", s), 1)
                for s in range(2):
                    dve.wait_ge(S("Bb", s), i + 1)
                    dve.wait_ge(S("E", s), i + 1)
                    v.tensor_tensor(LT[s], EV[s], bank(4 * s + 3), ALU.mult).then_inc(S("Eb", s), 1)
                dve.drain()

            def chunk(i):
                for s in range(2):
                    b0 = 4 * s
                    dve.wait_ge(S("Gk", s), i + 1)
                    v.tensor_tensor(LT[s], LT[s], bank(b0 + 2), ALU.mult).then_inc(S("LT", s), 1)
                    dve.wait_ge(S("Gq", s), i + 1)
                    v.tensor_tensor(AT[s], EV[s], bank(b0 + 1), ALU.mult).then_inc(S("AT", s), 1)
                for s in range(2):
                    b0, c = 4 * s, 2 * i + s
                    dve.wait_ge(S("kt", s), i + 1)
                    v.tensor_tensor(heads(kbg[s]), heads(bank(b0)), over_cols(bx_all[:, c, :]), ALU.mult)
                    v.tensor_tensor(heads(ke[s]), heads(bank(b0)), heads(EV[s])[:, :, P - 1:P].broadcast_to([P, H, P]), ALU.mult)
                    dve.wait_ge(S("vt", s), i + 1)
                    v.tensor_tensor(heads(vb[s]), heads(bank(b0 + 3)), over_cols(be_all[:, c, :]), ALU.mult).then_inc(S("kvt", s), 1)
                for l in range(LEVELS):
                    for s in range(2):
                        b0 = 4 * s
                        if l == 0:
                            dve.wait_ge(S("LTp", s), 7 * i + 1)
                            v.scalar_tensor_tensor(heads(Tm[s]), heads(bank(b0 + 2)), -1.0, over_heads(level(0)), ALU.mult, ALU.mult)
                            dve.drain()
                            v.tensor_tensor(heads(Tm[s]), heads(Tm[s]), over_heads(ident), ALU.add).then_inc(S("Tl", s), 1)
                        else:
                            dve.wait_ge(S("LTp", s), 7 * i + l + 1)
                            v.tensor_tensor(heads(kP[s]), heads(bank(b0 + 2)), over_heads(level(l)), ALU.mult).then_inc(S("Pl", s), 1)
                    for s in range(2):
                        b0 = 4 * s
                        if l == 0:
                            continue
                        if l < LEVELS - 1:
                            dve.wait_ge(S("TP", s), 5 * i + l)
                            v.tensor_tensor(Tm[s], Tm[s], bank(b0 + 3), ALU.subtract).then_inc(S("Tl", s), 1)
                        dve.wait_ge(S("PU", s), 6 * i + l)
                        v.tensor_tensor(Um[s], Um[s], bank(b0), ALU.subtract).then_inc(S("Ul", s), 1)
                for s in range(2):
                    b0 = 4 * s
                    dve.wait_ge(S("kv", s), i + 1)
                    dve.wait_ge(S("egl", s), i + 1)
                    dve.wait_ge(S("o_ps", s), i + 1)
                    for h in range(H):
                        c_ = slice(h * P, (h + 1) * P)
                        last = v.scalar_tensor_tensor(Sm[:, c_], Sm[:, c_], egl[s][:, h:h + 1], bank(b0 + 2)[:, c_], ALU.mult, ALU.add)
                    last.then_inc(S("state"), 1)
                    dve.wait_ge(S("o_ss", s), i + 1)
                    mean_eps(oss[s], P).then_inc(S("o_var", s), 1)
                    dve.wait_ge(S("o_rs", s), i + 1)
                    v.tensor_tensor(heads(vb[s]), heads(bank(b0 + 1)), over_cols(oss[s]), ALU.mult).then_inc(S("o_norm", s), 1)
                for s in range(2):
                    b0 = 4 * s
                    dve.wait_ge(S("mixTa", s), i + 1)
                    v.tensor_copy(mixT[s][:, 0:4, :], heads(bank(b0 + 3)))
                    dve.wait_ge(S("mixTb", s), i + 1)
                    v.tensor_copy(mixT[s][:, 4:8, :], heads(bank(b0))).then_inc(S("mixT", s), 1)

            def residual(i):
                for s in range(2):
                    b0 = 4 * s
                    dve.wait_ge(S("xh_in", s), 16 * i + 16)
                    for n in range(2):
                        dve.wait_ge(S("proj", s), 2 * i + n + 1)
                        last = v.tensor_tensor(xh[s][:, 512 * n:512 * (n + 1)], xh[s][:, 512 * n:512 * (n + 1)], bank(b0 + 1 + n), ALU.add)
                    last.then_inc(S("h_ready", s), 1)

            start(0)
            with dve.Fori(0, TT // 2 - 1) as i:
                chunk(i)
                start(i + 1)
                residual(i)
            chunk(TT // 2 - 1)
            residual(TT // 2 - 1)
            v.memset(count[:], 0.0)
            dve.drain()
            for s in range(2):
                dve.sem_inc(S("rs_free", s), 1)
                dve.sem_inc(S("h2_out", s), 16)

            def norm(n):
                for s in range(2):
                    dve.wait_ge(S("h_ss", s), n + 1)
                    mean_eps(small[:, 28 + s:29 + s], D).then_inc(S("h_var", s), 1)
                for s in range(2):
                    dve.wait_ge(S("h_rs", s), n + 1)
                    dve.wait_ge(S("h2_out", s), 16 * n + 16)
                    v.scalar_tensor_tensor(h2[s], hr[s], small[:, 28 + s:29 + s], ffn_g[:], ALU.mult, ALU.mult
                                           ).then_inc(S("h2_ready", s), 1)
                dve.drain()
                for s in range(2):
                    dve.sem_inc(S("rs_free", s), 1)

            def transposed(i):
                for s in range(2):
                    dve.wait_ge(S("h2T_ps", s), i + 1)
                    v.tensor_copy(h2T[s], ps[:, 4 * s:4 * s + 2, :].rearrange("p a (b c) -> p (a b) c", b=4)).then_inc(S("h2T", s), 1)

            def best_four(i):
                for s in range(2):
                    t = 2 * i + s
                    dve.wait_ge(S("lg_ps", s), i + 1)
                    v.tensor_tensor(lg[s], bank(4 * s + 2)[:, 0:NE], rb[:], ALU.add)
                    dve.drain()
                    v.max(best[s], lg[s])
                    dve.drain()
                    v.max_index(best_at[s], best[s], lg[s])
                    v.tensor_copy(top[:, t, :], best[s])
                    dve.drain()
                    v.tensor_copy(ixf[s], best_at[s][:, 0:TOPK])
                    dve.drain()
                    v.tensor_copy(tixf[:, t, :], ixf[s])
                    v.tensor_tensor(oh[s], iota_e.unsqueeze(1).broadcast_to([P, TOPK, NE]),
                                    ixf[s].unsqueeze(2).broadcast_to([P, TOPK, NE]), ALU.is_equal)
                    dve.drain()
                    v.tensor_reduce(msk[s], oh[s].rearrange("p j e -> p e j"), AX.X, ALU.add).then_inc(S("mask", s), 1)
                for s in range(2):
                    t = 2 * i + s
                    dve.wait_ge(S("rank_ps", s), i + 1)
                    v.tensor_tensor(rnk[s], bank(4 * s + 3)[:, 0:NE], count[:], ALU.add)
                    dve.drain()
                    v.tensor_tensor(count[:], bank(4 * s + 3)[:, NE:2 * NE], count[:], ALU.add)
                    v.tensor_tensor(ohr[s], oh[s], rnk[s].unsqueeze(1).broadcast_to([P, TOPK, NE]), ALU.mult)
                    dve.drain()
                    v.tensor_reduce(rkf[s], ohr[s], AX.X, ALU.add)
                    dve.drain()
                    v.tensor_scalar(rkf[s], rkf[s], -1.0, None, ALU.add)
                    v.tensor_scalar(ixf[s], ixf[s], float(SEQ), None, ALU.mult)
                    dve.drain()
                    v.tensor_copy(ranks[:, t, :], rkf[s])
                    v.tensor_tensor(ldest[:, t, :], ixf[s], rkf[s], ALU.add).then_inc(S("ldest", s), 1)

            norm(0)
            with dve.Fori(0, TT // 2 - 1) as i:
                transposed(i)
                norm(i + 1)
                best_four(i)
            transposed(TT // 2 - 1)
            best_four(TT // 2 - 1)

        mixers.close()
        nc.clear_and_free_semaphores(list(sems.values()))
        sems.clear()
        nc.all_engine_barrier()

        @contextmanager
        def each_block(eng):
            with eng.Fori(0, NBLK // GROUP) as g:
                first = eng.value_load(tab[0:1, ds(g * (GROUP * TABC) + (TABC + 2), 1)], min_val=0, max_val=CAP)
                with eng.If(first > 0):
                    with eng.Fori(0, GROUP) as k:
                        b = g * GROUP + k
                        cnt = eng.value_load(tab[0:1, ds(b * TABC + (TABC + 2), 1)], min_val=0, max_val=CAP)
                        with eng.If(cnt > 0):
                            yield b, cnt

        ffn = ExitStack()
        block = ffn.enter_context(nc.Block())

        @block.sync
        def _(sp):
            sp.wait_ge(S("zrow_set"), 1)
            for j in range(CAP // P):
                sp.dma_start(y_dram[SEQ * TOPK + j * P:SEQ * TOPK + (j + 1) * P, :], zrow).then_inc(S("tail_zero", j), 16)
            sp.wait_ge(S("tab_ready"), 1)
            sp.dma_start(tab_dram, tabi[0:NBLK + 2, :]).then_inc(S("tab_out"), 16)
            sp.wait_ge(S("tab_out"), 16)
            sp.dma_start(tab[0:1, :], tab_dram.rearrange("(o b) c -> o (b c)", o=1)).then_inc(S("tab_in"), 16)
            for j in range(CAP // P):
                sp.wait_ge(S("tail_zero", j), 16)
            sp.sem_inc(S("y_tail"), 1)
            sp.wait_ge(S("tab_in"), 16)
            with each_block(sp) as (b, cnt):
                e = sp.value_load(tab[0:1, ds(b * TABC + TABC, 1)], min_val=0, max_val=NE - 1)
                for g in range(4):
                    sp.wait_ge(S("w_used", g), b + 1)
                    for q in range(2):
                        sp.dma_start(wslot[g][:, :, 256 * q:256 * (q + 1)],
                                     gu_v[ds(e, 1), :, :, q, 256 * g:256 * (g + 1)].rearrange("o p k n -> (o p) k n")
                                     ).then_inc(S(f"w_in{q}", g), 16)
                    if g == 0:
                        for j in range(2):
                            sp.wait_ge(S("xin", j), 16)
                for g in range(4, 6):
                    sp.wait_ge(S("w_used", g), b + 1)
                    sp.dma_start(wslot[g], dn_v[ds(e, 1), :, :, 512 * (g - 4):512 * (g - 3)].rearrange("o p k n -> (o p) k n")
                                 ).then_inc(S("w_in0", g), 16)
            h_v = h_dram.rearrange("(t p) c -> p t c", p=P)
            sp.dma_start(hc[:, 4:8, :], h_v[:, 4:8, :]).then_inc(S("hc_in", 4), 16)
            sp.wait_ge(S("exp_end"), 3)
            for q in range(4):
                sp.dma_start(hc[:, q, :], h_v[:, q, :]).then_inc(S("hc_in", q), 16)
            with sp.Fori(0, TT // 4) as i:
                for q in range(4):
                    sp.wait_ge(S("out_ready", q), i + 1)
                    sp.dma_start(out[0, ds((4 * i + q) * P, P), :], ho[q]).then_inc(S("out_done", q), 16)
                for q in range(4):
                    sp.wait_ge(S("out_done", q), 16 * i + 16)
                    sp.sem_inc(S("ho_free", q), 1)

        @block.gpsimd
        def _(pool):
            v = nc.gpsimd
            v.memset(zrow, 0.0).then_inc(S("zrow_set"), 1)
            v.memset(yv, 0.0).then_inc(S("yv"), 1)
            pool.wait_ge(S("tab_in"), 16)
            pool.wait_ge(S("exp_ready"), 3)
            pool.wait_ge(S("y_tail"), 1)
            pool.sem_inc(S("plan_done"), 1)

            def gather(b):
                lrow = pool.value_load(tab[0:1, ds(b * TABC + (TABC + 3), 1)], min_val=0, max_val=LROWS - CAP)
                pool.dma_start(idx, list_dram[ds(lrow, CAP), :].rearrange("(j p) o -> p (j o)", p=P),
                               allow_slow_non_contiguous=True).then_inc(S("idx_in"), 16)
                pool.wait_ge(S("idx_in"), 16 * b + 16)
                pool.sem_inc(S("gathering"), 1)
                for j in range(2):
                    pool.indirect_dma_start(xin[:, j, :], None, h2_dram,
                                            bass.IndirectOffsetOnAxis(ap=idx[:, j:j + 1], axis=0)).then_inc(S("xin", j), 16)

            gather(0)
            with each_block(pool) as (b, cnt):
                pool.wait_ge(S("xin_free"), b + 1)
                for j in range(2):
                    pool.wait_ge(S("xin", j), 16 * b + 16)
                gather(b + 1)
                for m in range(8):
                    pool.wait_ge(S("um", m % 2), 4 * b + m // 2 + 1)
                    if m == 0:
                        pool.wait_ge(S("hT_free"), b + 1)
                    v.tensor_tensor(gmn[m % 2], gmn[m % 2], umn[m % 2], ALU.mult).then_inc(S("gum", m % 2), 1)
                    pool.wait_ge(S("gum", m % 2), 4 * b + m // 2 + 1)
                    pool.wait_ge(S("sg", m % 2), 4 * b + m // 2 + 1)
                    v.tensor_tensor(hT[:, m, :], gmn[m % 2], sg[m % 2], ALU.mult).then_inc(S("hT"), 1)
            pool.wait_ge(S("exp_end"), 3)
            def root(t):
                pool.wait_ge(S("f_var", t % 4), t // 4 + 1)
                rsqrt(small[:, 32 + t % 4:33 + t % 4]).then_inc(S("f_rs", t % 4), 1)

            for t in range(TT):
                q = t % 4
                if t >= 4:
                    root(t - 4)
                    pool.wait_ge(S("yg_used", q), t // 4)
                for j in range(TOPK):
                    pool.indirect_dma_start(yg[q][j], None, y_dram,
                                            bass.IndirectOffsetOnAxis(ap=dest[:, t, j:j + 1], axis=0)).then_inc(S(f"yg{j}", q), 16)
            for t in range(TT - 4, TT):
                root(t)

        @block.scalar
        def _(act):
            a = nc.scalar
            act.wait_ge(S("top_rel"), 1)
            a.activation(gates[:], gates[:], ACT.Exp).then_inc(S("top_exp"), 1)
            act.wait_ge(S("tab_in"), 16)
            act.sem_inc(S("exp_ready"), 1)
            act.sem_inc(S("y_out"), 16)

            def store_before(b):
                row = act.value_load(tab[0:1, ds(b * TABC + 1, 1)], min_val=0, max_val=SEQ * TOPK - 1)
                cnt = act.value_load(tab[0:1, ds(b * TABC + 2, 1)], min_val=0, max_val=CAP)
                with act.If(cnt > P):
                    act.dma_start(y_dram[ds(row, CAP), :].rearrange("(j p) n -> p j n", p=P), yt).then_inc(S("y_out"), 16)
                with act.Else():
                    act.dma_start(y_dram[ds(row, P), :], yt[:, 0, :]).then_inc(S("y_out"), 16)

            act.wait_ge(S("plan_done"), 1)
            with each_block(act) as (b, cnt):
                for m in range(8):
                    act.wait_ge(S("gmn", m % 2), 4 * b + m // 2 + 1)
                    a.activation(sg[m % 2], gmn[m % 2], ACT.Sigmoid, scale=ALPHA).then_inc(S("sg", m % 2), 1)
                act.wait_ge(S("y_out"), 16 * b + 16)
                act.wait_ge(S("yt"), b + 1)
                act.sem_inc(S("rows_out"), 1)
                with act.If(b > 0):
                    store_before(b)
                with act.Else():
                    act.sem_inc(S("y_out"), 16)
                for d in range(8):
                    act.wait_ge(S("down", d % 2), 4 * b + d // 2 + 1)
                    if d % 4 == 3:
                        act.sem_inc(S("w_used", 4 + d // 4), 1)
                    if d == 7:
                        act.sem_inc(S("hT_free"), 1)
                    a.activation(yv[:, d, :], bank(6 + d % 2)[:, 0:CAP], ACT.Identity, bias=eb[:, 16 + d:17 + d]
                                 ).then_inc(S("yv"), 1)
            blocks = act.value_load(tab[0:1, 4:5], min_val=1, max_val=NBLK)
            act.wait_ge(S("y_out"), 16 * blocks + 16)
            act.wait_ge(S("yt"), blocks + 1)
            act.sem_inc(S("rows_out"), 1)
            store_before(blocks)
            act.wait_ge(S("y_out"), 16 * blocks + 32)
            act.sem_inc(S("exp_end"), 1)
            with act.Fori(0, TT // 4) as i:
                for q in range(4):
                    act.wait_ge(S("hsum", q), i + 1)
                    a.activation(hj, hc[:, 4 * i + q, :], ACT.Square, accum_out=small[:, 32 + q:33 + q]).then_inc(S("f_ss", q), 1)
                    act.drain()

        @block.tensor
        def _(pe):
            t_ = nc.tensor
            pe.wait_ge(S("tab_in"), 16)
            for g in range(6):
                pe.sem_inc(S("w_used", g), 1)
            pe.sem_inc(S("hT_free"), 1)
            pe.sem_inc(S("exp_ready"), 1)
            pe.wait_ge(S("plan_done"), 1)

            def rows_in(b):
                for j in range(2):
                    pe.wait_ge(S("xin", j), 16 * b + 16)
                    for r in range(2):
                        if j == 1:
                            pe.wait_ge(S("gu_bank", r), 2 * b + 1)
                        for k in range(4):
                            last = t_.transpose(bank(4 * (1 - j) + r)[:, k * P:(k + 1) * P],
                                                xin[:, j, (4 * r + k) * P:(4 * r + k + 1) * P], ident)
                        last.then_inc(S("xT_ps", r), 1)

            def rows_out(j, used):
                for r in range(2):
                    pe.wait_ge(S("tr_bank", r), used + 1)
                    for k in range(4):
                        last = t_.transpose(bank(6 + r)[:, k * P:(k + 1) * P], yv[:, 4 * r + k, j * P:(j + 1) * P], ident)
                    last.then_inc(S("yt_ps", r), 1)

            def gate_up(b, n):
                for m in range(8):
                    g, c = m // 2, (m % 2) * P
                    pe.wait_ge(S("gu_bank", m % 4), 2 * b + m // 4 + 1)
                    for q in range(2):
                        if m % 2 == 0:
                            pe.wait_ge(S(f"w_in{q}", g), 16 * b + 16)
                        for k in range(KT):
                            last = t_.matmul(bank(m % 4)[:, q * CAP:q * CAP + n], wslot[g][:, k, 256 * q + c:256 * q + c + P],
                                             xT[:, k, 0:n], start=(k == 0), stop=(k == KT - 1))
                    last.then_inc(S("gu_ps", m % 4), 1)
                    if m == 3:
                        pe.wait_ge(S("yv"), 8 * b + 1)
                        rows_out(0, 2 * b)
                    if m == 4:
                        rows_out(1, 2 * b + 1)

            def down(b, n):
                for d in range(8):
                    g, c = 4 + d // 4, (d % 4) * P
                    if d % 4 == 0:
                        pe.wait_ge(S("w_in0", g), 16 * b + 16)
                    if d < 2:
                        pe.wait_ge(S("tr_bank", d), 2 * b + 3)
                    else:
                        pe.wait_ge(S("yv"), 8 * b + d)
                    for k in range(KT):
                        if d == 0:
                            pe.wait_ge(S("hT"), 8 * b + k + 1)
                        last = t_.matmul(bank(6 + d % 2)[:, 0:n], wslot[g][:, k, c:c + P], hT[:, k, 0:n],
                                         start=(k == 0), stop=(k == KT - 1))
                    last.then_inc(S("down", d % 2), 1)

            def expert(b, n):
                pe.wait_ge(S("xT_sb"), 4 * b + 4)
                gate_up(b, n)
                rows_in(b + 1)
                down(b, n)

            def by_count(cnt, work, b, widths=WIDTHS):
                if len(widths) == 1:
                    work(b, widths[0])
                    return
                half = len(widths) // 2
                with pe.If(cnt > widths[half - 1]):
                    by_count(cnt, work, b, widths[half:])
                with pe.Else():
                    by_count(cnt, work, b, widths[:half])

            rows_in(0)
            with each_block(pe) as (b, cnt):
                by_count(cnt, expert, b)
            blocks = pe.value_load(tab[0:1, 4:5], min_val=1, max_val=NBLK)
            pe.wait_ge(S("yv"), 8 * blocks + 1)
            rows_out(0, 2 * blocks)
            rows_out(1, 2 * blocks + 1)
            pe.sem_inc(S("exp_end"), 1)

        @block.vector
        def _(dve):
            v = nc.vector
            def running(o, src, spare):
                v.tensor_copy(o, src)
                dve.drain()
                sh = 1
                while sh < NE:
                    v.tensor_copy(spare, o)
                    dve.drain()
                    v.tensor_tensor(o[:, sh:NE], spare[:, sh:NE], spare[:, 0:NE - sh], ALU.add)
                    dve.drain()
                    sh *= 2

            start, cblk, nblk, t0, t1, onehot, before = sc[0:7]
            running(start, count[:], t0)
            v.tensor_tensor(start, start, count[:], ALU.subtract)
            dve.drain()
            v.tensor_scalar(nblk, count[:], 0.0, None, ALU.is_gt)
            for n in range(1, SEQ // CAP):
                v.tensor_scalar(t0, count[:], float(n * CAP), None, ALU.is_gt)
                dve.drain()
                v.tensor_tensor(nblk, nblk, t0, ALU.add)
                dve.drain()
            running(cblk, nblk, t0)
            v.tensor_tensor(before, cblk, nblk, ALU.subtract)
            dve.drain()
            v.tensor_scalar(t0, before, blk, None, ALU.is_le)
            v.tensor_scalar(t1, cblk, blk, None, ALU.is_gt)
            dve.drain()
            v.tensor_tensor(onehot, t0, t1, ALU.mult)
            v.tensor_scalar(before, before, blk, -float(CAP), ALU.subtract, ALU.mult)
            v.tensor_scalar(sc[8], iota_e, float(SEQ), None, ALU.mult)
            dve.drain()
            v.tensor_tensor(t0, start, before, ALU.add)
            v.tensor_tensor(sc[8], sc[8], before, ALU.add)
            v.tensor_tensor(t1, count[:], before, ALU.subtract)
            dve.drain()
            v.tensor_tensor(t0, t0, onehot, ALU.mult)
            v.tensor_tensor(t1, t1, onehot, ALU.mult)
            v.tensor_tensor(sc[7], iota_e, onehot, ALU.mult)
            v.tensor_tensor(sc[8], sc[8], onehot, ALU.mult)
            dve.drain()
            v.tensor_reduce(tabf[:, 0:1], sc[7], AX.X, ALU.add)
            v.tensor_reduce(tabf[:, 1:2], t0, AX.X, ALU.add)
            v.tensor_reduce(tabf[:, 2:3], t1, AX.X, ALU.add)
            v.tensor_reduce(tabf[:, 3:4], sc[8], AX.X, ALU.add)
            v.tensor_copy(tabf[:, 4:5], cblk[:, NE - 1:NE])
            dve.drain()
            v.tensor_scalar(tabf[:, 2:3], tabf[:, 2:3], float(CAP), None, ALU.min)
            dve.drain()
            v.tensor_copy(tabi, tabf).then_inc(S("tab_ready"), 1)
            v.tensor_tensor(big, iota_e.unsqueeze(1).broadcast_to([P, TT * TOPK, NE]),
                            over_cols(tixf[:].rearrange("p t j -> p (t j)"), NE), ALU.is_equal)
            dve.drain()
            v.tensor_tensor(big, big, start.unsqueeze(1).broadcast_to([P, TT * TOPK, NE]), ALU.mult)
            dve.drain()
            v.tensor_reduce(desf, big, AX.X, ALU.add)
            dve.drain()
            v.tensor_tensor(dest[:].rearrange("p t j -> p (t j)"), desf, ranks[:].rearrange("p t j -> p (t j)"), ALU.add)
            v.tensor_tensor(gates[:], top[:, :, 0:TOPK], top[:, :, 0:1].broadcast_to([P, TT, TOPK]), ALU.subtract).then_inc(S("top_rel"), 1)
            dve.wait_ge(S("top_exp"), 1)
            v.tensor_reduce(gs, gates[:], AX.X, ALU.add)
            dve.drain()
            v.reciprocal(gs, gs)
            dve.drain()
            v.tensor_tensor(gates[:], gates[:], gs.unsqueeze(2).broadcast_to([P, TT, TOPK]), ALU.mult)
            dve.drain()
            dve.wait_ge(S("tab_in"), 16)
            for m in range(4):
                dve.sem_inc(S("gu_bank", m), 1)
            for r in range(2):
                dve.sem_inc(S("tr_bank", r), 1)
            dve.sem_inc(S("exp_ready"), 1)
            dve.wait_ge(S("plan_done"), 1)

            def rows_in(b):
                for j in range(2):
                    for r in range(2):
                        dve.wait_ge(S("xT_ps", r), 2 * b + j + 1)
                        v.tensor_copy(xT[:, 4 * r:4 * r + 4, j * P:(j + 1) * P], heads(bank(4 * (1 - j) + r))
                                      ).then_inc(S("xT_sb"), 1)
                dve.sem_inc(S("xin_free"), 1)

            def rows_out(j, b):
                for r in range(2):
                    dve.wait_ge(S("yt_ps", r), 2 * b + j + 1)
                    v.tensor_copy(yt[:, j, 512 * r:512 * (r + 1)], bank(6 + r)).then_inc(S("tr_bank", r), 1)

            rows_in(0)
            with each_block(dve) as (b, cnt):
                e = dve.value_load(tab[0:1, ds(b * TABC + TABC, 1)], min_val=0, max_val=NE - 1)
                v.tensor_copy(eb[:, 0:16], bgu_T[:, ds(e * 16, 16)])
                v.tensor_copy(eb[:, 16:24], bd_T[:, ds(e * 8, 8)])
                dve.drain()
                for m in range(8):
                    r = m % 2
                    dve.wait_ge(S("gu_ps", m % 4), 2 * b + m // 4 + 1)
                    if m % 2 == 1:
                        dve.sem_inc(S("w_used", m // 2), 1)
                    if m >= 2:
                        dve.wait_ge(S("hT"), 8 * b + m - 1)
                    v.tensor_scalar(gmn[r], bank(m % 4)[:, 0:CAP], eb[:, m:m + 1], LIMIT, ALU.add, ALU.min).then_inc(S("gmn", r), 1)
                    v.tensor_scalar(umn[r], bank(m % 4)[:, CAP:2 * CAP], eb[:, 8 + m:9 + m], LIMIT, ALU.add, ALU.min)
                    dve.drain()
                    dve.sem_inc(S("gu_bank", m % 4), 1)
                    v.tensor_scalar(umn[r], umn[r], -LIMIT, 1.0, ALU.max, ALU.add)
                    dve.drain()
                    dve.wait_ge(S("sg", r), 4 * b + m // 2 + 1)
                    dve.sem_inc(S("um", r), 1)
                    if m == 3:
                        dve.wait_ge(S("y_out"), 16 * b + 16)
                        rows_out(0, b)
                    if m == 4:
                        rows_out(1, b)
                        dve.drain()
                        dve.sem_inc(S("yt"), 1)
                rows_in(b + 1)
                dve.wait_ge(S("hT"), 8 * b + 8)
                dve.wait_ge(S("yv"), 8 * b + 9)
                dve.sem_inc(S("eb_used"), 1)
            blocks = dve.value_load(tab[0:1, 4:5], min_val=1, max_val=NBLK)
            dve.wait_ge(S("y_out"), 16 * blocks + 16)
            rows_out(0, blocks)
            rows_out(1, blocks)
            dve.drain()
            dve.sem_inc(S("yt"), 1)
            dve.sem_inc(S("exp_end"), 1)
            for q in range(4):
                dve.sem_inc(S("ho_free", q), 1)
            with dve.Fori(0, TT // 4) as i:
                def norm(q, n):
                    dve.wait_ge(S("f_ss", q), n)
                    mean_eps(small[:, 32 + q:33 + q], D).then_inc(S("f_var", q), 1)
                    dve.wait_ge(S("f_rs", q), n)
                    dve.wait_ge(S("ho_free", q), n)
                    v.scalar_tensor_tensor(ho[q], hc[:, 4 * i + q, :], small[:, 32 + q:33 + q], fin_g[:], ALU.mult, ALU.mult
                                           ).then_inc(S("out_ready", q), 1)

                for q in range(4):
                    dve.wait_ge(S("hc_in", q), 16)
                    dve.wait_ge(S("hc_in", 4), 16)
                    for j in range(TOPK):
                        dve.wait_ge(S(f"yg{j}", q), 16 * i + 16)
                        v.scalar_tensor_tensor(hc[:, 4 * i + q, :], yg[q][j], gates[:, 4 * i + q, j:j + 1],
                                               hc[:, 4 * i + q, :], ALU.mult, ALU.add)
                        dve.drain()
                    dve.sem_inc(S("hsum", q), 1)
                    dve.sem_inc(S("yg_used", q), 1)
                    if q:
                        norm(q - 1, i + 1)
                norm(3, i + 1)

        ffn.close()


_INS = ["x", "norm_mix_g", "w_in", "gm_norm_g", "gm_ws", "gm_bs", "dn_conv_w", "dn_a_log", "dn_dt_bias", "dn_norm_g",
        "w_out", "norm_ffn_g", "router_w", "router_b", "exp_w_gu", "exp_b_gu", "exp_w_down", "exp_b_down", "final_norm_g"]


def _constants(np):
    i = np.arange(P)
    row, col = i[:, None], i[None, :]
    c = np.zeros((P, NCST), np.float32)
    c[:, C_ID:C_ID + P] = row == col
    c[:, C_TRI:C_TRI + P] = row <= col
    c[:, C_ONE:C_ONE + P] = 1.0
    for l in range(LEVELS):
        c[:, C_LV + P * l:C_LV + P * (l + 1)] = ((row >> l) ^ (col >> l) == 1) & (row > col)
    c[:, C_M0T:C_M0T + P] = ((row ^ col) == 1) & (row < col)
    c[:, C_IOTA:C_IOTA + NE] = np.arange(NE)
    c[:, C_PART] = i - 1
    c[:, C_HALF], c[:, C_EPS] = -0.5, EPS
    return c, (np.arange(TT)[None, :] * P + i[:, None]).astype(np.int32)


def kernel(**inputs):
    import numpy as np
    import concourse.bacc as bacc
    from concourse.bass_utils import run_bass_kernel_spmd as run

    dt = mybir.dt
    nc = bacc.Bacc("TRN2", target_bir_lowering=False, num_devices=1)
    arrays, args = {}, []
    for name in _INS:
        a = np.ascontiguousarray(inputs[name])
        arrays[f"in_{name}"] = a
        args.append(nc.dram_tensor(f"in_{name}", a.shape, dt.float32, kind="ExternalInput").ap())
    arrays["consts"], arrays["tok_ids"] = _constants(np)
    args.append(nc.dram_tensor("consts", (P, NCST), dt.float32, kind="ExternalInput").ap())
    args.append(nc.dram_tensor("tok_ids", (P, TT), dt.int32, kind="ExternalInput").ap())
    args.append(nc.dram_tensor("out", (1, SEQ, D), dt.float32, kind="ExternalOutput").ap())
    kind = "Internal"
    args.append(nc.dram_tensor("h_dram", (SEQ, D), dt.float32, kind=kind).ap())
    args.append(nc.dram_tensor("h2_dram", (SEQ, D), dt.float32, kind=kind).ap())
    args.append(nc.dram_tensor("list_dram", (LROWS, 1), dt.int32, kind=kind).ap())
    args.append(nc.dram_tensor("tab_dram", (NBLK + 2, TABC), dt.int32, kind=kind).ap())
    args.append(nc.dram_tensor("y_dram", (SLOTS, D), dt.float32, kind="Internal").ap())
    program(nc, *args)
    r = run(nc, [arrays], core_ids=[0])
    return r.results[0]["out"]
```
